# Optimizing a Trainium2 kernel written in Bass

```python
import jax, jax.numpy as jnp
from jax import lax
import numpy as np

D_MODEL = 1024
BATCH = 1
SEQ = 1024
DEPTH = 1

MEM_LEN = 256
RMS_EPS = 1e-6
F_GROUPS = 8
F_GROUP_DIM = 64
F_WIDTH = F_GROUPS * F_GROUP_DIM
MLA_HEADS = 8
QK_NOPE_DIM = 64
QK_ROPE_DIM = 32
V_HEAD_DIM = 64
Q_LORA_RANK = 384
KV_LORA_RANK = 256
ROPE_THETA = 10000.0
Q_BLOCK = 128
MLA_OUT = MLA_HEADS * V_HEAD_DIM
MIX_WIDTH = F_WIDTH + MLA_OUT
IN_WIDTH = F_WIDTH + Q_LORA_RANK + KV_LORA_RANK + QK_ROPE_DIM
IN_SPLITS = (F_WIDTH, F_WIDTH + Q_LORA_RANK, F_WIDTH + Q_LORA_RANK + KV_LORA_RANK)
MEM_HEADS = 4
MEM_HEAD_DIM = D_MODEL // MEM_HEADS
N_EXPERTS = 16
CAPACITY_FACTOR = 2
D_EXPERT = D_MODEL


def rms_norm(x, g):
    xf = x.astype(jnp.float32)
    y = xf * lax.rsqrt(jnp.mean(xf * xf, axis=-1, keepdims=True) + RMS_EPS)
    return (y * g.astype(jnp.float32)).astype(x.dtype)

def rope_tables(positions):
    freqs = 1.0 / (ROPE_THETA ** (jnp.arange(0, QK_ROPE_DIM, 2, dtype=jnp.float32) / QK_ROPE_DIM))
    ang = positions.astype(jnp.float32)[..., None] * freqs
    return jnp.cos(ang), jnp.sin(ang)

def apply_rope(x, cos, sin):
    xf = x.astype(jnp.float32)
    x1, x2 = jnp.split(xf, 2, axis=-1)
    out = jnp.concatenate([x1 * cos - x2 * sin, x1 * sin + x2 * cos], axis=-1)
    return out.astype(x.dtype)

def fourier_mix(u_f, w_fourier):
    B, S, _ = u_f.shape
    ug = u_f.reshape(B, S, F_GROUPS, F_GROUP_DIM).astype(jnp.float32)
    z = jnp.fft.fft2(ug, axes=(1, 3), norm="ortho").real.astype(u_f.dtype)
    y = jnp.einsum("bsgc,gce->bsge", z, w_fourier)
    return y.reshape(B, S, F_WIDTH)

def mla_attention(u_q, u_kv, u_kr, cos, sin, g_q_lat, w_q_up, g_kv_lat, w_kv_up):
    B, S, _ = u_q.shape
    q = (rms_norm(u_q, g_q_lat) @ w_q_up).reshape(B, S, MLA_HEADS, QK_NOPE_DIM + QK_ROPE_DIM)
    q_nope, q_rope = q[..., :QK_NOPE_DIM], q[..., QK_NOPE_DIM:]
    q_rope = apply_rope(q_rope, cos[:, :, None, :], sin[:, :, None, :])
    kv = (rms_norm(u_kv, g_kv_lat) @ w_kv_up).reshape(B, S, MLA_HEADS, QK_NOPE_DIM + V_HEAD_DIM)
    k_nope, v = kv[..., :QK_NOPE_DIM], kv[..., QK_NOPE_DIM:]
    k_rope = apply_rope(u_kr, cos, sin)
    scale = (QK_NOPE_DIM + QK_ROPE_DIM) ** -0.5
    nb = S // Q_BLOCK
    qn = q_nope.reshape(B, nb, Q_BLOCK, MLA_HEADS, QK_NOPE_DIM).swapaxes(0, 1)
    qr = q_rope.reshape(B, nb, Q_BLOCK, MLA_HEADS, QK_ROPE_DIM).swapaxes(0, 1)

    def block(args):
        qn_b, qr_b = args
        s = (jnp.einsum("bqhd,bkhd->bhqk", qn_b, k_nope)
             + jnp.einsum("bqhd,bkd->bhqk", qr_b, k_rope))
        p = jax.nn.softmax(s.astype(jnp.float32) * scale, axis=-1).astype(v.dtype)
        return jnp.einsum("bhqk,bkhd->bqhd", p, v)

    o = lax.map(block, (qn, qr))
    return o.swapaxes(0, 1).reshape(B, S, MLA_OUT)

def memory_cross_attention(hq, mn, w_mem_q, w_mem_kv, w_mem_o):
    B, S, D = hq.shape
    M = mn.shape[1]
    q = (hq @ w_mem_q).reshape(B, S, MEM_HEADS, MEM_HEAD_DIM)
    k, v = jnp.split(mn @ w_mem_kv, 2, axis=-1)
    k = k.reshape(B, M, MEM_HEADS, MEM_HEAD_DIM)
    v = v.reshape(B, M, MEM_HEADS, MEM_HEAD_DIM)
    s = jnp.einsum("bshd,bmhd->bhsm", q, k).astype(jnp.float32) * (MEM_HEAD_DIM ** -0.5)
    p = jax.nn.softmax(s, axis=-1).astype(v.dtype)
    o = jnp.einsum("bhsm,bmhd->bshd", p, v).reshape(B, S, D)
    return o @ w_mem_o

def expert_choice_moe(h, w_router, w_gate, w_up, w_down):
    B, S, D = h.shape
    cap = CAPACITY_FACTOR * S // N_EXPERTS
    aff = jax.nn.softmax((h @ w_router).astype(jnp.float32), axis=-1)
    gates, idx = lax.top_k(aff.swapaxes(1, 2), cap)
    xin = jax.vmap(lambda hb, ib: hb[ib])(h, idx)
    a = jnp.einsum("becd,edf->becf", xin, w_gate)
    b = jnp.einsum("becd,edf->becf", xin, w_up)
    y = jnp.einsum("becf,efd->becd", jax.nn.silu(a) * b, w_down)
    y = y * gates.astype(y.dtype)[..., None]
    out = jax.vmap(lambda ib, yb: jnp.zeros((S, D), yb.dtype).at[ib].add(yb))(
        idx.reshape(B, -1), y.reshape(B, -1, D))
    return out

def first_inputs(seed: int = 0) -> dict:
    key = jax.random.key(seed)
    ks = jax.random.split(key, 24)
    f32 = jnp.float32

    def nrm(k, shape, fan_in):
        return jax.random.normal(k, shape, f32) * (fan_in ** -0.5)

    def gain(k, shape):
        return 1.0 + 0.02 * jax.random.normal(k, shape, f32)

    L = DEPTH
    x = jax.random.normal(ks[0], (BATCH, SEQ, D_MODEL), f32)
    mem = jax.random.normal(ks[1], (BATCH, MEM_LEN, D_MODEL), f32)
    offs = jax.random.randint(ks[2], (BATCH, 1), 0, 1024, dtype=jnp.int32)
    positions = offs + jnp.arange(SEQ, dtype=jnp.int32)[None, :]
    return {
        "x": x,
        "mem": mem,
        "positions": positions,
        "g_mix": gain(ks[3], (L, D_MODEL)),
        "w_in": nrm(ks[4], (L, D_MODEL, IN_WIDTH), D_MODEL),
        "g_q_lat": gain(ks[5], (L, Q_LORA_RANK)),
        "w_q_up": nrm(ks[6], (L, Q_LORA_RANK, MLA_HEADS * (QK_NOPE_DIM + QK_ROPE_DIM)), Q_LORA_RANK),
        "g_kv_lat": gain(ks[7], (L, KV_LORA_RANK)),
        "w_kv_up": nrm(ks[8], (L, KV_LORA_RANK, MLA_HEADS * (QK_NOPE_DIM + V_HEAD_DIM)), KV_LORA_RANK),
        "w_fourier": nrm(ks[9], (L, F_GROUPS, F_GROUP_DIM, F_GROUP_DIM), F_GROUP_DIM),
        "w_out": nrm(ks[10], (L, MIX_WIDTH, D_MODEL), MIX_WIDTH),
        "g_mem_q": gain(ks[11], (L, D_MODEL)),
        "g_mem_kv": gain(ks[12], (L, D_MODEL)),
        "w_mem_q": nrm(ks[13], (L, D_MODEL, D_MODEL), D_MODEL),
        "w_mem_kv": nrm(ks[14], (L, D_MODEL, 2 * D_MODEL), D_MODEL),
        "w_mem_o": nrm(ks[15], (L, D_MODEL, D_MODEL), D_MODEL),
        "g_ffn": gain(ks[16], (L, D_MODEL)),
        "w_router": nrm(ks[17], (L, D_MODEL, N_EXPERTS), D_MODEL),
        "w_exp_gate": nrm(ks[18], (L, N_EXPERTS, D_MODEL, D_EXPERT), D_MODEL),
        "w_exp_up": nrm(ks[19], (L, N_EXPERTS, D_MODEL, D_EXPERT), D_MODEL),
        "w_exp_down": nrm(ks[20], (L, N_EXPERTS, D_EXPERT, D_MODEL), D_EXPERT),
        "g_final": gain(ks[21], (D_MODEL,)),
    }

def first_block(x, mem, positions, g_mix, w_in, g_q_lat, w_q_up, g_kv_lat, w_kv_up, w_fourier,
              w_out, g_mem_q, g_mem_kv, w_mem_q, w_mem_kv, w_mem_o, g_ffn, w_router,
              w_exp_gate, w_exp_up, w_exp_down, g_final):
    cos, sin = rope_tables(positions)
    for l in range(DEPTH):
        h = rms_norm(x, g_mix[l])
        u = h @ w_in[l]
        u_f, u_q, u_kv, u_kr = jnp.split(u, IN_SPLITS, axis=-1)
        y_f = fourier_mix(u_f, w_fourier[l])
        y_a = mla_attention(u_q, u_kv, u_kr, cos, sin, g_q_lat[l], w_q_up[l], g_kv_lat[l], w_kv_up[l])
        x = x + jnp.concatenate([y_f, y_a], axis=-1) @ w_out[l]
        x = x + memory_cross_attention(rms_norm(x, g_mem_q[l]), rms_norm(mem, g_mem_kv[l]),
                                       w_mem_q[l], w_mem_kv[l], w_mem_o[l])
        x = x + expert_choice_moe(rms_norm(x, g_ffn[l]), w_router[l],
                                  w_exp_gate[l], w_exp_up[l], w_exp_down[l])
    return rms_norm(x, g_final)


CONV_WIDTH = 1024
CONV_SIZE = 31
HEAD_DIM = 64
HEADS_PER_GROUP = 8
DILATION_GROUPS = ((128, 1), (512, 4), (2048, 16))
N_GROUPS = len(DILATION_GROUPS)
N_ATT_HEADS = N_GROUPS * HEADS_PER_GROUP
ATT_QKV = N_ATT_HEADS * HEAD_DIM
ATT_OUT = HEADS_PER_GROUP * HEAD_DIM
ROT_DIM = HEAD_DIM // 4
ROPE_THETA_2 = 500000.0
BLOCK = 128
MAX_POS_OFFSET = 4096
EPS = 1e-6
NEG_INF = -1e30

IN_SPLITS_2 = (CONV_WIDTH, CONV_WIDTH, CONV_WIDTH,
             ATT_QKV, ATT_QKV, ATT_QKV, ATT_OUT,
             D_MODEL, D_MODEL)
IN_COLS = sum(IN_SPLITS_2)


def _rmsnorm(x, g):
    xf = x.astype(jnp.float32)
    y = xf * lax.rsqrt(jnp.mean(xf * xf, axis=-1, keepdims=True) + EPS)
    return (y * g.astype(jnp.float32)).astype(x.dtype)

def _layernorm(x, g, b):
    xf = x.astype(jnp.float32)
    mu = jnp.mean(xf, axis=-1, keepdims=True)
    var = jnp.mean(jnp.square(xf - mu), axis=-1, keepdims=True)
    y = (xf - mu) * lax.rsqrt(var + EPS)
    return (y * g.astype(jnp.float32) + b.astype(jnp.float32)).astype(x.dtype)

def _partial_rope(t, positions):
    half = ROT_DIM // 2
    inv_freq = ROPE_THETA_2 ** (-(jnp.arange(half, dtype=jnp.float32) * 2.0 / ROT_DIM))
    ang = positions.astype(jnp.float32)[..., None] * inv_freq
    cos = jnp.cos(ang)[:, :, None, :]
    sin = jnp.sin(ang)[:, :, None, :]
    tf = t.astype(jnp.float32)
    t1, t2 = tf[..., :half], tf[..., half:ROT_DIM]
    out = jnp.concatenate([t1 * cos - t2 * sin, t2 * cos + t1 * sin, tf[..., ROT_DIM:]], axis=-1)
    return out.astype(t.dtype)

def _dilated_window_group(q, k, v, window, dilation):
    b, s, h, e = q.shape
    L = s // dilation
    w_sub = window // dilation
    nb = -(-L // BLOCK)
    lp = nb * BLOCK

    def to_sub(t):
        return t.reshape(b, L, dilation, h, e).transpose(0, 2, 3, 1, 4)

    qs, ks, vs = to_sub(q), to_sub(k), to_sub(v)
    qs = jnp.pad(qs, ((0, 0), (0, 0), (0, 0), (0, lp - L), (0, 0)))
    ks = jnp.pad(ks, ((0, 0), (0, 0), (0, 0), (BLOCK, lp - L), (0, 0)))
    vs = jnp.pad(vs, ((0, 0), (0, 0), (0, 0), (BLOCK, lp - L), (0, 0)))
    qb = qs.reshape(b, dilation, h, nb, BLOCK, e)

    def band(t):
        prev = t[:, :, :, :lp].reshape(b, dilation, h, nb, BLOCK, e)
        cur = t[:, :, :, BLOCK:].reshape(b, dilation, h, nb, BLOCK, e)
        return jnp.concatenate([prev, cur], axis=-2)

    kb, vb = band(ks), band(vs)
    scores = jnp.einsum('bdhnqe,bdhnke->bdhnqk', qb.astype(jnp.float32),
                        kb.astype(jnp.float32)) * (e ** -0.5)
    qi = jnp.arange(BLOCK)[:, None]
    kj = jnp.arange(2 * BLOCK)[None, :]
    dist = qi + BLOCK - kj
    key_idx = jnp.arange(nb)[:, None, None] * BLOCK - BLOCK + kj[None]
    mask = (dist >= 0) & (dist <= w_sub) & (key_idx >= 0)
    scores = jnp.where(mask, scores, NEG_INF)
    m = jnp.max(scores, axis=-1)
    p = jnp.exp(scores - m[..., None])
    den = jnp.sum(p, axis=-1)
    o = jnp.einsum('bdhnqk,bdhnke->bdhnqe', p, vb.astype(jnp.float32)) / den[..., None]

    def from_sub(t):
        tail = t.shape[5:]
        t = t.reshape((b, dilation, h, lp) + tail)[:, :, :, :L]
        t = jnp.moveaxis(t, 3, 1)
        return t.reshape((b, s, h) + tail)

    return from_sub(o), from_sub(m), from_sub(den)

def second_inputs(seed: int = 0) -> dict:
    key = jax.random.key(seed)
    ks = jax.random.split(key, 16)
    f32 = jnp.float32
    x = jax.random.normal(ks[0], (BATCH, SEQ, D_MODEL), f32)
    c = jax.random.normal(ks[1], (BATCH, D_MODEL), f32)
    positions = (jnp.arange(SEQ, dtype=jnp.int32)[None, :]
                 + jax.random.randint(ks[2], (BATCH, 1), 0, MAX_POS_OFFSET, dtype=jnp.int32))
    norm_g = 1.0 + 0.05 * jax.random.normal(ks[3], (DEPTH, D_MODEL), f32)
    w_ada = 0.5 * D_MODEL ** -0.5 * jax.random.normal(ks[4], (DEPTH, D_MODEL, 3 * D_MODEL), f32)
    b_ada = 0.02 * jax.random.normal(ks[5], (DEPTH, 3 * D_MODEL), f32)
    w_in = D_MODEL ** -0.5 * jax.random.normal(ks[6], (DEPTH, D_MODEL, IN_COLS), f32)
    conv_w = CONV_SIZE ** -0.5 * jax.random.normal(ks[7], (DEPTH, CONV_SIZE, CONV_WIDTH), f32)
    conv_b = 0.02 * jax.random.normal(ks[8], (DEPTH, CONV_WIDTH), f32)
    conv_ln_g = 1.0 + 0.05 * jax.random.normal(ks[9], (DEPTH, CONV_WIDTH), f32)
    conv_ln_b = 0.02 * jax.random.normal(ks[10], (DEPTH, CONV_WIDTH), f32)
    w_conv_out = CONV_WIDTH ** -0.5 * jax.random.normal(ks[11], (DEPTH, CONV_WIDTH, D_MODEL), f32)
    w_att_out = ATT_OUT ** -0.5 * jax.random.normal(ks[12], (DEPTH, ATT_OUT, D_MODEL), f32)
    w_o = D_MODEL ** -0.5 * jax.random.normal(ks[13], (DEPTH, D_MODEL, D_MODEL), f32)
    final_g = 1.0 + 0.05 * jax.random.normal(ks[14], (D_MODEL,), f32)
    return {"x": x, "c": c, "positions": positions, "norm_g": norm_g,
            "w_ada": w_ada, "b_ada": b_ada, "w_in": w_in, "conv_w": conv_w,
            "conv_b": conv_b, "conv_ln_g": conv_ln_g, "conv_ln_b": conv_ln_b,
            "w_conv_out": w_conv_out, "w_att_out": w_att_out, "w_o": w_o,
            "final_g": final_g}

def second_block(x, c, positions, norm_g, w_ada, b_ada, w_in, conv_w, conv_b, conv_ln_g,
              conv_ln_b, w_conv_out, w_att_out, w_o, final_g):
    b, s, _ = x.shape
    split_idx = np.cumsum(IN_SPLITS_2)[:-1].tolist()
    for layer in range(DEPTH):
        mod = c @ w_ada[layer] + b_ada[layer]
        shift, scale, gate = [t[:, None, :] for t in jnp.split(mod, 3, axis=-1)]
        h = _rmsnorm(x, norm_g[layer]) * (1.0 + scale) + shift

        proj = h @ w_in[layer]
        (glu_a, glu_b, z_conv, q, k, v, z_att, g_conv, g_att) = jnp.split(proj, split_idx, axis=-1)

        u = glu_a * jax.nn.sigmoid(glu_b)
        u = lax.conv_general_dilated(
            u, conv_w[layer][:, None, :].astype(u.dtype), window_strides=(1,),
            padding=[(CONV_SIZE - 1, 0)], dimension_numbers=('NWC', 'WIO', 'NWC'),
            feature_group_count=CONV_WIDTH) + conv_b[layer]
        u = jax.nn.silu(_layernorm(u, conv_ln_g[layer], conv_ln_b[layer]))
        y_conv = (u * jax.nn.silu(z_conv)) @ w_conv_out[layer]

        q = _partial_rope(q.reshape(b, s, N_ATT_HEADS, HEAD_DIM), positions)
        k = _partial_rope(k.reshape(b, s, N_ATT_HEADS, HEAD_DIM), positions)
        v = v.reshape(b, s, N_ATT_HEADS, HEAD_DIM)
        outs, maxes, dens = [], [], []
        for gi, (window, dilation) in enumerate(DILATION_GROUPS):
            sl = slice(gi * HEADS_PER_GROUP, (gi + 1) * HEADS_PER_GROUP)
            o_g, m_g, d_g = _dilated_window_group(q[:, :, sl], k[:, :, sl], v[:, :, sl],
                                                  window, dilation)
            outs.append(o_g); maxes.append(m_g); dens.append(d_g)
        m_all = jnp.maximum(jnp.maximum(maxes[0], maxes[1]), maxes[2])
        wts = [d_g * jnp.exp(m_g - m_all) for m_g, d_g in zip(maxes, dens)]
        w_sum = wts[0] + wts[1] + wts[2]
        att = (wts[0][..., None] * outs[0] + wts[1][..., None] * outs[1]
               + wts[2][..., None] * outs[2]) / w_sum[..., None]
        att = att.reshape(b, s, ATT_OUT).astype(x.dtype)
        y_att = (att * jax.nn.silu(z_att)) @ w_att_out[layer]

        merged = jax.nn.sigmoid(g_conv) * y_conv + jax.nn.sigmoid(g_att) * y_att
        x = x + gate * (merged @ w_o[layer])
    return _rmsnorm(x, final_g)


def setup_inputs(seed=0):
    out = dict(first_inputs(seed))
    for name, value in second_inputs(seed + 1).items():
        if name != "x":
            out[name + "_2"] = value
    return out


def reference(
    x, mem, positions, g_mix, w_in, g_q_lat, w_q_up, g_kv_lat, w_kv_up, w_fourier, w_out,
    g_mem_q, g_mem_kv, w_mem_q, w_mem_kv, w_mem_o, g_ffn, w_router, w_exp_gate, w_exp_up,
    w_exp_down, g_final, c_2, positions_2, norm_g_2, w_ada_2, b_ada_2, w_in_2, conv_w_2,
    conv_b_2, conv_ln_g_2, conv_ln_b_2, w_conv_out_2, w_att_out_2, w_o_2, final_g_2,
):
    x = first_block(
        x, mem, positions, g_mix, w_in, g_q_lat, w_q_up, g_kv_lat, w_kv_up, w_fourier, w_out,
        g_mem_q, g_mem_kv, w_mem_q, w_mem_kv, w_mem_o, g_ffn, w_router, w_exp_gate, w_exp_up,
        w_exp_down, g_final,
    )
    return second_block(
        x, c_2, positions_2, norm_g_2, w_ada_2, b_ada_2, w_in_2, conv_w_2, conv_b_2,
        conv_ln_g_2, conv_ln_b_2, w_conv_out_2, w_att_out_2, w_o_2, final_g_2,
    )


_drawn_inputs = setup_inputs


def setup_inputs(seed=0):
    import zlib

    import numpy as np

    out = dict(_drawn_inputs(seed))
    spreads = {}
    factors = {'g_mix': 4.673,
     'g_q_lat': 8.0,
     'g_kv_lat': 8.0,
     'g_mem_q': 8.0,
     'g_mem_kv': 7.788,
     'g_ffn': 3.864,
     'g_final': 2.715,
     'norm_g_2': 5.1,
     'b_ada_2': 6.473,
     'conv_b_2': 8.0,
     'conv_ln_g_2': 7.711,
     'conv_ln_b_2': 32.223}
    for name, (base, spread) in spreads.items():
        noise = np.random.default_rng([zlib.crc32(name.encode()), seed]).standard_normal(out[name].shape)
        drawn = base * np.exp(spread * noise) if base else spread * noise
        out[name] = __import__('jax').numpy.asarray(drawn.astype(out[name].dtype))
    for name, factor in factors.items():
        out[name] = (out[name] * factor).astype(out[name].dtype)
    return out
```

```python
from contextlib import ExitStack

import concourse.bass as bass
import numpy as np
from concourse import mybir

F32 = mybir.dt.float32
I32 = mybir.dt.int32
U32 = mybir.dt.uint32
ALU = mybir.AluOpType
ACT = mybir.ActivationFunctionType
AX = mybir.AxisListType

P = 128
S = 1024
D = 1024
T = S // P
KC = D // P
NB = 512
MEM = 256
FW, QL, KVL, ROPE = 512, 384, 256, 32
H1, NOPE, VD = 8, 64, 64
HD1 = NOPE + ROPE
MH, MD = 4, 256
NE, CAP = 16, 128
G2N, H2, E2 = 3, 8, 64
ROT2 = E2 // 4
TAPS = 31
EPS = 1e-6
NEG = -1e30
RING = 3
RADIX = 8

(R_MIX, R_MQ, R_MKV, R_FFN, R_N2, R_SHIFT, R_SCALE, R_GATE, R_CB, R_LNG, R_LNB, R_C, R_QL, R_KVL,
 R_TAP) = range(15)
NROW = R_TAP + TAPS


def constants():
    two_pi = 2 * np.pi
    p, k = np.arange(P)[:, None], np.arange(P)[None, :]
    tw = np.zeros((P, 2, RADIX, 2, P), np.float64)
    for r in range(RADIX):
        ang = two_pi * ((p * (RADIX * k + r)) % S) / S
        tw[:, 0, r, 0], tw[:, 0, r, 1] = np.cos(ang), np.sin(ang)
        flip = -1.0 if r > RADIX // 2 else 1.0
        tw[:, 1, r, 0], tw[:, 1, r, 1] = flip * np.sin(ang), -flip * np.cos(ang)
    c = np.arange(64)
    ang = two_pi * ((c[:, None] * c[None, :]) % 64) / 64
    chan = np.zeros((P, 2, P))
    norm = 1.0 / np.sqrt(S * 64)
    for b in range(2):
        chan[64 * b:64 * b + 64, 0, 64 * b:64 * b + 64] = np.cos(ang) * norm
        chan[64 * b:64 * b + 64, 1, 64 * b:64 * b + 64] = -np.sin(ang) * norm
    f1 = (1.0 / (np.float32(10000.0) ** (np.arange(0, ROPE, 2, dtype=np.float32) / np.float32(ROPE)))).astype(np.float32)
    f2 = (np.float32(500000.0) ** (-(np.arange(ROT2 // 2, dtype=np.float32) * np.float32(2.0) / np.float32(ROT2)))).astype(np.float32)
    freq = np.concatenate([f1, f2])[None, :].repeat(P, 0)
    q, kk = np.arange(P)[:, None], np.arange(P)[None, :]
    prev = np.where(kk >= q, 0.0, NEG)
    cur = np.where(kk <= q, 0.0, NEG)
    pair = np.where((q % 2 == kk % 2) & (kk <= q), 0.0, NEG)
    return {
        "k_ident": np.eye(P, dtype=np.float32),
        "k_twiddle": tw.reshape(P, -1).astype(np.float32),
        "k_chan": chan.reshape(P, -1).astype(np.float32),
        "k_freq": freq.astype(np.float32),
        "k_mask": np.concatenate([prev, cur, pair], 1).astype(np.float32),
    }


class Bank:

    def __init__(self, full, free):
        self.full, self.free = full, free
        self.count = [0] * 8
        self.last = [[] for _ in range(8)]
        self.next = 0
        self.at = {}
        self.order = []

    def add(self, name, pair=False, bank=None):
        if bank is None:
            if pair and self.next % 2:
                self.next = (self.next + 1) % 8
            bank = self.next
            self.next = (self.next + (2 if pair else 1)) % 8
        waits = self.last[bank] + (self.last[bank + 1] if pair else [])
        self.count[bank] += 1
        assert name not in self.at, name
        self.at[name] = (bank, self.count[bank], waits)
        self.last[bank] = [(bank, self.count[bank])]
        if pair:
            self.last[bank + 1] = [(bank, self.count[bank])]
        self.order.append(name)

    def begin(self, pe, name):
        for b, v in self.at[name][2]:
            pe.wait_ge(self.free[b], v)
        return self.at[name][0]

    def end(self, ins, name):
        ins.then_inc(self.full[self.at[name][0]], 1)

    def wait(self, eng, name):
        b, v, _ = self.at[name]
        eng.wait_ge(self.full[b], v)
        return b

    def done(self, ins, name):
        ins.then_inc(self.free[self.at[name][0]], 1)

    def read(self, eng, name):
        b, v, _ = self.at[name]
        eng.wait_ge(self.free[b], v)


def build(nc, A, out):
    sems = {}
    ctx = ExitStack()
    with ctx:
        def sem(name):
            if name not in sems:
                sems[name] = ctx.enter_context(nc.semaphore(name))
            return sems[name]

        full = [sem(f"psum_full{i}") for i in range(8)]
        free = [sem(f"psum_free{i}") for i in range(8)]
        w_full = [sem(f"weights_in{i}") for i in range(RING)]
        bk = Bank(full, free)

        arena = ctx.enter_context(nc.sbuf_tensor("arena", [P, 53200], F32))
        PS = ctx.enter_context(nc.psum_tensor("ps", [P, 8, NB], F32))

        def mem(at, n):
            return arena[:, at:at + n]

        X0, HT0, GA0, GB0, GC0, W0, S0 = 0, 8192, 16384, 24576, 32768, 36864, 49152
        X = mem(X0, 8192).rearrange("p (t d) -> p t d", t=T)
        HT = mem(HT0, 8192).rearrange("p (k s) -> p k s", k=KC)
        ring = [mem(W0 + 4096 * i, 4096) for i in range(RING)]
        at = [S0]

        def small(n):
            at[0] += n
            assert at[0] <= 53200
            return mem(at[0] - n, n)

        ident = small(P)
        cols = small(KC * NROW).rearrange("p (k r) -> p k r", r=NROW)
        NF = 16 * T + 8 * 3 * T
        sin_t, cos_t = small(NF), small(NF)
        router = small(KC * NE).rearrange("p (k e) -> p k e", e=NE)
        HN = [small(D) for _ in range(2)]
        mask = small(3 * P)
        st = small(160)
        half = small(8)
        affine = small(2 * KC)

        def tab1(t_, which):
            return (sin_t if which else cos_t)[:, 16 * t:16 * t + 16]

        dram = {n: nc.dram_tensor(n, s, F32, kind="Internal").ap()
                for n, s in (("h0", (S, D)), ("acc", (S, D)), ("x4", (S, D)),
                             ("num1", (S, 528)), ("num2", (S, 528)))}

        def kcol(w, c0, n):
            return w[:, c0:c0 + n].rearrange("(k p) n -> p k n", p=P)

        w_in, w_in2 = A["w_in"][0], A["w_in_2"][0]
        weights = []

        def wadd(name, src, k, n, last):
            weights.append((name, src, k, n, last))

        wadd("in0", kcol(w_in, 0, NB), 8, NB, ("uf", T - 1))
        wadd("in1", kcol(w_in, NB, NB), 8, NB, ("ub", T - 1))
        wadd("in2", kcol(w_in, 2 * NB, 160), 8, 160, ("ub", T - 1))
        wadd("twiddle", A["k_twiddle"].rearrange("p (k n) -> p k n", k=2), 2, 2048, ("pq", 3, 3))
        wadd("kvup", A["w_kv_up"][0].rearrange("(k p) n -> p k n", p=P), 2, 1024, ("kv", T - 1, 1))
        wadd("qup", A["w_q_up"][0].rearrange("(k p) n -> p k n", p=P), 3, 768, ("q", T - 1, 1))
        for i in range(2):
            wadd(f"out{i}", kcol(A["w_out"][0], NB * i, NB), 8, NB, ("y1", T - 1, i))
        for i in range(4):
            wadd(f"mkv{i}", kcol(A["w_mem_kv"][0], NB * i, NB), 8, NB,
                 ("mk", 4 * i + 3) if i < 2 else ("mv", 1, i - 2))
        for i in range(2):
            wadd(f"mq{i}", kcol(A["w_mem_q"][0], NB * i, NB), 8, NB, ("mq", 4 * i + 3, 1))
        for i in range(2):
            wadd(f"mo{i}", kcol(A["w_mem_o"][0], NB * i, NB), 8, NB, ("ym", T - 1, i))
        for i in range(6):
            wadd(f"ada{i}", kcol(A["w_ada_2"][0], NB * i, NB), 8, NB, ("ada", i))
        n_moe0 = len(weights)
        MOE_W = 6
        n_post = n_moe0 + MOE_W * NE
        post = []

        def padd(name, src, k, n, last):
            post.append((name, src, k, n, last))

        for i in range(2):
            padd(f"ga{i}", kcol(w_in2, NB * i, NB), 8, NB, ("glu_b", i, 3, 1))
            padd(f"gb{i}", kcol(w_in2, D + NB * i, NB), 8, NB, ("glu_b", i, 3, 1))
        GORDER = (1, 2, 0)
        for g in GORDER:
            for j, c in enumerate("qkv"):
                padd(f"{c}{g}", kcol(w_in2, 3072 + 1536 * j + NB * g, NB), 8, NB, ("w" + c, g, T - 1))
        padd("za", kcol(w_in2, 7680, NB), 8, NB, ("za", 3, 1))
        for i in range(2):
            padd(f"gt{i}", kcol(w_in2, 9216 + NB * i, NB), 8, NB, ("gt", 4 * i + 3, 1))
            if i == 0:
                padd("ao", A["w_att_out_2"][0].rearrange("(k p) n -> p k n", p=P), 4, 1024, ("ya", 7, 1))
        for i in range(2):
            padd(f"zc{i}", kcol(w_in2, 2048 + NB * i, NB), 8, NB, ("zc", 4 * i + 3, 1))
        for i in range(2):
            padd(f"gc{i}", kcol(w_in2, 8192 + NB * i, NB), 8, NB, ("gc", 4 * i + 3, 1))
            padd(f"co{i}", kcol(A["w_conv_out_2"][0], NB * i, NB), 8, NB, ("yc", 4 * i + 3, 1))
        for i in range(2):
            padd(f"wo{i}", kcol(A["w_o_2"][0], NB * i, NB), 8, NB, ("y2", T - 1, i))
        seq = {w[0]: i for i, w in enumerate(weights)}
        seq.update({w[0]: n_post + i for i, w in enumerate(post)})
        shape = {w[0]: (w[2], w[3]) for w in weights + post}

        def wslot(n):
            return n % RING

        def wview(name):
            k, n = shape[name]
            return ring[wslot(seq[name])][:, 0:k * n].rearrange("p (k n) -> p k n", k=k)

        def w_wait(pe, name):
            n = seq[name]
            pe.wait_ge(w_full[wslot(n)], 16 * (n // RING + 1))

        bk.add("cols")
        for c in range(2):
            bk.add(("bd", c))
        for t in range(T):
            bk.add(("n1", t, 0)), bk.add(("n1", t, 1))
        for t in range(T):
            bk.add(("uf", t))
        for t in range(T):
            bk.add(("ua", t)), bk.add(("ub", t))
            if t >= 1:
                bk.add(("lt", t - 1, 0)), bk.add(("lt", t - 1, 1))
        bk.add(("lt", T - 1, 0)), bk.add(("lt", T - 1, 1))
        for c in range(4):
            for r in range(4):
                bk.add(("pq", c, r))
            for h in range(2):
                bk.add(("yf", c, h))
        for t in range(T):
            bk.add(("kv", t, 0)), bk.add(("kv", t, 1))
            if t >= 1:
                bk.add(("kt", t - 1, 0)), bk.add(("kt", t - 1, 1))
        bk.add(("kt", T - 1, 0)), bk.add(("kt", T - 1, 1))
        for t in range(T):
            bk.add(("q", t, 0)), bk.add(("q", t, 1))
            if t >= 1:
                bk.add(("qt", t - 1, 0)), bk.add(("qt", t - 1, 1))
        bk.add(("qt", T - 1, 0)), bk.add(("qt", T - 1, 1))

        NS = T * H1

        def att1_steps():
            for n in range(-1, NS + 1):
                if n + 1 < NS:
                    yield "s", n + 1
                if 0 <= n < NS:
                    yield "pt", n
                if n - 1 >= 0:
                    yield "pv", n - 1
                    if (n - 1) % H1 == 2 and n - 1 > H1:
                        yield "y", (n - 1) // H1 - 1
            yield "pv_end", 0
            yield "y", T - 1

        for kind, n in att1_steps():
            t, h = divmod(n, H1)
            if kind == "s":
                bk.add(("s1", n), pair=True, bank=2 * (n % 2))
            elif kind == "pt":
                bk.add(("pt", n, 0), bank=4), bk.add(("pt", n, 1), bank=5)
            elif kind == "pv" and h == 0:
                bk.add(("o1", t), bank=6)
            elif kind == "y":
                bk.add(("ot", n), bank=7)
                bk.add(("y1", n, 0), bank=7), bk.add(("y1", n, 1), bank=7)
        bk.next = 0
        for m in range(2):
            bk.add(("nm", m, 0)), bk.add(("nm", m, 1))
        for c in range(8):
            bk.add(("mk", c))
            bk.add(("n2", c, 0)), bk.add(("n2", c, 1))
        for n in range(2):
            for m in range(2):
                bk.add(("mv", m, n))
        for c in range(8):
            bk.add(("mq", c, 0)), bk.add(("mq", c, 1))

        def att2_steps():
            for t in range(-1, T + 2):
                if t + 1 < T:
                    yield "s", t + 1
                if 0 <= t < T:
                    yield "pt", t
                if t - 1 >= 0 and t - 1 < T:
                    yield "y", t - 1
                if t - 2 >= 0 and t - 2 < T:
                    yield "r", t - 2
                if 0 <= t < T:
                    yield "pv", t

        for kind, t in att2_steps():
            if kind == "s":
                bk.add(("s2", t, 0)), bk.add(("s2", t, 1))
            elif kind == "pt":
                bk.add(("p2", t, 0)), bk.add(("p2", t, 1))
            elif kind == "pv":
                bk.add(("o2", t, 0)), bk.add(("o2", t, 1))
            elif kind == "y":
                bk.add(("om", t, 0)), bk.add(("om", t, 1))
                bk.add(("ym", t, 0)), bk.add(("ym", t, 1))
            else:
                bk.add(("n3", t, 0)), bk.add(("n3", t, 1))
                bk.add(("lg", t))
        for c in range(2):
            bk.add(("aft", c))
        for i in range(6):
            bk.add(("ada", i))
        bk.add(("idx",))
        bk.next = 0
        for c in range(2):
            bk.add(("tr0", c))
        bk.next = 2
        MOE = ("g0", "u0", "g1", "u1", "tr0", "tr1", "d0", "d1")
        MOE_BANK = {k: (2 + i) % 8 for i, k in enumerate(MOE)}
        moe_base = list(bk.count)
        moe_first = [list(x) for x in bk.last]
        for e in range(NE):
            for k in MOE:
                if e == NE - 1 and k.startswith("tr"):
                    continue
                b = MOE_BANK[k]
                bk.count[b] += 1
                bk.last[b] = [(b, bk.count[b])]

        def moe_val(k, e):
            return moe_base[MOE_BANK[k]] + 1 + e

        bk.next = 0
        for t in range(T):
            bk.add(("n4", t, 0)), bk.add(("n4", t, 1))
        for i in range(2):
            for c in range(4):
                for h in range(2):
                    bk.add(("glu_a", i, c, h)), bk.add(("glu_b", i, c, h))
        def keys_of(g, tile):
            if g == 0:
                return [tile] if tile == 0 else [tile - 1, tile]
            if g == 1:
                return [tile] if tile % 2 == 0 else [tile - 1, tile]
            return [tile]

        tiles2 = [(g, t) for g in GORDER for t in range(T)]

        def win_steps():
            for i in range(len(tiles2) + 2):
                if i < len(tiles2):
                    yield "qkv", i
                if i - 2 >= 0 and tiles2[i - 2][0] == 0:
                    yield "at", i - 2
                if 0 <= i - 1 < len(tiles2):
                    yield "att", i - 1

        for kind, i in win_steps():
            g, t = tiles2[i]
            if kind == "qkv":
                bk.add(("wq", g, t)), bk.add(("wk", g, t)), bk.add(("wv", g, t))
                bk.add(("qkt", g, t, 0)), bk.add(("qkt", g, t, 1))
            elif kind == "att":
                for hp in range(4):
                    bk.add(("sw", g, t, hp))
                for hp in range(4):
                    bk.add(("pw", g, t, hp))
                bk.add(("ow", g, t))
            else:
                bk.add(("at", t))
        for c in range(4):
            for h in range(2):
                bk.add(("za", c, h))
        for c in range(8):
            for h in range(2):
                bk.add(("gt", c, h)), bk.add(("ya", c, h))
        for t in range(T + 1):
            if t < T:
                bk.add(("c1", t, 0)), bk.add(("c1", t, 1))
            if t >= 1:
                bk.add(("c2", t - 1, 0)), bk.add(("c2", t - 1, 1))
        for c in range(8):
            for h in range(2):
                bk.add(("zc", c, h))
        for c in range(8):
            for h in range(2):
                bk.add(("gc", c, h)), bk.add(("yc", c, h))
        for t in range(T):
            bk.add(("y2", t, 0)), bk.add(("y2", t, 1))

        uf = mem(GC0, 4096).rearrange("p (t c) -> p t c", t=T)
        gdft = mem(GA0, 4096).rearrange("p (j c) -> p j c", j=8)
        tdft = mem(GB0, 4096).rearrange("p (j c) -> p j c", j=8)
        kvn = mem(GA0 + 4096, 2048).rearrange("p (k s) -> p k s", k=2)
        uq = [mem(GA0 + 6144 + 672 * i, 672) for i in range(2)]
        krt = mem(GA0 + 7488, 256).rearrange("p (t c) -> p t c", t=T)
        mixf = mem(GB0, 4096).rearrange("p (c s) -> p c s", c=4)
        qn = mem(GB0 + 4096, 3072).rearrange("p (k s) -> p k s", k=3)
        bd = mem(GB0 + 7168, 1024).rearrange("p (m c j) -> p m c j", m=2, c=4)
        wbd = mem(GB0, 512).rearrange("p (c j) -> p c j", c=4)
        chan = mem(GB0 + 512, 256).rearrange("p (m j) -> p m j", m=2)
        rows = mem(GB0 + 1024, 1024)
        freq = mem(GB0 + 2048, 24)
        posi = mem(GB0 + 2080, 32).bitcast(I32).rearrange("p (g t) -> p g t", g=4)
        posf = mem(GB0 + 2112, 32).rearrange("p (g t) -> p g t", g=4)
        ang = mem(GB0 + 2176, NF)
        ang2 = mem(GB0 + 2176 + NF, NF)
        pq = mem(HT0, 8192).rearrange("p (c r m k) -> p c r m k", c=4, r=8, m=2)
        KT = arena[0:HD1, HT0:HT0 + 8192].rearrange("p (h s) -> p h s", h=H1)
        QT = arena[0:HD1, GA0:GA0 + 8192].rearrange("p (h s) -> p h s", h=H1)
        V1 = mem(GC0, 4096).rearrange("p (t c) -> p t c", t=T)
        pexp = [mem(GB0 + 4096 + 1024 * i, 1024) for i in range(2)]
        ptr = [mem(GB0 + 6144 + 1024 * i, 1024).rearrange("p (k q) -> p k q", k=8) for i in range(2)]
        o1 = [HN[0][:, 512 * i:512 * i + 512] for i in range(2)]
        mixa = [HN[1][:, 512 * i:512 * i + 512].rearrange("p (c s) -> p c s", c=4) for i in range(2)]
        memx = mem(GA0, 2048).rearrange("p (m d) -> p m d", m=2)
        mnT = mem(GB0 + 2048, 2048).rearrange("p (k s) -> p k s", k=KC)
        KM = mem(GB0 + 4096, 2048).rearrange("p (k s) -> p k s", k=KC)
        VM = mem(GB0 + 6144, 2048).rearrange("p (m d) -> p m d", m=2)
        QM = mem(GA0, 8192).rearrange("p (k s) -> p k s", k=KC)
        p2 = [mem(GC0 + 1024 * i, 1024) for i in range(2)]
        pt2 = [mem(GC0 + 2048 + 1024 * i, 1024) for i in range(2)]
        om = [mem(GB0 + 1024 * i, 1024) for i in range(2)]
        omt = [mem(GB0 + 2048 + 1024 * i, 1024).rearrange("p (k s) -> p k s", k=KC) for i in range(2)]
        rt = [mem(HT0 + 1024 * i, 1024).rearrange("p (k s) -> p k s", k=KC) for i in range(2)]
        aff = mem(HT0 + 2048, P).rearrange("p (t e) -> p t e", e=NE)
        affT = arena[0:NE, HT0 + 3072:HT0 + 4096]
        vals = arena[0:NE, HT0 + 4096:HT0 + 4096 + CAP]
        inds = arena[0:NE, HT0 + 4224:HT0 + 4224 + CAP].bitcast(U32)
        indf = arena[0:NE, HT0 + 4352:HT0 + 4352 + CAP]
        gateT = mem(HT0 + 4480, NE)
        idxT = mem(HT0 + 4496, NE).bitcast(U32)
        idx_g = [mem(HT0 + 4520 + i, 1).bitcast(U32) for i in range(2)]
        idx_s = [mem(HT0 + 4524 + i, 1).bitcast(U32) for i in range(2)]
        xg = [mem(GA0 + 1024 * i, 1024) for i in range(2)]
        xt = [mem(GA0 + 2048 + 1024 * i, 1024).rearrange("p (k s) -> p k s", k=KC) for i in range(2)]
        hid = [mem(GA0 + 4096 + 1024 * i, 1024) for i in range(2)]
        sil = [mem(GA0 + 6144 + 512 * i, 512) for i in range(2)]
        ye = [mem(GB0 + 1024 * i, 1024) for i in range(2)]
        cb = mem(GB0 + 2048, 1024).rearrange("p (k m) -> p k m", k=KC)
        gate_b = mem(X0 + 7168, 1024)
        bgate = mem(GB0 + 4096, 1024)
        gfin = mem(GB0 + 5120, 1024)
        modc = mem(HT0 + 5120, 2 * KC)
        gate_t = mem(GB0 + 6144, 1024)
        U = mem(GA0, 8192).rearrange("p (k s) -> p k s", k=KC)
        sig = [mem(GC0 + 512 * i, 512) for i in range(2)]
        C = mem(GB0, 8192).rearrange("p (k s) -> p k s", k=KC)
        qT2 = [mem(X0 + 512 * i, 512).rearrange("p (h s) -> p h s", h=4) for i in range(2)]
        kT2 = [mem(X0 + 1024 + 512 * i, 512).rearrange("p (h s) -> p h s", h=4) for i in range(3)]
        V2 = [mem(X0 + 2560 + 512 * i, 512) for i in range(3)]
        pw = [mem(X0 + 4096 + 512 * i, 512) for i in range(2)]
        pwt = [mem(X0 + 5120 + 512 * i, 512).rearrange("p (j q) -> p j q", j=4) for i in range(2)]
        num = mem(X0 + 6144, 528)
        rtmp2 = [mem(X0 + 6672 + 128 * i, 128).rearrange("p (h f) -> p h f", f=8) for i in range(3)]
        lst = mem(X0 + 7056, 32)
        wcomb = mem(X0 + 7088, 80)
        qks = HN[0]
        lnum = [HN[1][:, 0:512], HN[1][:, 512:1024]]
        attT = mem(GC0, 4096).rearrange("p (c s) -> p c s", c=4)
        M = mem(GA0, 8192).rearrange("p (k s) -> p k s", k=KC)
        xr = [mem(X0 + 1024 * i, 1024) for i in range(2)]
        junk = mem(X0 + 2048, 1024)
        fg = mem(X0 + 4096, 1024)

        rtmp = [mask[:, 128 * i:128 * i + 128] for i in range(3)]
        negm, rsum, rrec = mask[:, 0:64], mask[:, 64:128], mask[:, 128:192]

        def tile(t):
            return slice(P * t, P * t + P)

        def gain(row, k0, k1, n=P):
            return cols[:, k0:k1, row].unsqueeze(2).to_broadcast([P, k1 - k0, n])

        def b4(b, n=4):
            return PS[:, b, 0:n * P].rearrange("p (k s) -> p k s", k=n)

        def wait_sum(eng, name, v):
            if v > 0:
                eng.wait_ge(sem(name), v)

        class Chain:

            def __init__(self, eng, name):
                self.eng, self.sem, self.n = eng, sem(name), 0

            def __call__(self, ins):
                self.n += 1
                ins.then_inc(self.sem, 1)
                self.eng.wait_ge(self.sem, self.n)

        def pv_wait(eng, n):
            t, h = divmod(n, H1)
            if h == H1 - 1:
                bk.wait(eng, ("o1", t))
            else:
                eng.wait_ge(sem("pv_done"), (H1 - 1) * t + h + 1)

        def win_head(u, j):
            return 4 * (u // 2) + u % 2 + 2 * j

        def num_before(i):
            return sum(16 for g, _ in tiles2[:i] if g != 0)

        def wv_wait(eng, i, hp):
            if hp < 0:
                i, hp = i - 1, hp + 4
                if i < 0:
                    return
            if hp == 3:
                bk.wait(eng, ("ow", *tiles2[i]))
            else:
                eng.wait_ge(sem("wv_done"), 3 * i + hp + 1)

        block = ctx.enter_context(nc.Block())

        @block.sync
        def _(sp):
            def fetch(n, w):
                name, src, k, cnt, _ = w
                if n >= RING:
                    prev = (weights[n - RING] if n - RING < n_moe0 else post[n - RING - n_post])
                    if prev[4] is not None:
                        bk.wait(sp, prev[4])
                if src is not None:
                    dst = ring[wslot(n)][:, 0:k * cnt].rearrange("p (k n) -> p k n", k=k)
                    sp.dma_start(dst, src).then_inc(w_full[wslot(n)], 16)
                else:
                    sp.sem_inc(w_full[wslot(n)], 16)

            for n, w in enumerate(weights):
                fetch(n, w)
            for n in range(n_moe0 - RING, n_moe0):
                if weights[n][4] is not None:
                    bk.wait(sp, weights[n][4])

            def expert_blocks(e):
                for j, (w, c) in enumerate((("gate", 0), ("up", 0), ("gate", 1), ("up", 1), ("down", 0), ("down", 1))):
                    was = ("g0", "u0", "g1", "u1", "d0", "d1")[(j + RING) % MOE_W]
                    sp.wait_ge(full[MOE_BANK[was]], moe_val(was, e) - (1 if j < RING else 0))
                    src = A[f"w_exp_{w}"][0, bass.ds(e, 1), :, NB * c:NB * c + NB].rearrange("o (k p) n -> p (o k) n", p=P)
                    slot = (n_moe0 + j) % RING
                    sp.dma_start(ring[slot].rearrange("p (k n) -> p k n", k=KC), src).then_inc(w_full[slot], 16)

            with sp.Fori(0, NE, 1) as e:
                expert_blocks(e)
            for i, w in enumerate(post):
                if i < RING:
                    was = ("u1", "d0", "d1")[i]
                    sp.wait_ge(full[MOE_BANK[was]], moe_val(was, NE - 1))
                fetch2 = w
                if i >= RING:
                    bk.wait(sp, post[i - RING][4])
                dst = wview(w[0])
                sp.dma_start(dst, w[1]).then_inc(w_full[wslot(n_post + i)], 16)
            for t in range(T):
                sp.wait_ge(sem("out_ready"), t + 1)
                sp.dma_start(out[0, tile(t), :], HN[t % 2]).then_inc(sem(f"out_done{t % 2}"), 16)
            for i in range(2):
                sp.wait_ge(sem(f"out_done{i}"), 16 * (T // 2))

        @block.gpsimd
        def _(pool):
            ch = Chain(pool, "pool_chain")

            def rstd(dst, src, n):
                ch(nc.gpsimd.tensor_scalar(dst, src, 1.0 / n, EPS, ALU.mult, ALU.add))
                return nc.gpsimd.tensor_tensor(dst, dst, half[:, 0:dst.shape[1]], ALU.pow)

            nc.gpsimd.memset(half[:, 0:4], -0.5)
            nc.gpsimd.memset(half[:, 4:8], float(np.pi / 2)).then_inc(sem("halves"), 1)
            nc.gpsimd.memset(wbd, 0.0)
            ch(nc.gpsimd.memset(rows[0:NROW, :], 0.0))
            wf = A["w_fourier"][0].rearrange("(c b) i j -> b i c j", b=2)
            for b in range(2):
                pool.dma_start(wbd[64 * b:64 * b + 64, :, 64 * b:64 * b + 64], wf[b]).then_inc(sem("wbd_in"), 16)
            vecs = [(R_MIX, A["g_mix"]), (R_MQ, A["g_mem_q"]), (R_MKV, A["g_mem_kv"]), (R_FFN, A["g_ffn"]),
                    (R_N2, A["norm_g_2"]), (R_CB, A["conv_b_2"]), (R_LNG, A["conv_ln_g_2"]),
                    (R_LNB, A["conv_ln_b_2"]), (R_C, A["c_2"]), (R_QL, A["g_q_lat"]), (R_KVL, A["g_kv_lat"])]
            for r, v in vecs:
                pool.dma_start(rows[r:r + 1, 0:v.shape[1]], v).then_inc(sem("rows_in"), 16)
            pool.dma_start(rows[R_SHIFT:R_SHIFT + 3, :], A["b_ada_2"][0].rearrange("(r d) -> r d", r=3)).then_inc(sem("rows_in"), 16)
            pool.dma_start(rows[R_TAP:R_TAP + TAPS, :], A["conv_w_2"][0]).then_inc(sem("rows_in"), 16)

            for t in range(T):
                pool.wait_ge(sem("n1_ssq"), t + 1)
                rstd(st[:, 8 + t:9 + t], st[:, t:t + 1], D).then_inc(sem("n1_rstd"), 1)

            c8 = float(np.sqrt(0.5))
            X8 = [uf[:, t, :] for t in range(8)]
            td = [tdft[:, j, :] for j in range(8)]
            G = [gdft[:, j, :] for j in range(8)]
            tt = nc.gpsimd.tensor_tensor
            s_, d_ = td[0:4], td[4:8]
            steps = []
            for j in range(4):
                steps.append(lambda j=j: tt(s_[j], X8[j], X8[j + 4], ALU.add))
                steps.append(lambda j=j: tt(d_[j], X8[j], X8[j + 4], ALU.subtract))
            steps += [
                lambda: tt(G[2], s_[0], s_[2], ALU.subtract),
                lambda: tt(G[3], s_[3], s_[1], ALU.subtract),
                lambda: tt(s_[0], s_[0], s_[2], ALU.add),
                lambda: tt(s_[1], s_[1], s_[3], ALU.add),
                lambda: tt(G[0], s_[0], s_[1], ALU.add),
                lambda: tt(G[1], s_[0], s_[1], ALU.subtract),
                lambda: tt(s_[2], d_[1], d_[3], ALU.subtract),
                lambda: tt(s_[3], d_[1], d_[3], ALU.add),
                lambda: nc.gpsimd.tensor_scalar(s_[2], s_[2], c8, 0.0, ALU.mult, ALU.add),
                lambda: nc.gpsimd.tensor_scalar(s_[3], s_[3], c8, 0.0, ALU.mult, ALU.add),
                lambda: tt(G[4], d_[0], s_[2], ALU.add),
                lambda: tt(G[6], d_[0], s_[2], ALU.subtract),
                lambda: tt(G[7], d_[2], s_[3], ALU.subtract),
                lambda: tt(d_[2], d_[2], s_[3], ALU.add),
                lambda: nc.gpsimd.tensor_scalar(G[5], d_[2], -1.0, 0.0, ALU.mult, ALU.add),
            ]
            bk.read(pool, ("uf", T - 1))
            pool.wait_ge(sem("tables"), 1)
            bk.read(pool, ("bd", 1))
            bk.read(pool, "cols")
            for t in range(T):
                pool.wait_ge(sem("l_ssq"), 2 * t + 2)
                a, b = st[:, 16 + 2 * t:17 + 2 * t], st[:, 17 + 2 * t:18 + 2 * t]
                ra, rb = st[:, 32 + 2 * t:33 + 2 * t], st[:, 33 + 2 * t:34 + 2 * t]
                nc.gpsimd.tensor_scalar(ra, a, 1.0 / QL, EPS, ALU.mult, ALU.add)
                ch(nc.gpsimd.tensor_scalar(rb, b, 1.0 / KVL, EPS, ALU.mult, ALU.add))
                r2 = st[:, 32 + 2 * t:34 + 2 * t]
                nc.gpsimd.tensor_tensor(r2, r2, half[:, 0:2], ALU.pow).then_inc(sem("l_rstd"), 1)
                for f in steps[3 * t:3 * t + 3]:
                    ch(f())
            pool.sem_inc(sem("dft_done"), 1)

            for t in range(T):
                if t >= 2:
                    bk.wait(pool, ("kt", t - 2, 1))
                else:
                    bk.wait(pool, ("lt", T - 2 + t, 1))
                pool.wait_ge(sem("kr_done"), t + 1)
                kt_ = HN[t % 2][:, 0:H1 * HD1].rearrange("p (h c) -> p h c", h=H1)
                nc.gpsimd.tensor_copy(kt_[:, :, NOPE:HD1], krt[:, t, :].unsqueeze(1).to_broadcast([P, H1, ROPE])).then_inc(sem("k_rope"), 1)

            bk.wait(pool, ("s1", NS - 1))
            for m in range(2):
                pool.dma_start(memx[:, m, :], A["mem"][0, tile(m), :]).then_inc(sem(f"mem_in{m}"), 16)
            for m in range(2):
                pool.wait_ge(sem("nm_ssq"), m + 1)
                rstd(st[:, 50 + m:51 + m], st[:, 48 + m:49 + m], D).then_inc(sem("nm_rstd"), 1)
            for t in range(T):
                pool.wait_ge(sem("n2_ssq"), t + 1)
                rstd(st[:, 60 + t:61 + t], st[:, 52 + t:53 + t], D).then_inc(sem("n2_rstd"), 1)
            for t in range(T):
                bk.read(pool, ("ym", t, 1))
                pool.dma_start(dram["acc"][tile(t), :], X[:, t, :]).then_inc(sem("acc_out"), 16)
                pool.wait_ge(sem("n3_ssq"), t + 1)
                rstd(st[:, 76 + t:77 + t], st[:, 68 + t:69 + t], D).then_inc(sem("n3_rstd"), 1)
                pool.wait_ge(sem("n3_hn"), t + 1)
                pool.dma_start(dram["h0"][tile(t), :], HN[t % 2]).then_inc(sem(f"h0_out{t % 2}"), 16)
            nc.gpsimd.tensor_copy(cb, cols[:, :, R_C:R_C + 1].to_broadcast([P, KC, P])).then_inc(sem("c_wide"), 1)
            bcast = lambda v: v.rearrange("(o d) -> o d", o=1).to_broadcast([P, D])
            pool.dma_start(bgate, bcast(A["b_ada_2"][0, 2 * D:3 * D])).then_inc(sem("wide_in"), 16)
            pool.dma_start(gfin, bcast(A["g_final"])).then_inc(sem("wide_in"), 16)
            pool.dma_start(mask, A["k_mask"]).then_inc(sem("mask_in"), 16)
            for i in range(4):
                bk.read(pool, ("ada", i))
            mv_ = modc.rearrange("p (m k) -> p m k", m=2)
            av_ = affine.rearrange("p (m k) -> p m k", m=2)
            nc.gpsimd.tensor_tensor(av_[:, 1, :], mv_[:, 0, :], cols[:, :, R_SHIFT], ALU.add)
            ch(nc.gpsimd.tensor_tensor(av_[:, 0, :], mv_[:, 1, :], cols[:, :, R_SCALE], ALU.add))
            ch(nc.gpsimd.tensor_scalar(av_[:, 0, :], av_[:, 0, :], 1.0, 0.0, ALU.add, ALU.add))
            nc.gpsimd.tensor_tensor(av_[:, 0, :], av_[:, 0, :], cols[:, :, R_N2], ALU.mult).then_inc(sem("affine"), 1)
            bk.read(pool, ("ada", 5))
            pool.wait_ge(sem("wide_in"), 32)
            nc.gpsimd.tensor_tensor(gate_t, gate_t, bgate, ALU.add).then_inc(sem("gate"), 1)

            def gather(e, par, k, wait):
                if wait is not None:
                    wait()
                nc.gpsimd.tensor_copy(idx_g[par], idxT[:, bass.ds(e, 1)]).then_inc(sem("idx_g"), 1)
                pool.wait_ge(sem("idx_g"), e + 1)
                pool.sem_inc(sem("pool_step"), 1)
                pool.indirect_dma_start(xg[par], None, dram["h0"], bass.IndirectOffsetOnAxis(ap=idx_g[par], axis=0)).then_inc(sem(f"xg_in{par}"), 16)

            def scatter(e, par):
                pool.wait_ge(sem("scattered"), 16 * e)
                nc.gpsimd.tensor_copy(idx_s[par], idxT[:, bass.ds(e, 1)]).then_inc(sem("idx_s"), 1)
                pool.wait_ge(sem("idx_s"), e + 1)
                pool.wait_ge(sem("y_ready"), 2 * e + 2)
                pool.sem_inc(sem("pool_step"), 1)
                pool.indirect_dma_start(dram["acc"], bass.IndirectOffsetOnAxis(ap=idx_s[par], axis=0), ye[par], None, compute_op=ALU.add).then_inc(sem("scattered"), 16)

            bk.read(pool, ("idx",))
            for i in range(2):
                pool.wait_ge(sem(f"h0_out{i}"), 16 * (T // 2))
            pool.wait_ge(sem("acc_out"), 16 * T)
            gather(0, 0, 0, None)
            gather(1, 1, 0, None)

            def scatter_first(par):
                nc.gpsimd.tensor_copy(idx_s[par], idxT[:, 0:1]).then_inc(sem("idx_s"), 1)
                pool.wait_ge(sem("idx_s"), 1)
                pool.wait_ge(sem("y_ready"), 2)
                pool.indirect_dma_start(dram["acc"], bass.IndirectOffsetOnAxis(ap=idx_s[par], axis=0), ye[par], None, compute_op=ALU.add).then_inc(sem("scattered"), 16)

            scatter_first(0)
            bk.wait(pool, ("tr0", 1))
            gather(2, 0, 0, None)
            with pool.Fori(0, (NE - 4) // 2 + 0, 1) as j:
                for sub in range(2):
                    e = 2 * j + 1 + sub
                    par = (1 + sub) % 2
                    scatter(e, par)
                    pool.wait_ge(full[MOE_BANK["tr1"]], moe_val("tr1", e - 1))
                    gather(e + 2, par, 0, None)
            for e in range(NE - 3, NE):
                scatter(e, e % 2)
                if e + 2 < NE:
                    pool.wait_ge(full[MOE_BANK["tr1"]], moe_val("tr1", e - 1))
                    gather(e + 2, e % 2, 0, None)
            pool.wait_ge(sem("scattered"), 16 * NE)
            for t in range(T):
                pool.dma_start(X[:, t, :], dram["acc"][tile(t), :]).then_inc(sem(f"x_back{t}"), 16)
            for t in range(T):
                pool.wait_ge(sem("n4a_ssq"), t + 1)
                rstd(st[:, 92 + t:93 + t], st[:, 84 + t:85 + t], D).then_inc(sem("n4a_rstd"), 1)
                pool.wait_ge(sem("n4a_x"), t + 1)
                pool.dma_start(dram["x4"][tile(t), :], X[:, t, :]).then_inc(sem("x4_out"), 16)
                pool.wait_ge(sem("n4b_ssq"), t + 1)
                rstd(st[:, 108 + t:109 + t], st[:, 100 + t:101 + t], D).then_inc(sem("n4b_rstd"), 1)

            pending = 0
            for i, (g, t) in enumerate(tiles2):
                if g != 0:
                    pool.wait_ge(sem("num_ready"), i + 1)
                    if g == 1:
                        r, b = divmod(t, 2)
                        dst = dram["num1"].rearrange("(b j r) c -> b r j c", b=2, r=4)[b, r]
                        pool.dma_start(dst, num).then_inc(sem("num_out"), 16)
                        pending += 16
                    else:
                        dst = dram["num2"].rearrange("(j m) c -> m j c", m=8)[t]
                        pool.dma_start(dst, num).then_inc(sem("num_out"), 16)
                        pending += 16
            pool.wait_ge(sem("num_out"), pending)
            for t in range(T):
                if t >= 1:
                    pool.wait_ge(sem("comb_done"), t)
                for gi, n in enumerate(("num1", "num2")):
                    pool.dma_start(lnum[gi], dram[n][tile(t), 0:512]).then_inc(sem("lnum_in"), 16)
                    pool.dma_start(lst[:, 16 * gi:16 * gi + 16], dram[n][tile(t), 512:528]).then_inc(sem("lnum_in"), 16)

            for t in range(T):
                pool.wait_ge(sem("ln_var"), t + 1)
                v = st[:, 16 + 2 * t + 1:16 + 2 * t + 2]
                ch(nc.gpsimd.tensor_scalar(st[:, 32 + t:33 + t], v, 1.0, EPS, ALU.mult, ALU.add))
                nc.gpsimd.tensor_tensor(st[:, 32 + t:33 + t], st[:, 32 + t:33 + t], half[:, 0:1], ALU.pow).then_inc(sem("ln_rstd"), 1)
            bk.wait(pool, ("at", T - 1))
            pool.dma_start(fg, bcast(A["final_g_2"])).then_inc(sem("fg_in"), 16)
            pool.wait_ge(sem("x4_out"), 16 * T)
            for t in range(T):
                if t >= 2:
                    pool.wait_ge(sem("xr_used"), t - 1)
                pool.dma_start(xr[t % 2], dram["x4"][tile(t), :]).then_inc(sem(f"xr_in{t % 2}"), 16)
                if t >= 1:
                    pool.wait_ge(sem("n5_ssq"), t)
                    rstd(st[:, 60 + t - 1:60 + t], st[:, 52 + t - 1:52 + t], D).then_inc(sem("n5_rstd"), 1)
            pool.wait_ge(sem("n5_ssq"), T)
            rstd(st[:, 60 + T - 1:60 + T], st[:, 52 + T - 1:52 + T], D).then_inc(sem("n5_rstd"), 1)

        @block.scalar
        def _(act):
            ch = Chain(act, "act_chain")

            def copy(name, dst, src, scale=1.0):
                ins = nc.scalar.activation(dst, src, ACT.Copy, scale=scale)
                bk.done(ins, name)

            act.dma_start(ident, A["k_ident"]).then_inc(sem("ident_in"), 16)
            for t in range(T):
                act.dma_start(X[:, t, :], A["x"][0, tile(t), :]).then_inc(sem(f"x_in{t}"), 16)
                if t == 0:
                    act.dma_start(chan, A["k_chan"].rearrange("p (m j) -> p m j", m=2)).then_inc(sem("chan_in"), 16)
                    act.dma_start(freq, A["k_freq"]).then_inc(sem("pos_in"), 16)
                    with nc.allow_non_contiguous_dma("positions"):
                        act.dma_start(posi[:, 0, :], A["positions"].rearrange("o (t p) -> p (o t)", p=P)).then_inc(sem("pos_in"), 16)
                        act.dma_start(posi[:, 1, :], A["positions_2"].rearrange("o (t p) -> p (o t)", p=P)).then_inc(sem("pos_in"), 16)
                        for b in range(2):
                            act.dma_start(posi[:, 2, b:8:2], A["positions_2"][0].rearrange("(b j r) -> b j r", b=2, r=4)[b]).then_inc(sem("pos_in"), 16)
                        act.dma_start(posi[:, 3, :], A["positions_2"][0].rearrange("(j m) -> j m", m=8)).then_inc(sem("pos_in"), 16)
                    act.dma_start(router, A["w_router"][0].rearrange("(k p) e -> p k e", p=P)).then_inc(sem("router_in"), 16)

            act.wait_ge(sem("ang"), 1)
            act.wait_ge(sem("halves"), 1)
            nc.scalar.activation(sin_t, ang, ACT.Sin)
            nc.scalar.activation(cos_t, ang2, ACT.Sin, bias=half[:, 4:5], scale=-1.0).then_inc(sem("tables"), 1)
            for m in range(2):
                b = bk.wait(act, ("bd", m))
                copy(("bd", m), bd[:, m], b4(b))

            def square(src, n, acc, jk):
                return nc.scalar.activation(jk[:, 0:n], src, ACT.Square, accum_out=acc)

            for t in range(T):
                act.wait_ge(sem(f"x_in{t}"), 16)
                if t >= 2:
                    bk.wait(act, ("n1", t - 2, 1))
                square(X[:, t, :], D, st[:, t:t + 1], HN[t % 2]).then_inc(sem("n1_ssq"), 1)
            for t in range(T):
                b = bk.wait(act, ("uf", t))
                copy(("uf", t), uf[:, t, :], PS[:, b, :])
            for t in range(T):
                if t >= 2:
                    act.wait_ge(sem("l_hn"), t - 1)
                b = bk.wait(act, ("ua", t))
                copy(("ua", t), uq[t % 2][:, 0:512], PS[:, b, :])
                b = bk.wait(act, ("ub", t))
                copy(("ub", t), uq[t % 2][:, 512:672], PS[:, b, 0:160])
                bk.read(act, ("ua", t)), bk.read(act, ("ub", t))
                bk.wait(act, ("lt", t - 2, 1) if t >= 2 else ("n1", T - 2 + t, 1))
                square(uq[t % 2][:, 0:QL], QL, st[:, 16 + 2 * t:17 + 2 * t], HN[t % 2]).then_inc(sem("l_ssq"), 1)
                square(uq[t % 2][:, QL:QL + KVL], KVL, st[:, 17 + 2 * t:18 + 2 * t], HN[t % 2][:, QL:QL + KVL]).then_inc(sem("l_ssq"), 1)
            for c in range(4):
                for r in (0, 2):
                    b = bk.wait(act, ("pq", c, r))
                    copy(("pq", c, r), pq[:, c, 2 * r:2 * r + 2, :, :].rearrange("p r m k -> p (r m k)"), PS[:, b, :])
                for h in range(2):
                    b = bk.wait(act, ("yf", c, h))
                    copy(("yf", c, h), mixf[:, c, :].rearrange("p (k r) -> p r k", r=8)[:, 4 * h:4 * h + 4, :], b4(b))
            act.wait_ge(sem("dft_done"), 1)
            for t in range(T):
                bk.wait(act, ("kt", t - 2, 1) if t >= 2 else ("lt", T - 2 + t, 1))
                ktok = HN[t % 2][:, 0:H1 * HD1].rearrange("p (h c) -> p h c", h=H1)
                for j in range(2):
                    b = bk.wait(act, ("kv", t, j))
                    nc.scalar.activation(V1[:, t, 256 * j:256 * j + 256].rearrange("p (h c) -> p h c", h=4), b4(b)[:, :, 64:128], ACT.Copy)
                    copy(("kv", t, j), ktok[:, 4 * j:4 * j + 4, 0:NOPE], b4(b)[:, :, 0:64])
            for t in range(T + 1):
                if t < T:
                    bk.wait(act, ("qt", t - 2, 1) if t >= 2 else ("kt", T - 2 + t, 1))
                    b = bk.wait(act, ("q", t, 0))
                    copy(("q", t, 0), HN[t % 2][:, 0:512], PS[:, b, :])
                    b = bk.wait(act, ("q", t, 1))
                    copy(("q", t, 1), HN[t % 2][:, 512:768], PS[:, b, 0:256])
                if t >= 1:
                    for j in range(2):
                        b = bk.wait(act, ("qt", t - 1, j))
                        copy(("qt", t - 1, j), QT[:, 4 * j:4 * j + 4, tile(t - 1)], b4(b)[0:HD1], scale=HD1 ** -0.5)
            for kind, n in att1_steps():
                if kind == "s":
                    act.wait_ge(sem("a_max"), n + 1)
                    if n >= 2:
                        bk.wait(act, ("pt", n - 2, 1))
                    b = bk.wait(act, ("s1", n))
                    ins = nc.scalar.activation(pexp[n % 2], PS[:, b:b + 2, :].rearrange("p b n -> p (b n)"), ACT.Exp, bias=negm[:, n:n + 1], accum_out=rsum[:, n:n + 1])
                    bk.done(ins, ("s1", n))
                elif kind == "pt":
                    if n >= 2:
                        pv_wait(act, n - 2)
                    b = bk.wait(act, ("pt", n, 0))
                    copy(("pt", n, 0), ptr[n % 2][:, 0:4, :], b4(b))
                elif kind == "y":
                    b = bk.wait(act, ("ot", n))
                    copy(("ot", n), mixa[n % 2], b4(b))
            for m in range(2):
                act.wait_ge(sem(f"mem_in{m}"), 16)
                bk.wait(act, ("y1", T - 1, 1))
                square(memx[:, m, :], D, st[:, 48 + m:49 + m], HN[m]).then_inc(sem("nm_ssq"), 1)
            for c in range(8):
                bk.read(act, ("y1", c, 1))
                bk.wait(act, ("n2", c - 2, 1) if c >= 2 else ("nm", c, 1))
                square(X[:, c, :], D, st[:, 52 + c:53 + c], HN[c % 2]).then_inc(sem("n2_ssq"), 1)
                b = bk.wait(act, ("mk", c))
                copy(("mk", c), KM[:, c, :], PS[:, b, 0:MEM])
            for n in range(2):
                for m in range(2):
                    b = bk.wait(act, ("mv", m, n))
                    copy(("mv", m, n), VM[:, m, NB * n:NB * n + NB], PS[:, b, :])
            for c in range(8):
                for h in range(2):
                    b = bk.wait(act, ("mq", c, h))
                    copy(("mq", c, h), QM[:, c, NB * h:NB * h + NB], PS[:, b, :], scale=MD ** -0.5)
            for kind, t in att2_steps():
                if kind == "s":
                    if t >= 2:
                        bk.wait(act, ("p2", t - 2, 1))
                    for hp in range(2):
                        act.wait_ge(sem("m_max"), 2 * t + hp + 1)
                        b = bk.wait(act, ("s2", t, hp))
                        for hh in range(2):
                            i = 4 * t + 2 * hp + hh
                            ins = nc.scalar.activation(p2[t % 2][:, 256 * (2 * hp + hh):256 * (2 * hp + hh) + 256], PS[:, b, 256 * hh:256 * hh + 256], ACT.Exp, bias=negm[:, i:i + 1], accum_out=rsum[:, i:i + 1])
                        bk.done(ins, ("s2", t, hp))
                elif kind == "pt":
                    if t >= 2:
                        bk.wait(act, ("o2", t - 2, 0))
                    b = bk.wait(act, ("p2", t, 0))
                    copy(("p2", t, 0), pt2[t % 2][:, 0:512], PS[:, b, :])
                elif kind == "y":
                    if t >= 2:
                        bk.wait(act, ("ym", t - 2, 1))
                    for j in range(2):
                        b = bk.wait(act, ("om", t, j))
                        copy(("om", t, j), omt[t % 2][:, 4 * j:4 * j + 4, :], b4(b))
                elif kind == "r":
                    bk.read(act, ("ym", t, 1))
                    if t >= 2:
                        act.wait_ge(sem(f"h0_out{t % 2}"), 16 * (t // 2))
                    bk.wait(act, ("n3", t - 2, 1) if t >= 2 else ("n2", T - 2 + t, 1))
                    square(X[:, t, :], D, st[:, 68 + t:69 + t], HN[t % 2]).then_inc(sem("n3_ssq"), 1)
                    act.wait_ge(sem("r_max"), t + 1)
                    b = bk.wait(act, ("lg", t))
                    ins = nc.scalar.activation(aff[:, t, :], PS[:, b, 0:NE], ACT.Exp, bias=st[:, 120 + t:121 + t], accum_out=st[:, 128 + t:129 + t])
                    bk.done(ins, ("lg", t))
            for c in range(2):
                b = bk.wait(act, ("aft", c))
                copy(("aft", c), affT[:, NB * c:NB * c + NB], PS[0:NE, b, :])
            for i in range(6):
                b = bk.wait(act, ("ada", i))
                if i < 4:
                    copy(("ada", i), modc[:, 4 * i:4 * i + 4], PS[:, b, 0:4])
                else:
                    copy(("ada", i), gate_t[:, NB * (i - 4):NB * (i - 4) + NB], PS[:, b, :])

            def expert(e, par, e1):
                for i in range(2):
                    act.wait_ge(full[MOE_BANK[f"g{i}"]], moe_val(f"g{i}", e))
                    act.wait_ge(free[MOE_BANK[f"u{i}"]], moe_val(f"u{i}", e) - 1)
                    nc.scalar.activation(sil[i], PS[:, MOE_BANK[f"g{i}"], :], ACT.Silu).then_inc(free[MOE_BANK[f"g{i}"]], 1)
                if e1:
                    act.wait_ge(sem("scattered"), 16 * (e - 1))
                for i in range(2):
                    act.wait_ge(full[MOE_BANK[f"d{i}"]], moe_val(f"d{i}", e))
                    act.sem_inc(sem("act_step"), 1)
                    ins = nc.scalar.activation(ye[par][:, NB * i:NB * i + NB], PS[:, MOE_BANK[f"d{i}"], :], ACT.Copy, scale=gateT[:, bass.ds(e, 1)])
                    ins.then_inc(free[MOE_BANK[f"d{i}"]], 1)
                    act.wait_ge(free[MOE_BANK[f"d{i}"]], moe_val(f"d{i}", e))
                    act.sem_inc(sem("y_ready"), 1)

            bk.read(act, ("idx",))
            for e in range(2):
                expert(e, e, False)
            with act.Fori(1, NE // 2, 1) as j:
                for sub in range(2):
                    expert(2 * j + sub, sub, True)

            for t in range(T):
                act.wait_ge(sem(f"x_back{t}"), 16)
                bk.wait(act, ("n4", t - 2, 1) if t >= 2 else ("n3", T - 2 + t, 1))
                square(X[:, t, :], D, st[:, 84 + t:85 + t], HN[t % 2]).then_inc(sem("n4a_ssq"), 1)
                act.wait_ge(sem("n4a_x"), t + 1)
                square(X[:, t, :], D, st[:, 100 + t:101 + t], HN[t % 2]).then_inc(sem("n4b_ssq"), 1)
            n = 0
            for i in range(2):
                for c in range(4):
                    for h in range(2):
                        b = bk.wait(act, ("glu_b", i, c, h))
                        if n >= 2:
                            bk.read(act, ("glu_a", (n - 2) // 8, (n - 2) // 2 % 4, n % 2))
                        ins = nc.scalar.activation(sig[n % 2], PS[:, b, :], ACT.Sigmoid)
                        bk.done(ins, ("glu_b", i, c, h))
                        n += 1
            act.wait_ge(sem("x4_out"), 16 * T)
            for kind, i in win_steps():
                g, t = tiles2[i]
                if kind == "qkv":
                    if i >= 1:
                        bk.wait(act, ("qkt", *tiles2[i - 1], 1))
                    for j, nm in enumerate("qk"):
                        b = bk.wait(act, ("w" + nm, g, t))
                        copy(("w" + nm, g, t), qks[:, 512 * j:512 * j + 512], PS[:, b, :])
                    if i >= 3:
                        bk.wait(act, ("ow", *tiles2[i - 2]))
                    b = bk.wait(act, ("wv", g, t))
                    copy(("wv", g, t), V2[i % 3], PS[:, b, :])
                    if i >= 2:
                        bk.wait(act, ("sw", *tiles2[i - 2], 3))
                    b = bk.wait(act, ("qkt", g, t, 0))
                    copy(("qkt", g, t, 0), qT2[i % 2], b4(b), scale=E2 ** -0.5)
                    b = bk.wait(act, ("qkt", g, t, 1))
                    copy(("qkt", g, t, 1), kT2[i % 3], b4(b))
                elif kind == "att":
                    w = P * len(keys_of(g, t))
                    for hp in range(4):
                        m = 4 * i + hp
                        for hh in range(2):
                            h = win_head(hp, hh)
                            act.wait_ge(sem("w_max"), m + 1)
                            p_ = pw[hp % 2][:, w * hh:w * hh + w]
                            ins = nc.scalar.activation(p_, p_, ACT.Exp, bias=num[:, 512 + h:513 + h], accum_out=num[:, 520 + h:521 + h])
                        ins.then_inc(sem("w_exp"), 1)
                    if g == 0:
                        act.wait_ge(sem("c_diff"), t + 1)
                        nc.scalar.activation(wcomb[:, 0:24], wcomb[:, 0:24], ACT.Exp).then_inc(sem("c_exp"), 1)
                else:
                    b = bk.wait(act, ("at", t))
                    copy(("at", t), attT[:, :, tile(t)], b4(b))
            tmp = [HN[i][:, 0:512] for i in range(2)]
            m = 0
            bk.wait(act, ("at", T - 1))
            for c in range(4):
                for h in range(2):
                    b = bk.wait(act, ("za", c, h))
                    wait_sum(act, "tmp_used", m - 1)
                    ins = nc.scalar.activation(tmp[m % 2], PS[:, b, :], ACT.Silu)
                    bk.done(ins, ("za", c, h))
                    m += 1
            for c in range(8):
                for h in range(2):
                    b = bk.wait(act, ("gt", c, h))
                    wait_sum(act, "tmp_used", m - 1)
                    ins = nc.scalar.activation(tmp[m % 2], PS[:, b, :], ACT.Sigmoid)
                    bk.done(ins, ("gt", c, h))
                    m += 1
            for t in range(T):
                for j in range(2):
                    act.wait_ge(sem("ln_aff"), 2 * t + j + 1)
                    nc.scalar.activation(C[:, 4 * j:4 * j + 4, tile(t)], C[:, 4 * j:4 * j + 4, tile(t)], ACT.Silu).then_inc(sem("ln_silu"), 1)
            bk.wait(act, ("c2", T - 1, 1))
            for c in range(8):
                for h in range(2):
                    b = bk.wait(act, ("zc", c, h))
                    wait_sum(act, "tmp_used", m - 1)
                    ins = nc.scalar.activation(tmp[m % 2], PS[:, b, :], ACT.Silu)
                    bk.done(ins, ("zc", c, h))
                    m += 1
            for c in range(8):
                for h in range(2):
                    b = bk.wait(act, ("gc", c, h))
                    wait_sum(act, "tmp_used", m - 1)
                    ins = nc.scalar.activation(tmp[m % 2], PS[:, b, :], ACT.Sigmoid)
                    bk.done(ins, ("gc", c, h))
                    m += 1
            for t in range(T):
                act.wait_ge(sem("y2_sum"), 2 * t + 2)
                if t >= 1:
                    act.wait_ge(sem("n5_ssq"), t)
                square(HN[t % 2], D, st[:, 52 + t:53 + t], junk).then_inc(sem("n5_ssq"), 1)

        @block.vector
        def _(dve):
            v = nc.vector
            ch = Chain(dve, "dve_chain")
            bcs = lambda a, n: a.unsqueeze(2).to_broadcast([P, a.shape[1], n])

            dve.wait_ge(sem("pos_in"), 16 * 6)
            ch(v.tensor_copy(posf, posi))
            ang_1 = ang[:, 0:16 * T].rearrange("p (t f) -> p t f", f=16)
            ang_2 = ang[:, 16 * T:NF].rearrange("p (t f) -> p t f", f=8)
            v.tensor_tensor(ang_1, bcs(posf[:, 0, :], 16), freq[:, 0:16].unsqueeze(1).to_broadcast([P, T, 16]), ALU.mult)
            ch(v.tensor_tensor(ang_2, bcs(posf[:, 1:4, :].rearrange("p g t -> p (g t)"), 8), freq[:, 16:24].unsqueeze(1).to_broadcast([P, 3 * T, 8]), ALU.mult))
            ch(v.tensor_scalar(ang2, ang, float(1 / (2 * np.pi)), None, ALU.mult))
            magic = float(1.5 * 2 ** 23)
            ch(v.tensor_scalar(ang2, ang2, magic, None, ALU.add))
            ch(v.tensor_scalar(ang2, ang2, magic, None, ALU.subtract))
            rest = 2 * np.pi
            for bits in (6, 14, 22, None):
                part = float(np.float32(rest)) if bits is None else float(np.floor(rest * 2.0 ** bits) / 2.0 ** bits)
                rest -= part
                ch(v.scalar_tensor_tensor(ang, ang2, -part, ang, ALU.mult, ALU.add))
            pi = float(np.float32(np.pi))
            ch(v.tensor_scalar(ang, ang, pi, -pi, ALU.min, ALU.max))
            ch(v.tensor_scalar(ang2, ang, -1.0, None, ALU.mult))
            v.tensor_tensor(ang2, ang2, ang, ALU.max).then_inc(sem("ang"), 1)
            b = bk.wait(dve, "cols")
            bk.done(v.tensor_copy(cols, PS[:, b, 0:KC * NROW].rearrange("p (k r) -> p k r", r=NROW)), "cols")
            bk.read(dve, "cols")

            def scaled(name, t, src, dst, rs):
                dve.wait_ge(sem(name + "_rstd"), t + 1)
                v.tensor_scalar(dst, src, rs, None, ALU.mult).then_inc(sem(name + "_hn"), 1)

            def gained(name, dst, row, k0, n=4):
                b = bk.wait(dve, name)
                bk.done(v.tensor_tensor(dst, b4(b, n), gain(row, k0, k0 + n), ALU.mult), name)

            for t in range(T + 1):
                if t < T:
                    scaled("n1", t, X[:, t, :], HN[t % 2], st[:, 8 + t:9 + t])
                if t >= 1:
                    for j in range(2):
                        gained(("n1", t - 1, j), HT[:, 4 * j:4 * j + 4, tile(t - 1)], R_MIX, 4 * j)

            def rope(x1, x2, c, s, t1, t2, t3):
                v.tensor_tensor(t1, x1, c, ALU.mult)
                v.tensor_tensor(t2, x2, s, ALU.mult)
                ch(v.tensor_tensor(t3, x1, s, ALU.mult))
                ch(v.tensor_tensor(x1, t1, t2, ALU.subtract))
                ch(v.tensor_tensor(t1, x2, c, ALU.mult))
                return v.tensor_tensor(x2, t1, t3, ALU.add)

            dve.wait_ge(sem("tables"), 1)
            for t in range(T + 1):
                if t < T:
                    dve.wait_ge(sem("l_rstd"), t + 1)
                    v.tensor_scalar(HN[t % 2][:, 0:QL], uq[t % 2][:, 0:QL], st[:, 32 + 2 * t:33 + 2 * t], None, ALU.mult)
                    ch(v.tensor_scalar(HN[t % 2][:, QL:QL + KVL], uq[t % 2][:, QL:QL + KVL], st[:, 33 + 2 * t:34 + 2 * t], None, ALU.mult))
                    kr = uq[t % 2][:, 640:672]
                    c, s = cos_t[:, 16 * t:16 * t + 16], sin_t[:, 16 * t:16 * t + 16]
                    t1, t2, t3 = (x[:, 0:16] for x in rtmp)
                    ch(rope(kr[:, 0:16], kr[:, 16:32], c, s, t1, t2, t3))
                    v.tensor_copy(krt[:, t, :], kr).then_inc(sem("kr_done"), 1)
                    dve.wait_ge(sem("kr_done"), t + 1)
                    dve.sem_inc(sem("l_hn"), 1)
                if t >= 1:
                    u = t - 1
                    b = bk.wait(dve, ("lt", u, 0))
                    v.tensor_tensor(qn[:, :, tile(u)], b4(b)[:, 0:3], gain(R_QL, 0, 3), ALU.mult)
                    ins = v.tensor_tensor(kvn[:, 0:1, tile(u)], b4(b)[:, 3:4], gain(R_KVL, 0, 1), ALU.mult)
                    ch(v.engine_nop()) if False else None
                    bk.done(ins, ("lt", u, 0))
                    gained(("lt", u, 1), kvn[:, 1:2, tile(u)], R_KVL, 1, 1)
            for c in range(4):
                for r in (1, 3):
                    b = bk.wait(dve, ("pq", c, r))
                    bk.done(v.tensor_copy(pq[:, c, 2 * r:2 * r + 2, :, :].rearrange("p r m k -> p (r m k)"), PS[:, b, :]), ("pq", c, r))
            for t in range(T):
                for j in range(2):
                    b = bk.wait(dve, ("kt", t, j))
                    bk.done(v.tensor_copy(KT[:, 4 * j:4 * j + 4, tile(t)], b4(b)[0:HD1]), ("kt", t, j))
            for t in range(T):
                bk.read(dve, ("q", t, 0)), bk.read(dve, ("q", t, 1))
                if t >= 1:
                    dve.wait_ge(sem("q_rope"), t)
                q = HN[t % 2][:, 0:H1 * HD1].rearrange("p (h c) -> p h c", h=H1)
                c, s = (x[:, 16 * t:16 * t + 16].unsqueeze(1).to_broadcast([P, H1, 16]) for x in (cos_t, sin_t))
                t1, t2, t3 = (x.rearrange("p (h f) -> p h f", f=16) for x in rtmp)
                rope(q[:, :, NOPE:NOPE + 16], q[:, :, NOPE + 16:HD1], c, s, t1, t2, t3).then_inc(sem("q_rope"), 1)
            dve.wait_ge(sem("q_rope"), T)
            for kind, n in att1_steps():
                if kind == "s":
                    b = bk.wait(dve, ("s1", n))
                    v.tensor_reduce(negm[:, n:n + 1], PS[:, b:b + 2, :].rearrange("p b n -> p (b n)"), AX.X, ALU.max, negate=True).then_inc(sem("a_max"), 1)
                elif kind == "pt":
                    if n >= 2:
                        pv_wait(dve, n - 2)
                    b = bk.wait(dve, ("pt", n, 1))
                    bk.done(v.tensor_copy(ptr[n % 2][:, 4:8, :], b4(b)), ("pt", n, 1))
                elif kind == "pv" and n % H1 == H1 - 1:
                    t = n // H1
                    bk.read(dve, ("s1", n))
                    ch(v.reciprocal(rrec[:, 8 * t:8 * t + 8], rsum[:, 8 * t:8 * t + 8]))
                    b = bk.wait(dve, ("o1", t))
                    bk.done(v.tensor_tensor(o1[t % 2].rearrange("p (h c) -> p h c", h=H1), PS[:, b, :].rearrange("p (h c) -> p h c", h=H1), bcs(rrec[:, 8 * t:8 * t + 8], VD), ALU.mult), ("o1", t))
                elif kind == "y":
                    for j in range(2):
                        b = bk.wait(dve, ("y1", n, j))
                        x = X[:, n, NB * j:NB * j + NB]
                        bk.done(v.tensor_tensor(x, x, PS[:, b, :], ALU.add), ("y1", n, j))
            for m in range(2):
                scaled("nm", m, memx[:, m, :], HN[m], st[:, 50 + m:51 + m])
            for m in range(2):
                for j in range(2):
                    gained(("nm", m, j), mnT[:, 4 * j:4 * j + 4, tile(m)], R_MKV, 4 * j)
            for t in range(T):
                scaled("n2", t, X[:, t, :], HN[t % 2], st[:, 60 + t:61 + t])
                for j in range(2):
                    gained(("n2", t, j), HT[:, 4 * j:4 * j + 4, tile(t)], R_MQ, 4 * j)
            for kind, t in att2_steps():
                if kind == "s":
                    for hp in range(2):
                        b = bk.wait(dve, ("s2", t, hp))
                        i = 4 * t + 2 * hp
                        v.tensor_reduce(negm[:, i:i + 2], PS[:, b, :].rearrange("p (h k) -> p h k", h=2), AX.X, ALU.max, negate=True).then_inc(sem("m_max"), 1)
                elif kind == "pt":
                    if t >= 2:
                        bk.wait(dve, ("o2", t - 2, 1))
                    b = bk.wait(dve, ("p2", t, 1))
                    bk.done(v.tensor_copy(pt2[t % 2][:, 512:1024], PS[:, b, :]), ("p2", t, 1))
                elif kind == "pv":
                    bk.read(dve, ("s2", t, 0)), bk.read(dve, ("s2", t, 1))
                    ch(v.reciprocal(rrec[:, 4 * t:4 * t + 4], rsum[:, 4 * t:4 * t + 4]))
                    if t >= 2:
                        bk.wait(dve, ("om", t - 2, 1))
                    for hp in range(2):
                        b = bk.wait(dve, ("o2", t, hp))
                        bk.done(v.tensor_tensor(om[t % 2][:, NB * hp:NB * hp + NB].rearrange("p (h c) -> p h c", h=2), PS[:, b, :].rearrange("p (h c) -> p h c", h=2), bcs(rrec[:, 4 * t + 2 * hp:4 * t + 2 * hp + 2], MD), ALU.mult), ("o2", t, hp))
                elif kind == "y":
                    for j in range(2):
                        b = bk.wait(dve, ("ym", t, j))
                        x = X[:, t, NB * j:NB * j + NB]
                        bk.done(v.tensor_tensor(x, x, PS[:, b, :], ALU.add), ("ym", t, j))
                else:
                    scaled("n3", t, X[:, t, :], HN[t % 2], st[:, 76 + t:77 + t])
                    if t >= 2:
                        bk.wait(dve, ("lg", t - 2))
                    for j in range(2):
                        gained(("n3", t, j), rt[t % 2][:, 4 * j:4 * j + 4, :], R_FFN, 4 * j)
                    b = bk.wait(dve, ("lg", t))
                    v.tensor_reduce(st[:, 120 + t:121 + t], PS[:, b, 0:NE], AX.X, ALU.max, negate=True).then_inc(sem("r_max"), 1)
                    bk.read(dve, ("lg", t))
                    ch(v.reciprocal(st[:, 136 + t:137 + t], st[:, 128 + t:129 + t]))
                    v.tensor_scalar(aff[:, t, :], aff[:, t, :], st[:, 136 + t:137 + t], None, ALU.mult).then_inc(sem("aff"), 1)
            bk.read(dve, ("aft", 0)), bk.read(dve, ("aft", 1))
            for r in range(CAP // 8):
                top = vals[:, 8 * r:8 * r + 8]
                ch(v.max(top, affT))
                ch(v.max_index(inds[:, 8 * r:8 * r + 8], top, affT))
                ch(v.match_replace(affT, top, affT, -1.0))
            v.tensor_copy(indf, inds).then_inc(sem("top"), 1)
            b = bk.wait(dve, ("idx",))
            v.tensor_copy(gateT, PS[:, b, 0:NE])
            bk.done(v.tensor_copy(idxT, PS[:, b, NE:2 * NE]), ("idx",))

            def turned(par, banks, vals_):
                for j in range(2):
                    dve.wait_ge(full[banks[j]], vals_[j])
                    v.tensor_tensor(xt[par][:, 4 * j:4 * j + 4, :], b4(banks[j]), gain(R_FFN, 4 * j, 4 * j + 4), ALU.mult).then_inc(free[banks[j]], 1)

            turned(0, [bk.at[("tr0", j)][0] for j in range(2)], [bk.at[("tr0", j)][1] for j in range(2)])

            def expert(e, par, e1, last=False):
                if e1:
                    dve.wait_ge(full[MOE_BANK["d1"]], moe_val("d1", e) - 2)
                for i in range(2):
                    dve.wait_ge(free[MOE_BANK[f"g{i}"]], moe_val(f"g{i}", e))
                    dve.wait_ge(full[MOE_BANK[f"u{i}"]], moe_val(f"u{i}", e))
                    v.tensor_tensor(hid[par][:, NB * i:NB * i + NB], PS[:, MOE_BANK[f"u{i}"], :], sil[i], ALU.mult).then_inc(free[MOE_BANK[f"u{i}"]], 1)
                if not last:
                    turned(1 - par, [MOE_BANK["tr0"], MOE_BANK["tr1"]], [moe_val("tr0", e), moe_val("tr1", e)])

            for e in range(2):
                expert(e, e, False)
            with dve.Fori(1, NE // 2 - 1, 1) as j:
                for sub in range(2):
                    expert(2 * j + sub, sub, True)
            for e in range(NE - 2, NE):
                expert(e, e % 2, True, e == NE - 1)

            dve.wait_ge(sem("wide_in"), 32)
            dve.wait_ge(sem("affine"), 1)
            av_ = affine.rearrange("p (m k) -> p m k", m=2)
            for t in range(T):
                dve.wait_ge(sem("n4a_rstd"), t + 1)
                v.scalar_tensor_tensor(X[:, t, :], X[:, t, :], st[:, 92 + t:93 + t], gfin, ALU.mult, ALU.mult).then_inc(sem("n4a_x"), 1)
                scaled("n4b", t, X[:, t, :], HN[t % 2], st[:, 108 + t:109 + t])
                for j in range(2):
                    b = bk.wait(dve, ("n4", t, j))
                    h = HT[:, 4 * j:4 * j + 4, tile(t)]
                    m_, a_ = (bcs(av_[:, i, 4 * j:4 * j + 4], P) for i in range(2))
                    ch(v.tensor_tensor(h, b4(b), m_, ALU.mult))
                    bk.done(v.tensor_tensor(h, h, a_, ALU.add), ("n4", t, j))
            dve.wait_ge(sem("x4_out"), 16 * T)
            dve.wait_ge(sem("gate"), 1)
            v.tensor_copy(gate_b, gate_t).then_inc(sem("gate_moved"), 1)
            dve.wait_ge(sem("gate_moved"), 1)

            def conv_steps():
                for k in range(KC):
                    for j in reversed(range(TAPS)):
                        yield k, j
            conv = iter(list(conv_steps()))
            conv_n = [0]
            units = [(i, c, h) for i in range(2) for c in range(4) for h in range(2)]
            def conv_some(n, last_chunk):
                for _ in range(n):
                    if conv_n[0] // TAPS > last_chunk or conv_n[0] >= TAPS * KC:
                        return
                    k, j = next(conv)
                    if j == TAPS - 1:
                        bk.read(dve, ("glu_a", k // 4, k % 4, 1))
                        bk.read(dve, ("glu_a", k // 4, k % 4, 0))
                        ins = v.tensor_scalar(C[:, k, :], U[:, k, :], cols[:, k, R_TAP + j:R_TAP + j + 1], cols[:, k, R_CB:R_CB + 1], ALU.mult, ALU.add)
                    else:
                        d = TAPS - 1 - j
                        ins = v.scalar_tensor_tensor(C[:, k, d:S], U[:, k, 0:S - d], cols[:, k, R_TAP + j:R_TAP + j + 1], C[:, k, d:S], ALU.mult, ALU.add)
                    ins.then_inc(sem("conv"), 1)
                    conv_n[0] += 1
                    dve.wait_ge(sem("conv"), conv_n[0])

            for n, (i, c, h) in enumerate(units):
                bk.read(dve, ("glu_b", i, c, h))
                b = bk.wait(dve, ("glu_a", i, c, h))
                bk.done(v.tensor_tensor(U[:, 4 * i + c, NB * h:NB * h + NB], PS[:, b, :], sig[n % 2], ALU.mult), ("glu_a", i, c, h))
                conv_some(5, 4 * i + c - 1)

            dve.wait_ge(sem("mask_in"), 16)
            nstep = -(-(TAPS * KC - conv_n[0]) // (3 * T))
            for kind, i in win_steps():
                g, t = tiles2[i]
                if kind == "qkv":
                    bk.read(dve, ("wq", g, t)), bk.read(dve, ("wk", g, t))
                    x = qks.rearrange("p (h c) -> p h c", c=E2)
                    o = 16 * T + 8 * (T * g + t)
                    c, s = (y[:, o:o + 8].unsqueeze(1).to_broadcast([P, 2 * H2, 8]) for y in (cos_t, sin_t))
                    rope(x[:, :, 0:8], x[:, :, 8:16], c, s, *rtmp2).then_inc(sem("w_rope"), 1)
                    dve.wait_ge(sem("w_rope"), i + 1)
                    conv_some(nstep, KC)
                elif kind == "att":
                    nk = len(keys_of(g, t))
                    w = P * nk
                    mk = mask[:, 0:256] if nk == 2 else (mask[:, 256:384] if g == 2 else mask[:, 128:256])
                    if i >= 1 and tiles2[i - 1][0] != 0:
                        dve.wait_ge(sem("num_out"), num_before(i))
                    if i >= 1 and tiles2[i - 1][0] == 0:
                        bk.wait(dve, ("at", tiles2[i - 1][1]))

                    def weights_out(hp):
                        b = bk.wait(dve, ("pw", g, t, hp))
                        if hp >= 2 or i >= 1:
                            wv_wait(dve, i, hp - 2)
                        bk.done(v.tensor_copy(pwt[hp % 2][:, 0:2 * nk, :], b4(b)[:, 0:2 * nk]), ("pw", g, t, hp))

                    for hp in range(4):
                        b = bk.wait(dve, ("sw", g, t, hp))
                        if hp >= 2:
                            bk.wait(dve, ("pw", g, t, hp - 2))
                        for hh in range(2):
                            h = win_head(hp, hh)
                            ins = v.tensor_tensor_reduce(pw[hp % 2][:, w * hh:w * hh + w], PS[:, b, w * hh:w * hh + w], mk, 1.0, -3.0e38, ALU.add, ALU.max, num[:, 512 + h:513 + h])
                        bk.done(ins, ("sw", g, t, hp))
                        bk.read(dve, ("sw", g, t, hp))
                        nm = num[:, 512 + win_head(hp, 0):513 + win_head(hp, 1):2]
                        v.tensor_scalar(nm, nm, -1.0, None, ALU.mult).then_inc(sem("w_max"), 1)
                        if hp >= 1:
                            weights_out(hp - 1)
                    weights_out(3)
                    b = bk.wait(dve, ("ow", g, t))
                    bk.done(v.tensor_copy(num[:, 0:512], PS[:, b, :]), ("ow", g, t))
                    bk.read(dve, ("ow", g, t))
                    dve.wait_ge(sem("w_exp"), 4 * i + 4)
                    dve.wait_ge(sem("w_max"), 4 * i + 4)
                    dve.sem_inc(sem("num_ready"), 1)
                    if g == 0:
                        dve.wait_ge(sem("lnum_in"), 64 * (t + 1))
                        nm = [num[:, 512:520], lst[:, 0:8], lst[:, 16:24]]
                        dn = [num[:, 520:528], lst[:, 8:16], lst[:, 24:32]]
                        nall, wsum = wcomb[:, 24:32], wcomb[:, 32:40]
                        ch(v.tensor_tensor(nall, nm[0], nm[1], ALU.min))
                        ch(v.tensor_tensor(nall, nall, nm[2], ALU.min))
                        for j in range(3):
                            ins = v.tensor_tensor(wcomb[:, 8 * j:8 * j + 8], nall, nm[j], ALU.subtract)
                        ins.then_inc(sem("c_diff"), 1)
                        dve.wait_ge(sem("c_exp"), t + 1)
                        for j in range(3):
                            ins = v.tensor_tensor(wcomb[:, 40 + 8 * j:48 + 8 * j], wcomb[:, 8 * j:8 * j + 8], dn[j], ALU.mult)
                        ch(ins)
                        ch(v.tensor_tensor(wsum, wcomb[:, 40:48], wcomb[:, 48:56], ALU.add))
                        ch(v.tensor_tensor(wsum, wsum, wcomb[:, 56:64], ALU.add))
                        ch(v.reciprocal(wsum, wsum))
                        for j in range(3):
                            ins = v.tensor_tensor(wcomb[:, 8 * j:8 * j + 8], wcomb[:, 8 * j:8 * j + 8], wsum, ALU.mult)
                        ch(ins)
                        full_ = [num[:, 0:512], lnum[0], lnum[1]]
                        for j in range(3):
                            f3 = full_[j].rearrange("p (h c) -> p h c", h=H2)
                            ins = v.tensor_tensor(f3, f3, bcs(wcomb[:, 8 * j:8 * j + 8], E2), ALU.mult)
                        ch(ins)
                        ch(v.tensor_tensor(full_[0], full_[0], full_[1], ALU.add))
                        v.tensor_tensor(full_[0], full_[0], full_[2], ALU.add).then_inc(sem("comb_done"), 1)
            conv_some(TAPS * KC, KC)
            tmp = [HN[i][:, 0:512] for i in range(2)]
            m = 0
            for c in range(4):
                for h in range(2):
                    bk.read(dve, ("za", c, h))
                    a = attT[:, c, NB * h:NB * h + NB]
                    bk.read(dve, ("at", 4 * h + 3))
                    v.tensor_tensor(a, a, tmp[m % 2], ALU.mult).then_inc(sem("tmp_used"), 1)
                    m += 1
            for c in range(8):
                for h in range(2):
                    bk.read(dve, ("gt", c, h))
                    b = bk.wait(dve, ("ya", c, h))
                    ch(v.tensor_tensor(M[:, c, NB * h:NB * h + NB], PS[:, b, :], tmp[m % 2], ALU.mult))
                    v.sem_inc(sem("tmp_used"), 1)
                    v.sem_inc(free[b], 1)
                    m += 1
            for t in range(T + 1):
                if t < T:
                    bs = st[:, 68:80].rearrange("p (j s) -> p j s", j=2)
                    mv = st[:, 16 + 2 * t:18 + 2 * t]
                    bb = [bk.wait(dve, ("c1", t, j)) for j in range(2)]
                    for j in range(2):
                        ins = v.bn_stats(bs[:, j, :], PS[:, bb[j], :])
                    ch(ins)
                    ch(v.bn_aggr(mv, st[:, 68:80]))
                    v.sem_inc(sem("ln_var"), 1)
                    dve.wait_ge(sem("ln_rstd"), t + 1)
                    bk.wait(dve, ("c2", t - 2, 1)) if t >= 2 else None
                    for j in range(2):
                        bk.done(v.tensor_scalar(HN[t % 2][:, NB * j:NB * j + NB], PS[:, bb[j], :], mv[:, 0:1], st[:, 32 + t:33 + t], ALU.subtract, ALU.mult), ("c1", t, j))
                if t >= 1:
                    for j in range(2):
                        b = bk.wait(dve, ("c2", t - 1, j))
                        c_ = C[:, 4 * j:4 * j + 4, tile(t - 1)]
                        bk.done(v.tensor_tensor(c_, b4(b), gain(R_LNG, 4 * j, 4 * j + 4), ALU.mult), ("c2", t - 1, j))
                        bk.read(dve, ("c2", t - 1, j))
                        v.tensor_tensor(c_, c_, gain(R_LNB, 4 * j, 4 * j + 4), ALU.add).then_inc(sem("ln_aff"), 1)
            dve.wait_ge(sem("ln_silu"), 2 * T)
            for c in range(8):
                for h in range(2):
                    bk.read(dve, ("zc", c, h))
                    a = C[:, c, NB * h:NB * h + NB]
                    v.tensor_tensor(a, a, tmp[m % 2], ALU.mult).then_inc(sem("tmp_used"), 1)
                    m += 1
            for c in range(8):
                for h in range(2):
                    bk.read(dve, ("gc", c, h))
                    b = bk.wait(dve, ("yc", c, h))
                    a = M[:, c, NB * h:NB * h + NB]
                    bk.done(v.tensor_tensor(tmp[m % 2], PS[:, b, :], tmp[m % 2], ALU.mult), ("yc", c, h))
                    bk.read(dve, ("yc", c, h))
                    v.tensor_tensor(a, a, tmp[m % 2], ALU.add).then_inc(sem("tmp_used"), 1)
                    m += 1
            dve.wait_ge(sem("tmp_used"), m)
            for t in range(T + 1):
                if t < T:
                    dve.wait_ge(sem(f"xr_in{t % 2}"), 16 * (t // 2 + 1))
                    if t >= 2:
                        dve.wait_ge(sem(f"out_done{t % 2}"), 16 * (t // 2))
                    for j in range(2):
                        b = bk.wait(dve, ("y2", t, j))
                        o = HN[t % 2][:, NB * j:NB * j + NB]
                        bk.done(v.tensor_tensor(o, PS[:, b, :], gate_b[:, NB * j:NB * j + NB], ALU.mult), ("y2", t, j))
                        bk.read(dve, ("y2", t, j))
                        v.tensor_tensor(o, o, xr[t % 2][:, NB * j:NB * j + NB], ALU.add).then_inc(sem("y2_sum"), 1)
                    dve.wait_ge(sem("y2_sum"), 2 * t + 2)
                    dve.sem_inc(sem("xr_used"), 1)
                if t >= 1:
                    u = t - 1
                    dve.wait_ge(sem("n5_rstd"), u + 1)
                    if u == 0:
                        dve.wait_ge(sem("fg_in"), 16)
                    v.scalar_tensor_tensor(HN[u % 2], HN[u % 2], st[:, 60 + u:61 + u], fg, ALU.mult, ALU.mult).then_inc(sem("out_ready"), 1)

        @block.tensor
        def _(pe):
            mm = nc.tensor.matmul

            def turn(dst, src, n=P):
                return nc.tensor.transpose(dst, src, ident[0:n, 0:n])

            def turns(name, src, n=4):
                b = bk.begin(pe, name)
                for k in range(n):
                    ins = turn(PS[:, b, P * k:P * k + P], src[:, P * k:P * k + P])
                bk.end(ins, name)

            def product(name, lhs, rhs, n, out_=None):
                b = bk.begin(pe, name)
                o = out_(b) if out_ else PS[:, b, :]
                for k in range(n):
                    ins = mm(o, lhs(k), rhs(k), start=(k == 0), stop=(k == n - 1))
                bk.end(ins, name)

            pe.wait_ge(sem("ident_in"), 16)
            pe.wait_ge(sem("rows_in"), 16 * 13)
            b = bk.begin(pe, "cols")
            for k in range(KC):
                ins = turn(PS[:, b, NROW * k:NROW * k + NROW], rows[0:NROW, tile(k)], NROW)
            bk.end(ins, "cols")
            pe.wait_ge(sem("wbd_in"), 32)
            pe.wait_ge(sem("chan_in"), 16)
            for m in range(2):
                product(("bd", m), lambda k: chan[:, m, :], lambda k: wbd.rearrange("p c j -> p (c j)"), 1)
            for t in range(T):
                pe.wait_ge(sem("n1_hn"), t + 1)
                for j in range(2):
                    turns(("n1", t, j), HN[t % 2][:, NB * j:NB * j + NB])
            w_wait(pe, "in0")
            for t in range(T):
                bk.read(pe, ("n1", t, 0)), bk.read(pe, ("n1", t, 1))
                product(("uf", t), lambda k: HT[:, k, tile(t)], lambda k: wview("in0")[:, k, :], KC)
            w_wait(pe, "in1"), w_wait(pe, "in2")

            def latent_turn(t):
                pe.wait_ge(sem("l_hn"), t + 1)
                turns(("lt", t, 0), HN[t % 2][:, 0:512])
                turns(("lt", t, 1), HN[t % 2][:, 512:640], 1)

            for t in range(T):
                product(("ua", t), lambda k: HT[:, k, tile(t)], lambda k: wview("in1")[:, k, :], KC)
                product(("ub", t), lambda k: HT[:, k, tile(t)], lambda k: wview("in2")[:, k, :], KC, lambda b: PS[:, b, 0:160])
                if t >= 1:
                    latent_turn(t - 1)
            latent_turn(T - 1)
            w_wait(pe, "twiddle")
            pe.wait_ge(sem("dft_done"), 1)
            tw = ring[wslot(seq["twiddle"])].rearrange("p (m r n) -> p m r n", m=2, r=RADIX)
            parts = {0: (0, None), 4: (1, None), 2: (2, 3), 6: (2, 3), 1: (4, 5), 7: (4, 5), 3: (6, 7), 5: (6, 7)}
            for c in range(4):
                for rp in range(4):
                    b = bk.begin(pe, ("pq", c, rp))
                    for j in range(2):
                        r = 2 * rp + j
                        re, im = parts[r]
                        o = PS[:, b, 256 * j:256 * j + 256]
                        ins = mm(o, gdft[:, re, tile(c)], tw[:, 0, r, :], start=True, stop=im is None)
                        if im is not None:
                            ins = mm(o, gdft[:, im, tile(c)], tw[:, 1, r, :], start=False, stop=True)
                    bk.end(ins, ("pq", c, rp))
                bk.read(pe, ("bd", 0)), bk.read(pe, ("bd", 1))
                for h in range(2):
                    bk.read(pe, ("pq", c, 2 * h)), bk.read(pe, ("pq", c, 2 * h + 1))
                    product(("yf", c, h), lambda k: bd[:, k, c, :], lambda k: pq[:, c, 4 * h:4 * h + 4, k, :], 2, b4)
            w_wait(pe, "kvup")

            def head_turns(nm, t):
                for j in range(2):
                    b = bk.begin(pe, (nm, t, j))
                    for h in range(4):
                        ins = turn(PS[0:HD1, b, tile(h)], HN[t % 2][:, HD1 * (4 * j + h):HD1 * (4 * j + h) + HD1])
                    bk.end(ins, (nm, t, j))

            def key_turn(t):
                pe.wait_ge(sem("k_rope"), t + 1)
                bk.read(pe, ("kv", t, 0)), bk.read(pe, ("kv", t, 1))
                head_turns("kt", t)

            for t in range(T):
                for j in range(2):
                    bk.read(pe, ("lt", t, 0)), bk.read(pe, ("lt", t, 1))
                    product(("kv", t, j), lambda k: kvn[:, k, tile(t)], lambda k: wview("kvup")[:, k, NB * j:NB * j + NB], 2)
                if t >= 1:
                    key_turn(t - 1)
            key_turn(T - 1)
            w_wait(pe, "qup")

            def query_turn(t):
                pe.wait_ge(sem("q_rope"), t + 1)
                head_turns("qt", t)

            for t in range(T):
                product(("q", t, 0), lambda k: qn[:, k, tile(t)], lambda k: wview("qup")[:, k, 0:512], 3)
                product(("q", t, 1), lambda k: qn[:, k, tile(t)], lambda k: wview("qup")[:, k, 512:768], 3, lambda b: PS[:, b, 0:256])
                if t >= 1:
                    query_turn(t - 1)
            query_turn(T - 1)
            w_wait(pe, "out0"), w_wait(pe, "out1")
            for kind, n in att1_steps():
                t, h = divmod(n, H1)
                if kind == "s":
                    if n == 0:
                        for u in range(T):
                            for j in range(2):
                                bk.read(pe, ("kt", u, j)), bk.read(pe, ("qt", u, j))
                    b = bk.begin(pe, ("s1", n))
                    for j in range(2):
                        ins = mm(PS[:, b + j, :], QT[:, h, tile(t)], KT[:, h, NB * j:NB * j + NB], start=True, stop=True)
                    bk.end(ins, ("s1", n))
                elif kind == "pt":
                    bk.read(pe, ("s1", n))
                    for j in range(2):
                        turns(("pt", n, j), pexp[n % 2][:, NB * j:NB * j + NB])
                elif kind == "pv":
                    if h == 0:
                        bk.begin(pe, ("o1", t))
                    bk.read(pe, ("pt", n, 0)), bk.read(pe, ("pt", n, 1))
                    for k in range(8):
                        ins = mm(PS[:, 6, VD * h:VD * h + VD], ptr[n % 2][:, k, :], V1[:, k, VD * h:VD * h + VD], start=(k == 0), stop=(k == 7))
                    if h == H1 - 1:
                        bk.end(ins, ("o1", t))
                    else:
                        ins.then_inc(sem("pv_done"), 1)
                elif kind == "y":
                    bk.read(pe, ("o1", n))
                    turns(("ot", n), o1[n % 2])
                    bk.read(pe, ("ot", n))
                    if n == 0:
                        bk.read(pe, ("yf", 3, 1))
                    for j in range(2):
                        product(("y1", n, j), lambda k: mixf[:, k, tile(n)] if k < 4 else mixa[n % 2][:, k - 4, :], lambda k: wview(f"out{j}")[:, k, :], KC)
            for m in range(2):
                pe.wait_ge(sem("nm_hn"), m + 1)
                for j in range(2):
                    turns(("nm", m, j), HN[m][:, NB * j:NB * j + NB])
            for c in range(8):
                if c == 0:
                    for m in range(2):
                        bk.read(pe, ("nm", m, 0)), bk.read(pe, ("nm", m, 1))
                if c % 4 == 0:
                    w_wait(pe, f"mkv{c // 4}")
                product(("mk", c), lambda k: wview(f"mkv{c // 4}")[:, k, tile(c % 4)], lambda k: mnT[:, k, :], KC, lambda b: PS[:, b, 0:MEM])
                pe.wait_ge(sem("n2_hn"), c + 1)
                for j in range(2):
                    turns(("n2", c, j), HN[c % 2][:, NB * j:NB * j + NB])
            for n in range(2):
                w_wait(pe, f"mkv{2 + n}")
                for m in range(2):
                    product(("mv", m, n), lambda k: mnT[:, k, tile(m)], lambda k: wview(f"mkv{2 + n}")[:, k, :], KC)
            for t in range(T):
                bk.read(pe, ("n2", t, 0)), bk.read(pe, ("n2", t, 1))
            for c in range(8):
                if c % 4 == 0:
                    w_wait(pe, f"mq{c // 4}")
                for h in range(2):
                    product(("mq", c, h), lambda k: wview(f"mq{c // 4}")[:, k, tile(c % 4)], lambda k: HT[:, k, NB * h:NB * h + NB], KC)
            for c in range(8):
                bk.read(pe, ("mk", c)), bk.read(pe, ("mq", c, 0)), bk.read(pe, ("mq", c, 1))
            w_wait(pe, "mo0"), w_wait(pe, "mo1")
            pe.wait_ge(sem("router_in"), 16)
            for kind, t in att2_steps():
                if kind == "s":
                    for hp in range(2):
                        b = bk.begin(pe, ("s2", t, hp))
                        for hh in range(2):
                            h = 2 * hp + hh
                            for k in range(2):
                                ins = mm(PS[:, b, 256 * hh:256 * hh + 256], QM[:, 2 * h + k, tile(t)], KM[:, 2 * h + k, :], start=(k == 0), stop=(k == 1))
                        bk.end(ins, ("s2", t, hp))
                elif kind == "pt":
                    for hp in range(2):
                        bk.read(pe, ("s2", t, hp))
                        turns(("p2", t, hp), p2[t % 2][:, 512 * hp:512 * hp + 512])
                elif kind == "pv":
                    if t == 0:
                        for n in range(2):
                            bk.read(pe, ("mv", 0, n)), bk.read(pe, ("mv", 1, n))
                    for hp in range(2):
                        bk.read(pe, ("p2", t, hp))
                        b = bk.begin(pe, ("o2", t, hp))
                        for hh in range(2):
                            h = 2 * hp + hh
                            for k in range(2):
                                ins = mm(PS[:, b, 256 * hh:256 * hh + 256], pt2[t % 2][:, P * (2 * h + k):P * (2 * h + k) + P], VM[:, k, MD * h:MD * h + MD], start=(k == 0), stop=(k == 1))
                        bk.end(ins, ("o2", t, hp))
                elif kind == "y":
                    for j in range(2):
                        bk.read(pe, ("o2", t, j))
                        turns(("om", t, j), om[t % 2][:, NB * j:NB * j + NB])
                    bk.read(pe, ("om", t, 0)), bk.read(pe, ("om", t, 1))
                    for j in range(2):
                        product(("ym", t, j), lambda k: omt[t % 2][:, k, :], lambda k: wview(f"mo{j}")[:, k, :], KC)
                else:
                    pe.wait_ge(sem("n3_hn"), t + 1)
                    for j in range(2):
                        turns(("n3", t, j), HN[t % 2][:, NB * j:NB * j + NB])
                    bk.read(pe, ("n3", t, 0)), bk.read(pe, ("n3", t, 1))
                    product(("lg", t), lambda k: rt[t % 2][:, k, :], lambda k: router[:, k, :], KC, lambda b: PS[:, b, 0:NE])
            pe.wait_ge(sem("aff"), T)
            for c in range(2):
                b = bk.begin(pe, ("aft", c))
                for j in range(4):
                    ins = turn(PS[0:NE, b, tile(j)], aff[:, 4 * c + j, :])
                bk.end(ins, ("aft", c))
            for i in range(6):
                w_wait(pe, f"ada{i}")
                if i < 4:
                    b = bk.begin(pe, ("ada", i))
                    for c in range(4):
                        for k in range(KC):
                            ins = mm(PS[:, b, c:c + 1], wview(f"ada{i}")[:, k, tile(c)], cols[:, k, R_C:R_C + 1], start=(k == 0), stop=(k == KC - 1))
                    bk.end(ins, ("ada", i))
                else:
                    pe.wait_ge(sem("c_wide"), 1)
                    product(("ada", i), lambda k: cb[:, k, :], lambda k: wview(f"ada{i}")[:, k, :], KC)
            pe.wait_ge(sem("top"), 1)
            b = bk.begin(pe, ("idx",))
            turn(PS[:, b, 0:NE], vals, NE)
            ins = turn(PS[:, b, NE:2 * NE], indf, NE)
            bk.end(ins, ("idx",))
            pe.wait_ge(sem("xg_in0"), 16)
            for j in range(2):
                turns(("tr0", j), xg[0][:, NB * j:NB * j + NB])
            for w in moe_first:
                for b_, v_ in w:
                    pe.wait_ge(free[b_], v_)

            def expert(e, par, last=False, half_e=None):
                def use(k, n_block):
                    pe.wait_ge(free[MOE_BANK[k]], moe_val(k, e) - 1)
                    if n_block is not None:
                        slot = (n_moe0 + n_block) % RING
                        pe.wait_ge(w_full[slot], 32 * e + 16 * ((n_moe0 + n_block) // RING + 1))
                        return ring[slot].rearrange("p (k n) -> p k n", k=KC)

                for i in range(2):
                    for gu, nb in (("g", 2 * i), ("u", 2 * i + 1)):
                        w = use(f"{gu}{i}", nb)
                        o = PS[:, MOE_BANK[f"{gu}{i}"], :]
                        for f in range(4):
                            for k in range(KC):
                                ins = mm(o[:, tile(f)], w[:, k, tile(f)], xt[par][:, k, :], start=(k == 0), stop=(k == KC - 1))
                        ins.then_inc(full[MOE_BANK[f"{gu}{i}"]], 1)
                if not last:
                    pe.wait_ge(sem(f"xg_in{1 - par}"), 16 * half_e)
                    for j in range(2):
                        use(f"tr{j}", None)
                        for k in range(4):
                            ins = turn(PS[:, MOE_BANK[f"tr{j}"], tile(k)], xg[1 - par][:, NB * j + P * k:NB * j + P * k + P])
                        ins.then_inc(full[MOE_BANK[f"tr{j}"]], 1)
                for i in range(2):
                    w = use(f"d{i}", 4 + i)
                    for j in range(2):
                        pe.wait_ge(free[MOE_BANK[f"u{j}"]], moe_val(f"u{j}", e))
                    for k in range(KC):
                        ins = mm(PS[:, MOE_BANK[f"d{i}"], :], hid[par][:, tile(k)], w[:, k, :], start=(k == 0), stop=(k == KC - 1))
                    ins.then_inc(full[MOE_BANK[f"d{i}"]], 1)
                if not last:
                    for j in range(2):
                        pe.wait_ge(free[MOE_BANK[f"tr{j}"]], moe_val(f"tr{j}", e))

            for j in range(2):
                bk.read(pe, ("tr0", j))
            with pe.Fori(0, NE // 2 - 1, 1) as j:
                expert(2 * j, 0, half_e=j + 1)
                expert(2 * j + 1, 1, half_e=j + 2)
            expert(NE - 2, 0, half_e=NE // 2)
            expert(NE - 1, 1, last=True)
            for t in range(T):
                pe.wait_ge(sem("n4b_hn"), t + 1)
                for j in range(2):
                    turns(("n4", t, j), HN[t % 2][:, NB * j:NB * j + NB])
            for t in range(T):
                bk.read(pe, ("n4", t, 0)), bk.read(pe, ("n4", t, 1))

            def feature_major(name, w, c, h, src, n=KC):
                product(name, lambda k: wview(w)[:, k, tile(c)], lambda k: src[:, k, NB * h:NB * h + NB], n)

            for i in range(2):
                w_wait(pe, f"ga{i}"), w_wait(pe, f"gb{i}")
                for c in range(4):
                    for h in range(2):
                        feature_major(("glu_a", i, c, h), f"ga{i}", c, h, HT)
                        feature_major(("glu_b", i, c, h), f"gb{i}", c, h, HT)

            def group_tokens(g, t, k):
                if g == 0:
                    return HT[:, k, tile(t)]
                if g == 1:
                    r, b_ = divmod(t, 2)
                    return HT[:, k, :].rearrange("p (b j r) -> p b r j", b=2, r=4)[:, b_, r, :]
                return HT[:, k, :].rearrange("p (j m) -> p m j", m=8)[:, t, :]

            for kind, i in win_steps():
                g, t = tiles2[i]
                if kind == "qkv":
                    for nm in "qkv":
                        if t == 0:
                            w_wait(pe, f"{nm}{g}")
                        product(("w" + nm, g, t), lambda k: group_tokens(g, t, k), lambda k: wview(f"{nm}{g}")[:, k, :], KC)
                    pe.wait_ge(sem("w_rope"), i + 1)
                    turns(("qkt", g, t, 0), qks[:, 0:512])
                    turns(("qkt", g, t, 1), qks[:, 512:1024])
                elif kind == "att":
                    ks = keys_of(g, t)
                    nk = len(ks)
                    bk.read(pe, ("qkt", g, t, 0)), bk.read(pe, ("qkt", g, t, 1)), bk.read(pe, ("wv", g, t))
                    for hp in range(4):
                        b = bk.begin(pe, ("sw", g, t, hp))
                        lo = slice(64 * (hp % 2), 64 * (hp % 2) + 64)
                        for hh in range(2):
                            pair = win_head(hp, hh) // 2
                            for j in range(nk):
                                kt_ = kT2[(i - (nk - 1 - j)) % 3]
                                ins = mm(PS[:, b, P * (nk * hh + j):P * (nk * hh + j) + P], qT2[i % 2][lo, pair, :], kt_[lo, pair, :], start=True, stop=True)
                        bk.end(ins, ("sw", g, t, hp))

                    def values(hp):
                        bk.read(pe, ("pw", g, t, hp))
                        if hp == 0:
                            bk.begin(pe, ("ow", g, t))
                        b = bk.at[("ow", g, t)][0]
                        for hh in range(2):
                            h = win_head(hp, hh)
                            for j in range(nk):
                                ins = mm(PS[:, b, E2 * h:E2 * h + E2], pwt[hp % 2][:, nk * hh + j, :], V2[(i - (nk - 1 - j)) % 3][:, E2 * h:E2 * h + E2], start=(j == 0), stop=(j == nk - 1))
                        if hp == 3:
                            bk.end(ins, ("ow", g, t))
                        else:
                            ins.then_inc(sem("wv_done"), 1)

                    for hp in range(4):
                        pe.wait_ge(sem("w_exp"), 4 * i + hp + 1)
                        turns(("pw", g, t, hp), pw[hp % 2], 2 * nk)
                        if hp >= 1:
                            values(hp - 1)
                    values(3)
                else:
                    pe.wait_ge(sem("comb_done"), t + 1)
                    turns(("at", t), num[:, 0:512])
            w_wait(pe, "za")
            for c in range(4):
                for h in range(2):
                    feature_major(("za", c, h), "za", c, h, HT)
            pe.wait_ge(sem("tmp_used"), 8)
            for c in range(8):
                if c % 4 == 0:
                    w_wait(pe, f"gt{c // 4}")
                if c == 0:
                    w_wait(pe, "ao")
                for h in range(2):
                    feature_major(("gt", c, h), f"gt{c // 4}", c % 4, h, HT)
                    feature_major(("ya", c, h), "ao", c, h, attT, 4)
            pe.wait_ge(sem("conv"), TAPS * KC)
            for t in range(T + 1):
                if t < T:
                    for j in range(2):
                        b = bk.begin(pe, ("c1", t, j))
                        for k in range(4):
                            ins = turn(PS[:, b, tile(k)], C[:, 4 * j + k, tile(t)])
                        bk.end(ins, ("c1", t, j))
                if t >= 1:
                    for j in range(2):
                        bk.read(pe, ("c1", t - 1, j))
                    for j in range(2):
                        turns(("c2", t - 1, j), HN[(t - 1) % 2][:, NB * j:NB * j + NB])
            for c in range(8):
                if c % 4 == 0:
                    w_wait(pe, f"zc{c // 4}")
                for h in range(2):
                    feature_major(("zc", c, h), f"zc{c // 4}", c % 4, h, HT)
            pe.wait_ge(sem("tmp_used"), 8 + 16 + 16)
            for c in range(8):
                if c % 4 == 0:
                    w_wait(pe, f"gc{c // 4}"), w_wait(pe, f"co{c // 4}")
                for h in range(2):
                    feature_major(("gc", c, h), f"gc{c // 4}", c % 4, h, HT)
                    feature_major(("yc", c, h), f"co{c // 4}", c % 4, h, C)
            pe.wait_ge(sem("tmp_used"), 8 + 16 + 16 + 16)
            w_wait(pe, "wo0"), w_wait(pe, "wo1")
            for t in range(T):
                for j in range(2):
                    product(("y2", t, j), lambda k: M[:, k, tile(t)], lambda k: wview(f"wo{j}")[:, k, :], KC)


_INS = ["x", "mem", "positions", "g_mix", "w_in", "g_q_lat", "w_q_up", "g_kv_lat", "w_kv_up", "w_fourier", "w_out",
        "g_mem_q", "g_mem_kv", "w_mem_q", "w_mem_kv", "w_mem_o", "g_ffn", "w_router", "w_exp_gate", "w_exp_up",
        "w_exp_down", "g_final", "c_2", "positions_2", "norm_g_2", "w_ada_2", "b_ada_2", "w_in_2", "conv_w_2",
        "conv_b_2", "conv_ln_g_2", "conv_ln_b_2", "w_conv_out_2", "w_att_out_2", "w_o_2", "final_g_2"]


def kernel(**inputs):
    import concourse.bacc as bacc
    from concourse.bass_utils import run_bass_kernel_spmd

    nc = bacc.Bacc("TRN2", target_bir_lowering=False, num_devices=1)
    arrays = {f"in_{n}": np.ascontiguousarray(inputs[n]) for n in _INS}
    arrays.update({f"in_{n}": v for n, v in constants().items()})
    A = {n[3:]: nc.dram_tensor(n, a.shape, mybir.dt.from_np(a.dtype), kind="ExternalInput").ap() for n, a in arrays.items()}
    out = nc.dram_tensor("out_0", (1, S, D), F32, kind="ExternalOutput").ap()
    build(nc, A, out)
    r = run_bass_kernel_spmd(nc, [arrays], core_ids=[0])
    return r.results[0]["out_0"]
```

```python
from contextlib import ExitStack

import concourse.bass as bass
import numpy as np
from concourse import mybir

F32 = mybir.dt.float32
F32R = mybir.dt.float32r
I32 = mybir.dt.int32
U32 = mybir.dt.uint32
ALU = mybir.AluOpType
ACT = mybir.ActivationFunctionType
AX = mybir.AxisListType

P = 128
S = 1024
D = 1024
T = S // P
KC = D // P
NB = 512
MEM = 256
FW, QL, KVL, ROPE = 512, 384, 256, 32
H1, NOPE, VD = 8, 64, 64
HD1 = NOPE + ROPE
MH, MD = 4, 256
NE, CAP = 16, 128
G2N, H2, E2 = 3, 8, 64
ROT2 = E2 // 4
TAPS = 31
EPS = 1e-6
NEG = -1e30
RING = 3
RADIX = 8

(R_MIX, R_MQ, R_MKV, R_FFN, R_N2, R_SHIFT, R_SCALE, R_GATE, R_CB, R_LNG, R_LNB, R_C, R_QL, R_KVL,
 R_TAP) = range(15)
NROW = R_TAP + TAPS


def constants():
    two_pi = 2 * np.pi
    p, k = np.arange(P)[:, None], np.arange(P)[None, :]
    tw = np.zeros((P, 2, RADIX, 2, P), np.float64)
    for r in range(RADIX):
        ang = two_pi * ((p * (RADIX * k + r)) % S) / S
        tw[:, 0, r, 0], tw[:, 0, r, 1] = np.cos(ang), np.sin(ang)
        flip = -1.0 if r > RADIX // 2 else 1.0
        tw[:, 1, r, 0], tw[:, 1, r, 1] = flip * np.sin(ang), -flip * np.cos(ang)
    c = np.arange(64)
    ang = two_pi * ((c[:, None] * c[None, :]) % 64) / 64
    chan = np.zeros((P, 2, P))
    norm = 1.0 / np.sqrt(S * 64)
    for b in range(2):
        chan[64 * b:64 * b + 64, 0, 64 * b:64 * b + 64] = np.cos(ang) * norm
        chan[64 * b:64 * b + 64, 1, 64 * b:64 * b + 64] = -np.sin(ang) * norm
    f1 = (1.0 / (np.float32(10000.0) ** (np.arange(0, ROPE, 2, dtype=np.float32) / np.float32(ROPE)))).astype(np.float32)
    f2 = (np.float32(500000.0) ** (-(np.arange(ROT2 // 2, dtype=np.float32) * np.float32(2.0) / np.float32(ROT2)))).astype(np.float32)
    freq = np.concatenate([f1, f2])[None, :].repeat(P, 0)
    q, kk = np.arange(P)[:, None], np.arange(P)[None, :]
    prev = np.where(kk >= q, 0.0, NEG)
    cur = np.where(kk <= q, 0.0, NEG)
    pair = np.where((q % 2 == kk % 2) & (kk <= q), 0.0, NEG)
    return {
        "k_ident": np.eye(P, dtype=np.float32),
        "k_twiddle": tw.reshape(P, -1).astype(np.float32),
        "k_chan": chan.reshape(P, -1).astype(np.float32),
        "k_freq": freq.astype(np.float32),
        "k_mask": np.concatenate([prev, cur, pair], 1).astype(np.float32),
    }


class Bank:

    def __init__(self, full, free):
        self.full, self.free = full, free
        self.count = [0] * 8
        self.last = [[] for _ in range(8)]
        self.next = 0
        self.at = {}
        self.order = []

    def add(self, name, pair=False, bank=None):
        if bank is None:
            if pair and self.next % 2:
                self.next = (self.next + 1) % 8
            bank = self.next
            self.next = (self.next + (2 if pair else 1)) % 8
        waits = self.last[bank] + (self.last[bank + 1] if pair else [])
        self.count[bank] += 1
        assert name not in self.at, name
        self.at[name] = (bank, self.count[bank], waits)
        self.last[bank] = [(bank, self.count[bank])]
        if pair:
            self.last[bank + 1] = [(bank, self.count[bank])]
        self.order.append(name)

    def begin(self, pe, name):
        for b, v in self.at[name][2]:
            pe.wait_ge(self.free[b], v)
        return self.at[name][0]

    def end(self, ins, name):
        ins.then_inc(self.full[self.at[name][0]], 1)

    def wait(self, eng, name):
        b, v, _ = self.at[name]
        eng.wait_ge(self.full[b], v)
        return b

    def done(self, ins, name):
        ins.then_inc(self.free[self.at[name][0]], 1)

    def read(self, eng, name):
        b, v, _ = self.at[name]
        eng.wait_ge(self.free[b], v)


def build(nc, A, out):
    sems = {}
    ctx = ExitStack()
    with ctx:
        def sem(name):
            if name not in sems:
                sems[name] = ctx.enter_context(nc.semaphore(name))
            return sems[name]

        full = [sem(f"psum_full{i}") for i in range(8)]
        free = [sem(f"psum_free{i}") for i in range(8)]
        w_full = [sem(f"weights_in{i}") for i in range(RING)]
        bk = Bank(full, free)

        X0, HT0, GA0, GB0, GC0, W0, S0, END = 0, 8192, 16384, 24576, 32768, 36864, 49152, 53200
        starts = [X0, HT0, GA0, GB0, GC0] + [W0 + 4096 * i for i in range(RING)] + [S0, END]
        names = ["x", "ht", "a", "b", "c", "w0", "w1", "w2", "small"]
        with ExitStack() as first:
            regions = [first.enter_context(nc.sbuf_tensor(f"{n}_f32", [P, starts[i + 1] - starts[i]], F32)) for i, n in enumerate(names)]
        rounded = [ctx.enter_context(nc.sbuf_tensor(f"{n}_f32r", [P, starts[i + 1] - starts[i]], F32R)) for i, n in enumerate(names[:-1])]
        ctx.enter_context(nc.sbuf_tensor("small_place", [P, END - S0], F32))
        PS = ctx.enter_context(nc.psum_tensor("ps", [P, 8, NB], F32))

        def place(tensors, at, n):
            i = max(i for i in range(len(names)) if starts[i] <= at)
            assert at + n <= starts[i + 1]
            return tensors[i][:, at - starts[i]:at - starts[i] + n]

        def mem(at, n):
            return place(regions, at, n)

        def mem_r(at, n):
            return place(rounded, at, n)

        def value(part):
            return part.bitcast(F32)

        X = mem(X0, 8192).rearrange("p (t d) -> p t d", t=T)
        HT = mem(HT0, 8192).rearrange("p (k s) -> p k s", k=KC)
        ring = [mem(W0 + 4096 * i, 4096) for i in range(RING)]
        at = [S0]

        def small(n):
            at[0] += n
            assert at[0] <= END
            return mem(at[0] - n, n)

        ident = small(P)
        cols = small(KC * NROW).rearrange("p (k r) -> p k r", r=NROW)
        NF = 16 * T + 8 * 3 * T
        sin_t, cos_t = small(NF), small(NF)
        router = small(KC * NE).rearrange("p (k e) -> p k e", e=NE)
        HN = [small(D) for _ in range(2)]
        mask = small(3 * P)
        st = small(160)
        half = small(8)
        affine = small(2 * KC)

        def tab1(t_, which):
            return (sin_t if which else cos_t)[:, 16 * t:16 * t + 16]

        dram = {n: nc.dram_tensor(n, s, F32, kind="Internal").ap()
                for n, s in (("h0", (S, D)), ("acc", (S, D)), ("x4", (S, D)),
                             ("num1", (S, 528)), ("num2", (S, 528)), ("gate", (1, D)))}

        def kcol(w, c0, n):
            return w[:, c0:c0 + n].rearrange("(k p) n -> p k n", p=P)

        w_in, w_in2 = A["w_in"][0], A["w_in_2"][0]
        weights = []

        def wadd(name, src, k, n, last):
            weights.append((name, src, k, n, last))

        wadd("in0", kcol(w_in, 0, NB), 8, NB, ("uf", T - 1))
        wadd("in1", kcol(w_in, NB, NB), 8, NB, ("ub", T - 1))
        wadd("in2", kcol(w_in, 2 * NB, 160), 8, 160, ("ub", T - 1))
        wadd("twiddle", A["k_twiddle"].rearrange("p (k n) -> p k n", k=2), 2, 2048, ("pq", 3, 3))
        wadd("kvup", A["w_kv_up"][0].rearrange("(k p) n -> p k n", p=P), 2, 1024, ("kv", T - 1, 1))
        wadd("qup", A["w_q_up"][0].rearrange("(k p) n -> p k n", p=P), 3, 768, ("q", T - 1, 1))
        for i in range(2):
            wadd(f"out{i}", kcol(A["w_out"][0], NB * i, NB), 8, NB, ("y1", T - 1, i))
        for i in range(4):
            wadd(f"mkv{i}", kcol(A["w_mem_kv"][0], NB * i, NB), 8, NB,
                 ("mk", 4 * i + 3) if i < 2 else ("mv", 1, i - 2))
        for i in range(2):
            wadd(f"mq{i}", kcol(A["w_mem_q"][0], NB * i, NB), 8, NB, ("mq", 4 * i + 3, 1))
        for i in range(2):
            wadd(f"mo{i}", kcol(A["w_mem_o"][0], NB * i, NB), 8, NB, ("ym", T - 1, i))
        for i in range(6):
            wadd(f"ada{i}", kcol(A["w_ada_2"][0], NB * i, NB), 8, NB, ("ada", i))
        n_moe0 = len(weights)
        MOE_W = 6
        n_post = n_moe0
        post = []

        def padd(name, src, k, n, last):
            post.append((name, src, k, n, last))

        HB = NB // 2
        for i in range(4):
            padd(f"gb{i}", kcol(w_in2, D + HB * i, HB), 8, HB, ("glu_b", i, 1, 1))
            padd(f"ga{i}", kcol(w_in2, HB * i, HB), 8, HB, ("glu_a", i, 1, 1))
        GORDER = (1, 2, 0)
        for g in GORDER:
            for j, c in enumerate("qkv"):
                padd(f"{c}{g}", kcol(w_in2, 3072 + 1536 * j + NB * g, NB), 8, NB, ("w" + c, g, T - 1))
        for i in range(2):
            padd(f"za{i}", kcol(w_in2, 7680 + HB * i, HB), 8, HB, ("za", 3, 1))
        for i in range(4):
            padd(f"gt{i}", kcol(w_in2, 9216 + HB * i, HB), 8, HB, ("gt", 2 * i + 1, 1))
        padd("ao", A["w_att_out_2"][0].rearrange("(k p) n -> p k n", p=P), 4, 1024, ("ya", 7, 1))
        for i in range(4):
            padd(f"zc{i}", kcol(w_in2, 2048 + HB * i, HB), 8, HB, ("zc", 2 * i + 1, 1))
        for i in range(4):
            padd(f"gc{i}", kcol(w_in2, 8192 + HB * i, HB), 8, HB, ("gc", 2 * i + 1, 1))
            padd(f"co{i}", kcol(A["w_conv_out_2"][0], HB * i, HB), 8, HB, ("yc", 2 * i + 1, 1))
        for i in range(4):
            padd(f"wo{i}", kcol(A["w_o_2"][0], HB * i, HB), 8, HB, ("y2", i, T - 1))
        split_order = [w[0] for w in post if w[0][:2] in ("gb", "ga", "za", "gt", "zc", "gc", "wo")]
        seq = {w[0]: i for i, w in enumerate(weights)}
        seq.update({w[0]: n_post + i for i, w in enumerate(post)})
        shape = {w[0]: (w[2], w[3]) for w in weights + post}

        def wslot(n):
            return n % RING

        def wview(name):
            k, n = shape[name]
            return ring[wslot(seq[name])][:, 0:k * n].rearrange("p (k n) -> p k n", k=k)

        def w_wait(pe, name):
            n = seq[name]
            pe.wait_ge(w_full[wslot(n)], 16 * (n // RING + 1))

        def split_views(name):
            k, n = shape[name]
            slot = W0 + 4096 * wslot(seq[name])
            return [mem_r(slot + at_, k * n).rearrange("p (k n) -> p k n", k=k) for at_ in (2048, 0)]

        bk.add("cols")
        for c in range(2):
            bk.add(("bd", c))
        for t in range(T):
            bk.add(("n1", t, 0)), bk.add(("n1", t, 1))
        for t in range(T):
            bk.add(("uf", t))
        for t in range(T):
            bk.add(("ua", t)), bk.add(("ub", t))
            if t >= 1:
                bk.add(("lt", t - 1, 0)), bk.add(("lt", t - 1, 1))
        bk.add(("lt", T - 1, 0)), bk.add(("lt", T - 1, 1))
        for c in range(4):
            for r in range(4):
                bk.add(("pq", c, r))
            for h in range(2):
                bk.add(("yf", c, h))
        for t in range(T):
            bk.add(("kv", t, 0)), bk.add(("kv", t, 1))
            if t >= 1:
                bk.add(("kt", t - 1, 0)), bk.add(("kt", t - 1, 1))
        bk.add(("kt", T - 1, 0)), bk.add(("kt", T - 1, 1))
        for t in range(T):
            bk.add(("q", t, 0)), bk.add(("q", t, 1))
            if t >= 1:
                bk.add(("qt", t - 1, 0)), bk.add(("qt", t - 1, 1))
        bk.add(("qt", T - 1, 0)), bk.add(("qt", T - 1, 1))

        NS = T * H1

        def att1_steps():
            for n in range(-1, NS + 1):
                if n + 1 < NS:
                    yield "s", n + 1
                if 0 <= n < NS:
                    yield "pt", n
                if n - 1 >= 0:
                    yield "pv", n - 1
                    if (n - 1) % H1 == 2 and n - 1 > H1:
                        yield "y", (n - 1) // H1 - 1
            yield "pv_end", 0
            yield "y", T - 1

        for kind, n in att1_steps():
            t, h = divmod(n, H1)
            if kind == "s":
                bk.add(("s1", n), pair=True, bank=2 * (n % 2))
            elif kind == "pt":
                bk.add(("pt", n, 0), bank=4), bk.add(("pt", n, 1), bank=5)
            elif kind == "pv" and h == 0:
                bk.add(("o1", t), bank=6)
            elif kind == "y":
                bk.add(("ot", n), bank=7)
                bk.add(("y1", n, 0), bank=7), bk.add(("y1", n, 1), bank=7)
        bk.next = 0
        for m in range(2):
            bk.add(("nm", m, 0)), bk.add(("nm", m, 1))
        for c in range(8):
            bk.add(("mk", c))
            bk.add(("n2", c, 0)), bk.add(("n2", c, 1))
        for n in range(2):
            for m in range(2):
                bk.add(("mv", m, n))
        for c in range(8):
            bk.add(("mq", c, 0)), bk.add(("mq", c, 1))

        def att2_steps():
            for t in range(-1, T + 2):
                if t + 1 < T:
                    yield "s", t + 1
                if 0 <= t < T:
                    yield "pt", t
                if t - 1 >= 0 and t - 1 < T:
                    yield "y", t - 1
                if t - 2 >= 0 and t - 2 < T:
                    yield "r", t - 2
                if 0 <= t < T:
                    yield "pv", t

        for kind, t in att2_steps():
            if kind == "s":
                bk.add(("s2", t, 0)), bk.add(("s2", t, 1))
            elif kind == "pt":
                bk.add(("p2", t, 0)), bk.add(("p2", t, 1))
            elif kind == "pv":
                bk.add(("o2", t, 0)), bk.add(("o2", t, 1))
            elif kind == "y":
                bk.add(("om", t, 0)), bk.add(("om", t, 1))
                bk.add(("ym", t, 0)), bk.add(("ym", t, 1))
            else:
                bk.add(("n3", t, 0)), bk.add(("n3", t, 1))
                bk.add(("lg", t))
        for c in range(2):
            bk.add(("aft", c))
        for i in range(6):
            bk.add(("ada", i))
        bk.add(("idx",))
        bk.next = 0
        for c in range(2):
            bk.add(("tr0", c))
        bk.next = 2
        MOE = ("g0", "u0", "g1", "u1", "tr0", "tr1", "d0", "d1")
        MOE_BANK = {k: (2 + i) % 8 for i, k in enumerate(MOE)}
        moe_base = list(bk.count)
        moe_first = [list(x) for x in bk.last]
        for e in range(NE):
            for k in MOE:
                if e == NE - 1 and k.startswith("tr"):
                    continue
                b = MOE_BANK[k]
                bk.count[b] += 1
                bk.last[b] = [(b, bk.count[b])]

        def moe_val(k, e):
            return moe_base[MOE_BANK[k]] + 1 + e

        bk.next = 0
        for t in range(T):
            bk.add(("n4", t, 0)), bk.add(("n4", t, 1))
        QUAD = [(c, h) for h in range(2) for c in range(2)]
        for i in range(4):
            for c, h in QUAD:
                bk.add(("glu_b", i, c, h))
            for c, h in QUAD:
                bk.add(("glu_a", i, c, h))
        def keys_of(g, tile):
            if g == 0:
                return [tile] if tile == 0 else [tile - 1, tile]
            if g == 1:
                return [tile] if tile % 2 == 0 else [tile - 1, tile]
            return [tile]

        tiles2 = [(g, t) for g in GORDER for t in range(T)]

        def win_steps():
            for i in range(len(tiles2) + 2):
                if i < len(tiles2):
                    yield "qkv", i
                if i - 2 >= 0 and tiles2[i - 2][0] == 0:
                    yield "at", i - 2
                if 0 <= i - 1 < len(tiles2):
                    yield "att", i - 1

        for kind, i in win_steps():
            g, t = tiles2[i]
            if kind == "qkv":
                bk.add(("wq", g, t)), bk.add(("wk", g, t)), bk.add(("wv", g, t))
                bk.add(("qkt", g, t, 0)), bk.add(("qkt", g, t, 1))
            elif kind == "att":
                for hp in range(4):
                    bk.add(("sw", g, t, hp))
                for hp in range(4):
                    bk.add(("pw", g, t, hp))
                bk.add(("ow", g, t))
            else:
                bk.add(("at", t))
        ZA = [(c, h) for h in range(2) for c in range(4)]
        za_at = {3: [0], 4: [1], 5: [2], 6: [3], 7: [4, 5], 8: [6, 7]}
        for t in range(T + 1):
            if t < T:
                bk.add(("c1", t, 0)), bk.add(("c1", t, 1))
            for u in za_at.get(t, []):
                bk.add(("za", *ZA[u]))
            if t >= 1:
                bk.add(("c2", t - 1, 0)), bk.add(("c2", t - 1, 1))
        CH = [(c, h) for c in range(8) for h in range(2)]
        for nm in ("gt", "ya", "zc"):
            for c, h in CH:
                bk.add((nm, c, h))
        for i in range(4):
            for nm in ("gc", "yc"):
                for c, h in CH[4 * i:4 * i + 4]:
                    bk.add((nm, c, h))
        for j in range(4):
            for t in range(T):
                bk.add(("y2", j, t))

        uf = mem(GC0, 4096).rearrange("p (t c) -> p t c", t=T)
        gdft = mem(GA0, 4096).rearrange("p (j c) -> p j c", j=8)
        tdft = mem(GB0, 4096).rearrange("p (j c) -> p j c", j=8)
        kvn = mem(GA0 + 4096, 2048).rearrange("p (k s) -> p k s", k=2)
        uq = [mem(GA0 + 6144 + 672 * i, 672) for i in range(2)]
        krt = mem(GA0 + 7488, 256).rearrange("p (t c) -> p t c", t=T)
        mixf = mem(GB0, 4096).rearrange("p (c s) -> p c s", c=4)
        qn = mem(GB0 + 4096, 3072).rearrange("p (k s) -> p k s", k=3)
        bd = mem(GB0 + 7168, 1024).rearrange("p (m c j) -> p m c j", m=2, c=4)
        wbd = mem(GB0, 512).rearrange("p (c j) -> p c j", c=4)
        chan = mem(GB0 + 512, 256).rearrange("p (m j) -> p m j", m=2)
        rows = mem(GB0 + 1024, 1024)
        freq = mem(GB0 + 2048, 24)
        posi = mem(GB0 + 2080, 32).bitcast(I32).rearrange("p (g t) -> p g t", g=4)
        posf = mem(GB0 + 2112, 32).rearrange("p (g t) -> p g t", g=4)
        ang = mem(GB0 + 2176, NF)
        ang2 = mem(GB0 + 2176 + NF, NF)
        pq = mem(HT0, 8192).rearrange("p (c r m k) -> p c r m k", c=4, r=8, m=2)
        KT = mem(HT0, 8192)[0:HD1, :].rearrange("p (h s) -> p h s", h=H1)
        QT = mem(GA0, 8192)[0:HD1, :].rearrange("p (h s) -> p h s", h=H1)
        V1 = mem(GC0, 4096).rearrange("p (t c) -> p t c", t=T)
        pexp = [mem(GB0 + 4096 + 1024 * i, 1024) for i in range(2)]
        ptr = [mem(GB0 + 6144 + 1024 * i, 1024).rearrange("p (k q) -> p k q", k=8) for i in range(2)]
        o1 = [HN[0][:, 512 * i:512 * i + 512] for i in range(2)]
        mixa = [HN[1][:, 512 * i:512 * i + 512].rearrange("p (c s) -> p c s", c=4) for i in range(2)]
        memx = mem(GA0, 2048).rearrange("p (m d) -> p m d", m=2)
        mnT = mem(GB0 + 2048, 2048).rearrange("p (k s) -> p k s", k=KC)
        KM = mem(GB0 + 4096, 2048).rearrange("p (k s) -> p k s", k=KC)
        VM = mem(GB0 + 6144, 2048).rearrange("p (m d) -> p m d", m=2)
        QM = mem(GA0, 8192).rearrange("p (k s) -> p k s", k=KC)
        p2 = [mem(GC0 + 1024 * i, 1024) for i in range(2)]
        pt2 = [mem(GC0 + 2048 + 1024 * i, 1024) for i in range(2)]
        om = [mem(GB0 + 1024 * i, 1024) for i in range(2)]
        omt = [mem(GB0 + 2048 + 1024 * i, 1024).rearrange("p (k s) -> p k s", k=KC) for i in range(2)]
        rt = [mem(HT0 + 1024 * i, 1024).rearrange("p (k s) -> p k s", k=KC) for i in range(2)]
        aff = mem(HT0 + 2048, P).rearrange("p (t e) -> p t e", e=NE)
        affT = mem(HT0 + 3072, S)[0:NE, :]
        vals = mem(HT0 + 4096, CAP)[0:NE, :]
        inds = mem(HT0 + 4224, CAP)[0:NE, :].bitcast(U32)
        indf = mem(HT0 + 4352, CAP)[0:NE, :]
        gateT = mem(HT0 + 4480, NE)
        idxT = mem(HT0 + 4496, NE).bitcast(U32)
        idx_g = [mem(HT0 + 4520 + i, 1).bitcast(U32) for i in range(2)]
        idx_s = [mem(HT0 + 4524 + i, 1).bitcast(U32) for i in range(2)]
        moe_ring = ring + [mem(X0, 4096), mem(X0 + 4096, 4096), mem(GC0, 4096)]
        moe_slot = [moe_ring[(n_moe0 + j) % RING] for j in range(3)] + moe_ring[3:]
        moe_in = [sem(f"expert_weights_in{j}") for j in range(MOE_W)]
        down_hi = [mem_r(HT0, 4096), mem_r(GB0 + 4096, 4096)]
        down_lo = [mem_r(X0 + 4096, 4096), mem_r(GC0, 4096)]
        xg = [mem(GA0 + 1024 * i, 1024) for i in range(2)]
        xt = [mem(GA0 + 2048 + 1024 * i, 1024).rearrange("p (k s) -> p k s", k=KC) for i in range(2)]
        hid_hi = mem_r(GA0 + 4096, 1024)
        hid_lo = mem_r(GA0 + 5120, 1024)
        sil = [mem(GA0 + 6144 + 512 * i, 512) for i in range(2)]
        ye = [mem(GB0 + 1024 * i, 1024) for i in range(2)]
        cb = mem(GB0 + 5120, 1024).rearrange("p (k m) -> p k m", k=KC)
        gate_b = mem(HT0 + 1024, 1024)
        bgate = mem(GB0 + 4096, 1024)
        gfin = mem(GA0 + 7168, 1024)
        modc = mem(HT0 + 5120, 2 * KC)
        gate_t = mem(GB0 + 6144, 1024)
        U = mem(GA0, 8192).rearrange("p (k s) -> p k s", k=KC)
        XB = mem(GB0, 8192).rearrange("p (t d) -> p t d", t=T)
        n4_tmp = [mem(GC0 + 512 * i, 512) for i in range(4)]
        n4_junk = [mem(GC0 + 2048 + 1024 * i, 1024) for i in range(2)]
        HT_r, HT_Xr = (mem_r(at_, 8192).rearrange("p (k s) -> p k s", k=KC) for at_ in (HT0, X0))
        ht_1, ht_2 = (HT_r, HT_Xr), (HT_Xr, HT_r)
        sig = [mem(GC0 + 512 * i, 512) for i in range(8)]
        C = mem(GB0, 8192).rearrange("p (k s) -> p k s", k=KC)
        qT2 = [mem(X0 + 512 * i, 512).rearrange("p (h s) -> p h s", h=4) for i in range(2)]
        kT2 = [mem(X0 + 1024 + 512 * i, 512).rearrange("p (h s) -> p h s", h=4) for i in range(3)]
        V2 = [mem(X0 + 2560 + 512 * i, 512) for i in range(3)]
        pw = [mem(X0 + 4096 + 512 * i, 512) for i in range(2)]
        pwt = [mem(X0 + 5120 + 512 * i, 512).rearrange("p (j q) -> p j q", j=4) for i in range(2)]
        num = mem(X0 + 6144, 528)
        rtmp2 = [mem(X0 + 6672 + 128 * i, 128).rearrange("p (h f) -> p h f", f=8) for i in range(3)]
        lst = mem(X0 + 7056, 32)
        wcomb = mem(X0 + 7088, 80)
        qks = HN[0]
        lnum = [HN[1][:, 0:512], HN[1][:, 512:1024]]
        attT = mem(GC0, 4096).rearrange("p (c s) -> p c s", c=4)
        M = mem(GA0, 8192).rearrange("p (k s) -> p k s", k=KC)
        za_tmp = [mem(GA0 + 512 * i, 512) for i in range(2)]
        tmp = [HN[i][:, 512 * j:512 * j + 512] for i in range(2) for j in range(2)]
        Mr = mem_r(GA0, 8192).rearrange("p (k s) -> p k s", k=KC)
        M_part = [mem_r(GC0 + S * k, S) if k < 4 else mem_r(X0 + S * (k - 4), S) for k in range(KC)]
        M_hi = [M_part[k] if k in (4, 5) else Mr[:, k, :] for k in range(KC)]
        M_lo = [Mr[:, k, :] if k in (4, 5) else M_part[k] for k in range(KC)]
        fg = mem(HT0, 1024)
        junk = mem(HT0 + 2048, 1024)
        y2_tmp = [mem(HT0 + 3072 + HB * i, HB) for i in range(2)]

        rtmp = [mask[:, 128 * i:128 * i + 128] for i in range(3)]
        negm, rsum, rrec = mask[:, 0:64], mask[:, 64:128], mask[:, 128:192]

        def tile(t):
            return slice(P * t, P * t + P)

        def gain(row, k0, k1, n=P):
            return cols[:, k0:k1, row].unsqueeze(2).to_broadcast([P, k1 - k0, n])

        def b4(b, n=4):
            return PS[:, b, 0:n * P].rearrange("p (k s) -> p k s", k=n)

        def wait_sum(eng, name, v):
            if v > 0:
                eng.wait_ge(sem(name), v)

        class Chain:

            def __init__(self, eng, name):
                self.eng, self.sem, self.n = eng, sem(name), 0

            def __call__(self, ins):
                self.n += 1
                ins.then_inc(self.sem, 1)
                self.eng.wait_ge(self.sem, self.n)

        def pv_wait(eng, n):
            t, h = divmod(n, H1)
            if h == H1 - 1:
                bk.wait(eng, ("o1", t))
            else:
                eng.wait_ge(sem("pv_done"), (H1 - 1) * t + h + 1)

        def win_head(u, j):
            return 4 * (u // 2) + u % 2 + 2 * j

        def num_before(i):
            return sum(16 for g, _ in tiles2[:i] if g != 0)

        def wv_wait(eng, i, hp):
            if hp < 0:
                i, hp = i - 1, hp + 4
                if i < 0:
                    return
            if hp == 3:
                bk.wait(eng, ("ow", *tiles2[i]))
            else:
                eng.wait_ge(sem("wv_done"), 3 * i + hp + 1)

        block = ctx.enter_context(nc.Block())

        @block.sync
        def _(sp):
            def fetch(n, w):
                name, src, k, cnt, _ = w
                if n >= RING:
                    prev = (weights[n - RING] if n - RING < n_moe0 else post[n - RING - n_post])
                    if prev[4] is not None:
                        bk.wait(sp, prev[4])
                if src is not None:
                    dst = ring[wslot(n)][:, 0:k * cnt].rearrange("p (k n) -> p k n", k=k)
                    sp.dma_start(dst, src).then_inc(w_full[wslot(n)], 16)
                else:
                    sp.sem_inc(w_full[wslot(n)], 16)

            for n, w in enumerate(weights):
                fetch(n, w)
            for n in range(n_moe0 - RING, n_moe0):
                bk.wait(sp, weights[n][4])
            sp.wait_ge(sem("acc_out"), 16 * T)
            sp.wait_ge(sem("n3_ssq"), T)
            sp.wait_ge(sem("n3_hn"), T)
            bk.wait(sp, ("o2", T - 1, 1))
            with sp.Fori(0, NE, 1) as e:
                for j, (w, c) in enumerate((("gate", 0), ("up", 0), ("gate", 1), ("up", 1), ("down", 0), ("down", 1))):
                    was = ("g0", "u0", "g1", "u1", "d0", "d1")[j]
                    sp.wait_ge(full[MOE_BANK[was]], moe_val(was, e) - 1)
                    src = A[f"w_exp_{w}"][0, bass.ds(e, 1), :, NB * c:NB * c + NB].rearrange("o (k p) n -> p (o k) n", p=P)
                    sp.dma_start(moe_slot[j].rearrange("p (k n) -> p k n", k=KC), src).then_inc(moe_in[j], 16)
            for i, w in enumerate(post):
                if i < RING:
                    was = ("g0", "u0", "g1")[(n_post + i - n_moe0) % RING]
                    sp.wait_ge(full[MOE_BANK[was]], moe_val(was, NE - 1))
                fetch2 = w
                if i >= RING:
                    bk.wait(sp, post[i - RING][4])
                dst = wview(w[0])
                sp.dma_start(dst, w[1]).then_inc(w_full[wslot(n_post + i)], 16)
            for t in range(T):
                sp.wait_ge(sem("out_ready"), t + 1)
                sp.dma_start(out[0, tile(t), :], XB[:, t, :]).then_inc(sem("out_done"), 16)
            sp.wait_ge(sem("out_done"), 16 * T)

        @block.gpsimd
        def _(pool):
            ch = Chain(pool, "pool_chain")

            def rstd(dst, src, n):
                ch(nc.gpsimd.tensor_scalar(dst, src, 1.0 / n, EPS, ALU.mult, ALU.add))
                return nc.gpsimd.tensor_tensor(dst, dst, half[:, 0:dst.shape[1]], ALU.pow)

            nc.gpsimd.memset(half[:, 0:4], -0.5)
            nc.gpsimd.memset(half[:, 4:8], float(np.pi / 2)).then_inc(sem("halves"), 1)
            nc.gpsimd.memset(wbd, 0.0)
            ch(nc.gpsimd.memset(rows[0:NROW, :], 0.0))
            wf = A["w_fourier"][0].rearrange("(c b) i j -> b i c j", b=2)
            for b in range(2):
                pool.dma_start(wbd[64 * b:64 * b + 64, :, 64 * b:64 * b + 64], wf[b]).then_inc(sem("wbd_in"), 16)
            vecs = [(R_MIX, A["g_mix"]), (R_MQ, A["g_mem_q"]), (R_MKV, A["g_mem_kv"]), (R_FFN, A["g_ffn"]),
                    (R_N2, A["norm_g_2"]), (R_CB, A["conv_b_2"]), (R_LNG, A["conv_ln_g_2"]),
                    (R_LNB, A["conv_ln_b_2"]), (R_C, A["c_2"]), (R_QL, A["g_q_lat"]), (R_KVL, A["g_kv_lat"])]
            for r, v in vecs:
                pool.dma_start(rows[r:r + 1, 0:v.shape[1]], v).then_inc(sem("rows_in"), 16)
            pool.dma_start(rows[R_SHIFT:R_SHIFT + 3, :], A["b_ada_2"][0].rearrange("(r d) -> r d", r=3)).then_inc(sem("rows_in"), 16)
            pool.dma_start(rows[R_TAP:R_TAP + TAPS, :], A["conv_w_2"][0]).then_inc(sem("rows_in"), 16)

            for t in range(T):
                pool.wait_ge(sem("n1_ssq"), t + 1)
                rstd(st[:, 8 + t:9 + t], st[:, t:t + 1], D).then_inc(sem("n1_rstd"), 1)

            c8 = float(np.sqrt(0.5))
            X8 = [uf[:, t, :] for t in range(8)]
            td = [tdft[:, j, :] for j in range(8)]
            G = [gdft[:, j, :] for j in range(8)]
            tt = nc.gpsimd.tensor_tensor
            s_, d_ = td[0:4], td[4:8]
            steps = []
            for j in range(4):
                steps.append(lambda j=j: tt(s_[j], X8[j], X8[j + 4], ALU.add))
                steps.append(lambda j=j: tt(d_[j], X8[j], X8[j + 4], ALU.subtract))
            steps += [
                lambda: tt(G[2], s_[0], s_[2], ALU.subtract),
                lambda: tt(G[3], s_[3], s_[1], ALU.subtract),
                lambda: tt(s_[0], s_[0], s_[2], ALU.add),
                lambda: tt(s_[1], s_[1], s_[3], ALU.add),
                lambda: tt(G[0], s_[0], s_[1], ALU.add),
                lambda: tt(G[1], s_[0], s_[1], ALU.subtract),
                lambda: tt(s_[2], d_[1], d_[3], ALU.subtract),
                lambda: tt(s_[3], d_[1], d_[3], ALU.add),
                lambda: nc.gpsimd.tensor_scalar(s_[2], s_[2], c8, 0.0, ALU.mult, ALU.add),
                lambda: nc.gpsimd.tensor_scalar(s_[3], s_[3], c8, 0.0, ALU.mult, ALU.add),
                lambda: tt(G[4], d_[0], s_[2], ALU.add),
                lambda: tt(G[6], d_[0], s_[2], ALU.subtract),
                lambda: tt(G[7], d_[2], s_[3], ALU.subtract),
                lambda: tt(d_[2], d_[2], s_[3], ALU.add),
                lambda: nc.gpsimd.tensor_scalar(G[5], d_[2], -1.0, 0.0, ALU.mult, ALU.add),
            ]
            bk.read(pool, ("uf", T - 1))
            pool.wait_ge(sem("tables"), 1)
            bk.read(pool, ("bd", 1))
            bk.read(pool, "cols")
            for t in range(T):
                pool.wait_ge(sem("l_ssq"), 2 * t + 2)
                a, b = st[:, 16 + 2 * t:17 + 2 * t], st[:, 17 + 2 * t:18 + 2 * t]
                ra, rb = st[:, 32 + 2 * t:33 + 2 * t], st[:, 33 + 2 * t:34 + 2 * t]
                nc.gpsimd.tensor_scalar(ra, a, 1.0 / QL, EPS, ALU.mult, ALU.add)
                ch(nc.gpsimd.tensor_scalar(rb, b, 1.0 / KVL, EPS, ALU.mult, ALU.add))
                r2 = st[:, 32 + 2 * t:34 + 2 * t]
                nc.gpsimd.tensor_tensor(r2, r2, half[:, 0:2], ALU.pow).then_inc(sem("l_rstd"), 1)
                for f in steps[3 * t:3 * t + 3]:
                    ch(f())
            pool.sem_inc(sem("dft_done"), 1)

            for t in range(T):
                if t >= 2:
                    bk.wait(pool, ("kt", t - 2, 1))
                else:
                    bk.wait(pool, ("lt", T - 2 + t, 1))
                pool.wait_ge(sem("kr_done"), t + 1)
                kt_ = HN[t % 2][:, 0:H1 * HD1].rearrange("p (h c) -> p h c", h=H1)
                nc.gpsimd.tensor_copy(kt_[:, :, NOPE:HD1], krt[:, t, :].unsqueeze(1).to_broadcast([P, H1, ROPE])).then_inc(sem("k_rope"), 1)

            bk.wait(pool, ("s1", NS - 1))
            for m in range(2):
                pool.dma_start(memx[:, m, :], A["mem"][0, tile(m), :]).then_inc(sem(f"mem_in{m}"), 16)
            for m in range(2):
                pool.wait_ge(sem("nm_ssq"), m + 1)
                rstd(st[:, 50 + m:51 + m], st[:, 48 + m:49 + m], D).then_inc(sem("nm_rstd"), 1)
            for t in range(T):
                pool.wait_ge(sem("n2_ssq"), t + 1)
                rstd(st[:, 60 + t:61 + t], st[:, 52 + t:53 + t], D).then_inc(sem("n2_rstd"), 1)
            for t in range(T):
                bk.read(pool, ("ym", t, 1))
                pool.dma_start(dram["acc"][tile(t), :], X[:, t, :]).then_inc(sem("acc_out"), 16)
                pool.wait_ge(sem("n3_ssq"), t + 1)
                rstd(st[:, 76 + t:77 + t], st[:, 68 + t:69 + t], D).then_inc(sem("n3_rstd"), 1)
                pool.wait_ge(sem("n3_hn"), t + 1)
                pool.dma_start(dram["h0"][tile(t), :], HN[t % 2]).then_inc(sem(f"h0_out{t % 2}"), 16)
            nc.gpsimd.tensor_copy(cb, cols[:, :, R_C:R_C + 1].to_broadcast([P, KC, P])).then_inc(sem("c_wide"), 1)
            bcast = lambda v: v.rearrange("(o d) -> o d", o=1).to_broadcast([P, D])
            pool.dma_start(bgate, bcast(A["b_ada_2"][0, 2 * D:3 * D])).then_inc(sem("wide_in"), 16)
            pool.dma_start(mask, A["k_mask"]).then_inc(sem("mask_in"), 16)
            for i in range(4):
                bk.read(pool, ("ada", i))
            mv_ = modc.rearrange("p (m k) -> p m k", m=2)
            av_ = affine.rearrange("p (m k) -> p m k", m=2)
            nc.gpsimd.tensor_tensor(av_[:, 1, :], mv_[:, 0, :], cols[:, :, R_SHIFT], ALU.add)
            ch(nc.gpsimd.tensor_tensor(av_[:, 0, :], mv_[:, 1, :], cols[:, :, R_SCALE], ALU.add))
            ch(nc.gpsimd.tensor_scalar(av_[:, 0, :], av_[:, 0, :], 1.0, 0.0, ALU.add, ALU.add))
            nc.gpsimd.tensor_tensor(av_[:, 0, :], av_[:, 0, :], cols[:, :, R_N2], ALU.mult).then_inc(sem("affine"), 1)
            bk.read(pool, ("ada", 5))
            pool.dma_start(gfin, bcast(A["g_final"])).then_inc(sem("gfin_in"), 16)
            pool.wait_ge(sem("wide_in"), 16)
            nc.gpsimd.tensor_tensor(gate_t, gate_t, bgate, ALU.add).then_inc(sem("gate"), 1)
            pool.wait_ge(sem("gate"), 1)
            pool.dma_start(dram["gate"], gate_t[0:1, :]).then_inc(sem("gate_out"), 16)

            def gather(e, par, k, wait):
                if wait is not None:
                    wait()
                nc.gpsimd.tensor_copy(idx_g[par], idxT[:, bass.ds(e, 1)]).then_inc(sem("idx_g"), 1)
                pool.wait_ge(sem("idx_g"), e + 1)
                pool.sem_inc(sem("pool_step"), 1)
                pool.indirect_dma_start(xg[par], None, dram["h0"], bass.IndirectOffsetOnAxis(ap=idx_g[par], axis=0)).then_inc(sem(f"xg_in{par}"), 16)

            def scatter(e, par):
                pool.wait_ge(sem("scattered"), 16 * e)
                nc.gpsimd.tensor_copy(idx_s[par], idxT[:, bass.ds(e, 1)]).then_inc(sem("idx_s"), 1)
                pool.wait_ge(sem("idx_s"), e + 1)
                pool.wait_ge(sem("y_ready"), 2 * e + 2)
                pool.sem_inc(sem("pool_step"), 1)
                pool.indirect_dma_start(dram["acc"], bass.IndirectOffsetOnAxis(ap=idx_s[par], axis=0), ye[par], None, compute_op=ALU.add).then_inc(sem("scattered"), 16)

            bk.read(pool, ("idx",))
            for i in range(2):
                pool.wait_ge(sem(f"h0_out{i}"), 16 * (T // 2))
            pool.wait_ge(sem("acc_out"), 16 * T)
            gather(0, 0, 0, None)
            gather(1, 1, 0, None)

            def scatter_first(par):
                nc.gpsimd.tensor_copy(idx_s[par], idxT[:, 0:1]).then_inc(sem("idx_s"), 1)
                pool.wait_ge(sem("idx_s"), 1)
                pool.wait_ge(sem("y_ready"), 2)
                pool.indirect_dma_start(dram["acc"], bass.IndirectOffsetOnAxis(ap=idx_s[par], axis=0), ye[par], None, compute_op=ALU.add).then_inc(sem("scattered"), 16)

            scatter_first(0)
            bk.wait(pool, ("tr0", 1))
            gather(2, 0, 0, None)
            with pool.Fori(0, (NE - 4) // 2 + 0, 1) as j:
                for sub in range(2):
                    e = 2 * j + 1 + sub
                    par = (1 + sub) % 2
                    scatter(e, par)
                    pool.wait_ge(full[MOE_BANK["tr1"]], moe_val("tr1", e - 1))
                    gather(e + 2, par, 0, None)
            def split(name):
                k, n = shape[name]
                slot = W0 + 4096 * wslot(seq[name])
                w_wait(pool, name)
                ch(nc.gpsimd.tensor_scalar(mem_r(slot + 2048, k * n), mem(slot, k * n), 1.0, 0.0, ALU.mult, ALU.add))
                nc.gpsimd.tensor_tensor(mem_r(slot, k * n), mem(slot, k * n), value(mem_r(slot + 2048, k * n)), ALU.subtract).then_inc(sem("split"), 1)
                assert name == split_order[n_split[0]]
                n_split[0] += 1

            n_split = [0]
            for e in range(NE - 3, NE):
                if e == NE - 1:
                    split("gb0"), split("ga0")
                scatter(e, e % 2)
                if e + 2 < NE:
                    pool.wait_ge(full[MOE_BANK["tr1"]], moe_val("tr1", e - 1))
                    gather(e + 2, e % 2, 0, None)
            pool.wait_ge(sem("scattered"), 16 * NE)
            for t in range(T):
                pool.dma_start(XB[:, t, :], dram["acc"][tile(t), :]).then_inc(sem(f"x_back{t}"), 16)
            for t in range(T):
                pool.wait_ge(sem("n4a_ssq"), t + 1)
                rstd(st[:, 92 + t:93 + t], st[:, 84 + t:85 + t], D).then_inc(sem("n4a_rstd"), 1)
                pool.wait_ge(sem("n4a_x"), t + 1)
                pool.dma_start(dram["x4"][tile(t), :], XB[:, t, :]).then_inc(sem("x4_out"), 16)
                pool.wait_ge(sem("n4b_ssq"), t + 1)
                rstd(st[:, 108 + t:109 + t], st[:, 100 + t:101 + t], D).then_inc(sem("n4b_rstd"), 1)

            for name in split_order[2:8]:
                split(name)
            pending = 0
            for i, (g, t) in enumerate(tiles2):
                if g != 0:
                    pool.wait_ge(sem("num_ready"), i + 1)
                    if g == 1:
                        r, b = divmod(t, 2)
                        dst = dram["num1"].rearrange("(b j r) c -> b r j c", b=2, r=4)[b, r]
                        pool.dma_start(dst, num).then_inc(sem("num_out"), 16)
                        pending += 16
                    else:
                        dst = dram["num2"].rearrange("(j m) c -> m j c", m=8)[t]
                        pool.dma_start(dst, num).then_inc(sem("num_out"), 16)
                        pending += 16
            pool.wait_ge(sem("num_out"), pending)
            for t in range(T):
                if t >= 1:
                    pool.wait_ge(sem("comb_done"), t)
                for gi, n in enumerate(("num1", "num2")):
                    pool.dma_start(lnum[gi], dram[n][tile(t), 0:512]).then_inc(sem("lnum_in"), 16)
                    pool.dma_start(lst[:, 16 * gi:16 * gi + 16], dram[n][tile(t), 512:528]).then_inc(sem("lnum_in"), 16)

            rest = iter([(h, k) for h in range(2) for k in range(KC)])

            def ht_rest(n):
                for _ in range(n):
                    h, k = next(rest)
                    pool.wait_ge(sem("ht_hi"), KC * h + k + 1)
                    c = slice(NB * h, NB * h + NB)
                    nc.gpsimd.tensor_tensor(HT_r[:, k, c], HT[:, k, c], value(HT_Xr[:, k, c]), ALU.subtract).then_inc(sem("ht_lo"), 1)

            for t in range(T):
                pool.wait_ge(sem("ln_var"), t + 1)
                v = st[:, 16 + 2 * t + 1:16 + 2 * t + 2]
                ch(nc.gpsimd.tensor_scalar(st[:, 32 + t:33 + t], v, 1.0, EPS, ALU.mult, ALU.add))
                nc.gpsimd.tensor_tensor(st[:, 32 + t:33 + t], st[:, 32 + t:33 + t], half[:, 0:1], ALU.pow).then_inc(sem("ln_rstd"), 1)
                if t in (0, 1, 3, 4):
                    ht_rest(4)
                elif t == 2:
                    split("za0")
                elif t == 5:
                    split("za1")
                elif t == 6:
                    split("gt0")
            for name in split_order[11:22]:
                split(name)
            bk.wait(pool, ("gc", 7, 1))
            pool.dma_start(gate_b, dram["gate"].to_broadcast([P, D])).then_inc(sem("gate_in"), 16)
            pool.dma_start(fg, bcast(A["final_g_2"])).then_inc(sem("fg_in"), 16)
            pool.wait_ge(sem("x4_out"), 16 * T)
            split("wo0")
            bk.wait(pool, ("yc", 7, 1))
            for t in range(T):
                pool.dma_start(XB[:, t, :], dram["x4"][tile(t), :]).then_inc(sem(f"xr_in{t}"), 16)
            for i in range(1, 4):
                split(f"wo{i}")
            for t in range(T):
                pool.wait_ge(sem("n5_ssq"), t + 1)
                rstd(st[:, 60 + t:61 + t], st[:, 52 + t:53 + t], D).then_inc(sem("n5_rstd"), 1)

        @block.scalar
        def _(act):
            ch = Chain(act, "act_chain")

            def copy(name, dst, src, scale=1.0):
                ins = nc.scalar.activation(dst, src, ACT.Copy, scale=scale)
                bk.done(ins, name)

            act.dma_start(ident, A["k_ident"]).then_inc(sem("ident_in"), 16)
            for t in range(T):
                act.dma_start(X[:, t, :], A["x"][0, tile(t), :]).then_inc(sem(f"x_in{t}"), 16)
                if t == 0:
                    act.dma_start(chan, A["k_chan"].rearrange("p (m j) -> p m j", m=2)).then_inc(sem("chan_in"), 16)
                    act.dma_start(freq, A["k_freq"]).then_inc(sem("pos_in"), 16)
                    with nc.allow_non_contiguous_dma("positions"):
                        act.dma_start(posi[:, 0, :], A["positions"].rearrange("o (t p) -> p (o t)", p=P)).then_inc(sem("pos_in"), 16)
                        act.dma_start(posi[:, 1, :], A["positions_2"].rearrange("o (t p) -> p (o t)", p=P)).then_inc(sem("pos_in"), 16)
                        for b in range(2):
                            act.dma_start(posi[:, 2, b:8:2], A["positions_2"][0].rearrange("(b j r) -> b j r", b=2, r=4)[b]).then_inc(sem("pos_in"), 16)
                        act.dma_start(posi[:, 3, :], A["positions_2"][0].rearrange("(j m) -> j m", m=8)).then_inc(sem("pos_in"), 16)
                    act.dma_start(router, A["w_router"][0].rearrange("(k p) e -> p k e", p=P)).then_inc(sem("router_in"), 16)

            act.wait_ge(sem("ang"), 1)
            act.wait_ge(sem("halves"), 1)
            nc.scalar.activation(sin_t, ang, ACT.Sin)
            nc.scalar.activation(cos_t, ang2, ACT.Sin, bias=half[:, 4:5], scale=-1.0).then_inc(sem("tables"), 1)
            for m in range(2):
                b = bk.wait(act, ("bd", m))
                copy(("bd", m), bd[:, m], b4(b))

            def square(src, n, acc, jk):
                return nc.scalar.activation(jk[:, 0:n], src, ACT.Square, accum_out=acc)

            for t in range(T):
                act.wait_ge(sem(f"x_in{t}"), 16)
                if t >= 2:
                    bk.wait(act, ("n1", t - 2, 1))
                square(X[:, t, :], D, st[:, t:t + 1], HN[t % 2]).then_inc(sem("n1_ssq"), 1)
            for t in range(T):
                b = bk.wait(act, ("uf", t))
                copy(("uf", t), uf[:, t, :], PS[:, b, :])
            for t in range(T):
                if t >= 2:
                    act.wait_ge(sem("l_hn"), t - 1)
                b = bk.wait(act, ("ua", t))
                copy(("ua", t), uq[t % 2][:, 0:512], PS[:, b, :])
                b = bk.wait(act, ("ub", t))
                copy(("ub", t), uq[t % 2][:, 512:672], PS[:, b, 0:160])
                bk.read(act, ("ua", t)), bk.read(act, ("ub", t))
                bk.wait(act, ("lt", t - 2, 1) if t >= 2 else ("n1", T - 2 + t, 1))
                square(uq[t % 2][:, 0:QL], QL, st[:, 16 + 2 * t:17 + 2 * t], HN[t % 2]).then_inc(sem("l_ssq"), 1)
                square(uq[t % 2][:, QL:QL + KVL], KVL, st[:, 17 + 2 * t:18 + 2 * t], HN[t % 2][:, QL:QL + KVL]).then_inc(sem("l_ssq"), 1)
            for c in range(4):
                for r in (0, 2):
                    b = bk.wait(act, ("pq", c, r))
                    copy(("pq", c, r), pq[:, c, 2 * r:2 * r + 2, :, :].rearrange("p r m k -> p (r m k)"), PS[:, b, :])
                for h in range(2):
                    b = bk.wait(act, ("yf", c, h))
                    copy(("yf", c, h), mixf[:, c, :].rearrange("p (k r) -> p r k", r=8)[:, 4 * h:4 * h + 4, :], b4(b))
            act.wait_ge(sem("dft_done"), 1)
            for t in range(T):
                bk.wait(act, ("kt", t - 2, 1) if t >= 2 else ("lt", T - 2 + t, 1))
                ktok = HN[t % 2][:, 0:H1 * HD1].rearrange("p (h c) -> p h c", h=H1)
                for j in range(2):
                    b = bk.wait(act, ("kv", t, j))
                    nc.scalar.activation(V1[:, t, 256 * j:256 * j + 256].rearrange("p (h c) -> p h c", h=4), b4(b)[:, :, 64:128], ACT.Copy)
                    copy(("kv", t, j), ktok[:, 4 * j:4 * j + 4, 0:NOPE], b4(b)[:, :, 0:64])
            for t in range(T + 1):
                if t < T:
                    bk.wait(act, ("qt", t - 2, 1) if t >= 2 else ("kt", T - 2 + t, 1))
                    b = bk.wait(act, ("q", t, 0))
                    copy(("q", t, 0), HN[t % 2][:, 0:512], PS[:, b, :])
                    b = bk.wait(act, ("q", t, 1))
                    copy(("q", t, 1), HN[t % 2][:, 512:768], PS[:, b, 0:256])
                if t >= 1:
                    for j in range(2):
                        b = bk.wait(act, ("qt", t - 1, j))
                        copy(("qt", t - 1, j), QT[:, 4 * j:4 * j + 4, tile(t - 1)], b4(b)[0:HD1], scale=HD1 ** -0.5)
            for kind, n in att1_steps():
                if kind == "s":
                    act.wait_ge(sem("a_max"), n + 1)
                    if n >= 2:
                        bk.wait(act, ("pt", n - 2, 1))
                    b = bk.wait(act, ("s1", n))
                    ins = nc.scalar.activation(pexp[n % 2], PS[:, b:b + 2, :].rearrange("p b n -> p (b n)"), ACT.Exp, bias=negm[:, n:n + 1], accum_out=rsum[:, n:n + 1])
                    bk.done(ins, ("s1", n))
                elif kind == "pt":
                    if n >= 2:
                        pv_wait(act, n - 2)
                    b = bk.wait(act, ("pt", n, 0))
                    copy(("pt", n, 0), ptr[n % 2][:, 0:4, :], b4(b))
                elif kind == "y":
                    b = bk.wait(act, ("ot", n))
                    copy(("ot", n), mixa[n % 2], b4(b))
            for m in range(2):
                act.wait_ge(sem(f"mem_in{m}"), 16)
                bk.wait(act, ("y1", T - 1, 1))
                square(memx[:, m, :], D, st[:, 48 + m:49 + m], HN[m]).then_inc(sem("nm_ssq"), 1)
            for c in range(8):
                bk.read(act, ("y1", c, 1))
                bk.wait(act, ("n2", c - 2, 1) if c >= 2 else ("nm", c, 1))
                square(X[:, c, :], D, st[:, 52 + c:53 + c], HN[c % 2]).then_inc(sem("n2_ssq"), 1)
                b = bk.wait(act, ("mk", c))
                copy(("mk", c), KM[:, c, :], PS[:, b, 0:MEM])
            for n in range(2):
                for m in range(2):
                    b = bk.wait(act, ("mv", m, n))
                    copy(("mv", m, n), VM[:, m, NB * n:NB * n + NB], PS[:, b, :])
            for c in range(8):
                for h in range(2):
                    b = bk.wait(act, ("mq", c, h))
                    copy(("mq", c, h), QM[:, c, NB * h:NB * h + NB], PS[:, b, :], scale=MD ** -0.5)
            for kind, t in att2_steps():
                if kind == "s":
                    if t >= 2:
                        bk.wait(act, ("p2", t - 2, 1))
                    for hp in range(2):
                        act.wait_ge(sem("m_max"), 2 * t + hp + 1)
                        b = bk.wait(act, ("s2", t, hp))
                        for hh in range(2):
                            i = 4 * t + 2 * hp + hh
                            ins = nc.scalar.activation(p2[t % 2][:, 256 * (2 * hp + hh):256 * (2 * hp + hh) + 256], PS[:, b, 256 * hh:256 * hh + 256], ACT.Exp, bias=negm[:, i:i + 1], accum_out=rsum[:, i:i + 1])
                        bk.done(ins, ("s2", t, hp))
                elif kind == "pt":
                    if t >= 2:
                        bk.wait(act, ("o2", t - 2, 0))
                    b = bk.wait(act, ("p2", t, 0))
                    copy(("p2", t, 0), pt2[t % 2][:, 0:512], PS[:, b, :])
                elif kind == "y":
                    if t >= 2:
                        bk.wait(act, ("ym", t - 2, 1))
                    for j in range(2):
                        b = bk.wait(act, ("om", t, j))
                        copy(("om", t, j), omt[t % 2][:, 4 * j:4 * j + 4, :], b4(b))
                elif kind == "r":
                    bk.read(act, ("ym", t, 1))
                    if t >= 2:
                        act.wait_ge(sem(f"h0_out{t % 2}"), 16 * (t // 2))
                    bk.wait(act, ("n3", t - 2, 1) if t >= 2 else ("n2", T - 2 + t, 1))
                    square(X[:, t, :], D, st[:, 68 + t:69 + t], HN[t % 2]).then_inc(sem("n3_ssq"), 1)
                    act.wait_ge(sem("r_max"), t + 1)
                    b = bk.wait(act, ("lg", t))
                    ins = nc.scalar.activation(aff[:, t, :], PS[:, b, 0:NE], ACT.Exp, bias=st[:, 120 + t:121 + t], accum_out=st[:, 128 + t:129 + t])
                    bk.done(ins, ("lg", t))
            for c in range(2):
                b = bk.wait(act, ("aft", c))
                copy(("aft", c), affT[:, NB * c:NB * c + NB], PS[0:NE, b, :])
            for i in range(6):
                b = bk.wait(act, ("ada", i))
                if i < 4:
                    copy(("ada", i), modc[:, 4 * i:4 * i + 4], PS[:, b, 0:4])
                else:
                    copy(("ada", i), gate_t[:, NB * (i - 4):NB * (i - 4) + NB], PS[:, b, :])

            def expert(e, par, e1):
                for i in range(2):
                    act.wait_ge(full[MOE_BANK[f"g{i}"]], moe_val(f"g{i}", e))
                    act.wait_ge(free[MOE_BANK[f"u{i}"]], moe_val(f"u{i}", e) - 1)
                    nc.scalar.activation(sil[i], PS[:, MOE_BANK[f"g{i}"], :], ACT.Silu).then_inc(free[MOE_BANK[f"g{i}"]], 1)
                if e1:
                    act.wait_ge(sem("scattered"), 16 * (e - 1))
                for i in range(2):
                    act.wait_ge(full[MOE_BANK[f"d{i}"]], moe_val(f"d{i}", e))
                    act.sem_inc(sem("act_step"), 1)
                    ins = nc.scalar.activation(ye[par][:, NB * i:NB * i + NB], PS[:, MOE_BANK[f"d{i}"], :], ACT.Copy, scale=gateT[:, bass.ds(e, 1)])
                    ins.then_inc(free[MOE_BANK[f"d{i}"]], 1)
                    act.wait_ge(free[MOE_BANK[f"d{i}"]], moe_val(f"d{i}", e))
                    act.sem_inc(sem("y_ready"), 1)

            bk.read(act, ("idx",))
            for e in range(2):
                expert(e, e, False)
            with act.Fori(1, NE // 2, 1) as j:
                for sub in range(2):
                    expert(2 * j + sub, sub, True)

            for t in range(T + 1):
                if t < T:
                    act.wait_ge(sem(f"x_back{t}"), 16)
                    square(XB[:, t, :], D, st[:, 84 + t:85 + t], n4_junk[0]).then_inc(sem("n4a_ssq"), 1)
                    act.wait_ge(sem("n4a_x"), t + 1)
                    square(XB[:, t, :], D, st[:, 100 + t:101 + t], n4_junk[1]).then_inc(sem("n4b_ssq"), 1)
                if t >= 1:
                    u = t - 1
                    for j in range(2):
                        b = bk.wait(act, ("n4", u, j))
                        wait_sum(act, "n4_split", 2 * u + j - 3)
                        for k in range(4):
                            c = slice(P * k, P * k + P)
                            kk = 4 * j + k
                            ins = nc.scalar.activation(n4_tmp[(2 * u + j) % 4][:, c], PS[:, b, c], ACT.Identity, bias=affine[:, KC + kk:KC + kk + 1], scale=affine[:, kk:kk + 1])
                        bk.done(ins, ("n4", u, j))
            act.wait_ge(sem("n4_split"), 2 * T)
            for i in range(4):
                for pos, (c, h) in enumerate(QUAD):
                    b = bk.wait(act, ("glu_b", i, c, h))
                    if i >= 2:
                        bk.read(act, ("glu_a", i - 2, c, h))
                    ins = nc.scalar.activation(sig[(4 * i + pos) % 8], PS[:, b, :], ACT.Sigmoid)
                    bk.done(ins, ("glu_b", i, c, h))
            act.wait_ge(sem("ht_whole"), 2)
            for kind, i in win_steps():
                g, t = tiles2[i]
                if kind == "qkv":
                    if i >= 1:
                        bk.wait(act, ("qkt", *tiles2[i - 1], 1))
                    for j, nm in enumerate("qk"):
                        b = bk.wait(act, ("w" + nm, g, t))
                        copy(("w" + nm, g, t), qks[:, 512 * j:512 * j + 512], PS[:, b, :])
                    if i >= 3:
                        bk.wait(act, ("ow", *tiles2[i - 2]))
                    b = bk.wait(act, ("wv", g, t))
                    copy(("wv", g, t), V2[i % 3], PS[:, b, :])
                    if i >= 2:
                        bk.wait(act, ("sw", *tiles2[i - 2], 3))
                    b = bk.wait(act, ("qkt", g, t, 0))
                    copy(("qkt", g, t, 0), qT2[i % 2], b4(b), scale=E2 ** -0.5)
                    b = bk.wait(act, ("qkt", g, t, 1))
                    copy(("qkt", g, t, 1), kT2[i % 3], b4(b))
                elif kind == "att":
                    w = P * len(keys_of(g, t))
                    for hp in range(4):
                        m = 4 * i + hp
                        for hh in range(2):
                            h = win_head(hp, hh)
                            act.wait_ge(sem("w_max"), m + 1)
                            p_ = pw[hp % 2][:, w * hh:w * hh + w]
                            ins = nc.scalar.activation(p_, p_, ACT.Exp, bias=num[:, 512 + h:513 + h], accum_out=num[:, 520 + h:521 + h])
                        ins.then_inc(sem("w_exp"), 1)
                    if g == 0:
                        act.wait_ge(sem("c_diff"), t + 1)
                        nc.scalar.activation(wcomb[:, 0:24], wcomb[:, 0:24], ACT.Exp).then_inc(sem("c_exp"), 1)
                else:
                    b = bk.wait(act, ("at", t))
                    copy(("at", t), attT[:, :, tile(t)], b4(b))
            for h in range(2):
                for k in range(KC):
                    c = slice(NB * h, NB * h + NB)
                    nc.scalar.activation(HT_Xr[:, k, c], HT[:, k, c], ACT.Copy).then_inc(sem("ht_hi"), 1)
            act.wait_ge(sem("conv"), TAPS * KC)
            for t in range(T + 1):
                for u in za_at.get(t, []):
                    b = bk.wait(act, ("za", *ZA[u]))
                    wait_sum(act, "za_used", u - 1)
                    bk.done(nc.scalar.activation(za_tmp[u % 2], PS[:, b, :], ACT.Silu), ("za", *ZA[u]))
                if t >= 1:
                    for j in range(2):
                        act.wait_ge(sem("ln_aff"), 2 * (t - 1) + j + 1)
                        c_ = C[:, 4 * j:4 * j + 4, tile(t - 1)]
                        nc.scalar.activation(c_, c_, ACT.Silu).then_inc(sem("ln_silu"), 1)
            act.wait_ge(sem("za_used"), 8)
            for c, h in CH:
                b = bk.wait(act, ("gt", c, h))
                bk.done(nc.scalar.activation(M[:, c, NB * h:NB * h + NB], PS[:, b, :], ACT.Sigmoid), ("gt", c, h))
            for n, (c, h) in enumerate(CH):
                b = bk.wait(act, ("zc", c, h))
                wait_sum(act, "tmp_used", n - 3)
                bk.done(nc.scalar.activation(tmp[n % 4], PS[:, b, :], ACT.Silu), ("zc", c, h))
            for n, (c, h) in enumerate(CH):
                b = bk.wait(act, ("gc", c, h))
                act.wait_ge(sem("tmp_used"), 16 + n - 3)
                bk.done(nc.scalar.activation(tmp[n % 4], PS[:, b, :], ACT.Sigmoid), ("gc", c, h))
            for t in range(T):
                act.wait_ge(sem("y2_sum"), 3 * T + t + 1)
                if t >= 1:
                    act.wait_ge(sem("n5_ssq"), t)
                square(XB[:, t, :], D, st[:, 52 + t:53 + t], junk).then_inc(sem("n5_ssq"), 1)

        @block.vector
        def _(dve):
            v = nc.vector
            ch = Chain(dve, "dve_chain")
            bcs = lambda a, n: a.unsqueeze(2).to_broadcast([P, a.shape[1], n])

            dve.wait_ge(sem("pos_in"), 16 * 6)
            ch(v.tensor_copy(posf, posi))
            ang_1 = ang[:, 0:16 * T].rearrange("p (t f) -> p t f", f=16)
            ang_2 = ang[:, 16 * T:NF].rearrange("p (t f) -> p t f", f=8)
            v.tensor_tensor(ang_1, bcs(posf[:, 0, :], 16), freq[:, 0:16].unsqueeze(1).to_broadcast([P, T, 16]), ALU.mult)
            ch(v.tensor_tensor(ang_2, bcs(posf[:, 1:4, :].rearrange("p g t -> p (g t)"), 8), freq[:, 16:24].unsqueeze(1).to_broadcast([P, 3 * T, 8]), ALU.mult))
            ch(v.tensor_scalar(ang2, ang, float(1 / (2 * np.pi)), None, ALU.mult))
            magic = float(1.5 * 2 ** 23)
            ch(v.tensor_scalar(ang2, ang2, magic, None, ALU.add))
            ch(v.tensor_scalar(ang2, ang2, magic, None, ALU.subtract))
            rest = 2 * np.pi
            for bits in (6, 14, 22, None):
                part = float(np.float32(rest)) if bits is None else float(np.floor(rest * 2.0 ** bits) / 2.0 ** bits)
                rest -= part
                ch(v.scalar_tensor_tensor(ang, ang2, -part, ang, ALU.mult, ALU.add))
            pi = float(np.float32(np.pi))
            ch(v.tensor_scalar(ang, ang, pi, -pi, ALU.min, ALU.max))
            ch(v.tensor_scalar(ang2, ang, -1.0, None, ALU.mult))
            v.tensor_tensor(ang2, ang2, ang, ALU.max).then_inc(sem("ang"), 1)
            b = bk.wait(dve, "cols")
            bk.done(v.tensor_copy(cols, PS[:, b, 0:KC * NROW].rearrange("p (k r) -> p k r", r=NROW)), "cols")
            bk.read(dve, "cols")

            def scaled(name, t, src, dst, rs):
                dve.wait_ge(sem(name + "_rstd"), t + 1)
                v.tensor_scalar(dst, src, rs, None, ALU.mult).then_inc(sem(name + "_hn"), 1)

            def gained(name, dst, row, k0, n=4):
                b = bk.wait(dve, name)
                bk.done(v.tensor_tensor(dst, b4(b, n), gain(row, k0, k0 + n), ALU.mult), name)

            for t in range(T + 1):
                if t < T:
                    scaled("n1", t, X[:, t, :], HN[t % 2], st[:, 8 + t:9 + t])
                if t >= 1:
                    for j in range(2):
                        gained(("n1", t - 1, j), HT[:, 4 * j:4 * j + 4, tile(t - 1)], R_MIX, 4 * j)

            def rope(x1, x2, c, s, t1, t2, t3):
                v.tensor_tensor(t1, x1, c, ALU.mult)
                v.tensor_tensor(t2, x2, s, ALU.mult)
                ch(v.tensor_tensor(t3, x1, s, ALU.mult))
                ch(v.tensor_tensor(x1, t1, t2, ALU.subtract))
                ch(v.tensor_tensor(t1, x2, c, ALU.mult))
                return v.tensor_tensor(x2, t1, t3, ALU.add)

            dve.wait_ge(sem("tables"), 1)
            for t in range(T + 1):
                if t < T:
                    dve.wait_ge(sem("l_rstd"), t + 1)
                    v.tensor_scalar(HN[t % 2][:, 0:QL], uq[t % 2][:, 0:QL], st[:, 32 + 2 * t:33 + 2 * t], None, ALU.mult)
                    ch(v.tensor_scalar(HN[t % 2][:, QL:QL + KVL], uq[t % 2][:, QL:QL + KVL], st[:, 33 + 2 * t:34 + 2 * t], None, ALU.mult))
                    kr = uq[t % 2][:, 640:672]
                    c, s = cos_t[:, 16 * t:16 * t + 16], sin_t[:, 16 * t:16 * t + 16]
                    t1, t2, t3 = (x[:, 0:16] for x in rtmp)
                    ch(rope(kr[:, 0:16], kr[:, 16:32], c, s, t1, t2, t3))
                    v.tensor_copy(krt[:, t, :], kr).then_inc(sem("kr_done"), 1)
                    dve.wait_ge(sem("kr_done"), t + 1)
                    dve.sem_inc(sem("l_hn"), 1)
                if t >= 1:
                    u = t - 1
                    b = bk.wait(dve, ("lt", u, 0))
                    v.tensor_tensor(qn[:, :, tile(u)], b4(b)[:, 0:3], gain(R_QL, 0, 3), ALU.mult)
                    ins = v.tensor_tensor(kvn[:, 0:1, tile(u)], b4(b)[:, 3:4], gain(R_KVL, 0, 1), ALU.mult)
                    ch(v.engine_nop()) if False else None
                    bk.done(ins, ("lt", u, 0))
                    gained(("lt", u, 1), kvn[:, 1:2, tile(u)], R_KVL, 1, 1)
            for c in range(4):
                for r in (1, 3):
                    b = bk.wait(dve, ("pq", c, r))
                    bk.done(v.tensor_copy(pq[:, c, 2 * r:2 * r + 2, :, :].rearrange("p r m k -> p (r m k)"), PS[:, b, :]), ("pq", c, r))
            for t in range(T):
                for j in range(2):
                    b = bk.wait(dve, ("kt", t, j))
                    bk.done(v.tensor_copy(KT[:, 4 * j:4 * j + 4, tile(t)], b4(b)[0:HD1]), ("kt", t, j))
            for t in range(T):
                bk.read(dve, ("q", t, 0)), bk.read(dve, ("q", t, 1))
                if t >= 1:
                    dve.wait_ge(sem("q_rope"), t)
                q = HN[t % 2][:, 0:H1 * HD1].rearrange("p (h c) -> p h c", h=H1)
                c, s = (x[:, 16 * t:16 * t + 16].unsqueeze(1).to_broadcast([P, H1, 16]) for x in (cos_t, sin_t))
                t1, t2, t3 = (x.rearrange("p (h f) -> p h f", f=16) for x in rtmp)
                rope(q[:, :, NOPE:NOPE + 16], q[:, :, NOPE + 16:HD1], c, s, t1, t2, t3).then_inc(sem("q_rope"), 1)
            dve.wait_ge(sem("q_rope"), T)
            for kind, n in att1_steps():
                if kind == "s":
                    b = bk.wait(dve, ("s1", n))
                    v.tensor_reduce(negm[:, n:n + 1], PS[:, b:b + 2, :].rearrange("p b n -> p (b n)"), AX.X, ALU.max, negate=True).then_inc(sem("a_max"), 1)
                elif kind == "pt":
                    if n >= 2:
                        pv_wait(dve, n - 2)
                    b = bk.wait(dve, ("pt", n, 1))
                    bk.done(v.tensor_copy(ptr[n % 2][:, 4:8, :], b4(b)), ("pt", n, 1))
                elif kind == "pv" and n % H1 == H1 - 1:
                    t = n // H1
                    bk.read(dve, ("s1", n))
                    ch(v.reciprocal(rrec[:, 8 * t:8 * t + 8], rsum[:, 8 * t:8 * t + 8]))
                    b = bk.wait(dve, ("o1", t))
                    bk.done(v.tensor_tensor(o1[t % 2].rearrange("p (h c) -> p h c", h=H1), PS[:, b, :].rearrange("p (h c) -> p h c", h=H1), bcs(rrec[:, 8 * t:8 * t + 8], VD), ALU.mult), ("o1", t))
                elif kind == "y":
                    for j in range(2):
                        b = bk.wait(dve, ("y1", n, j))
                        x = X[:, n, NB * j:NB * j + NB]
                        bk.done(v.tensor_tensor(x, x, PS[:, b, :], ALU.add), ("y1", n, j))
            for m in range(2):
                scaled("nm", m, memx[:, m, :], HN[m], st[:, 50 + m:51 + m])
            for m in range(2):
                for j in range(2):
                    gained(("nm", m, j), mnT[:, 4 * j:4 * j + 4, tile(m)], R_MKV, 4 * j)
            for t in range(T):
                scaled("n2", t, X[:, t, :], HN[t % 2], st[:, 60 + t:61 + t])
                for j in range(2):
                    gained(("n2", t, j), HT[:, 4 * j:4 * j + 4, tile(t)], R_MQ, 4 * j)
            for kind, t in att2_steps():
                if kind == "s":
                    for hp in range(2):
                        b = bk.wait(dve, ("s2", t, hp))
                        i = 4 * t + 2 * hp
                        v.tensor_reduce(negm[:, i:i + 2], PS[:, b, :].rearrange("p (h k) -> p h k", h=2), AX.X, ALU.max, negate=True).then_inc(sem("m_max"), 1)
                elif kind == "pt":
                    if t >= 2:
                        bk.wait(dve, ("o2", t - 2, 1))
                    b = bk.wait(dve, ("p2", t, 1))
                    bk.done(v.tensor_copy(pt2[t % 2][:, 512:1024], PS[:, b, :]), ("p2", t, 1))
                elif kind == "pv":
                    bk.read(dve, ("s2", t, 0)), bk.read(dve, ("s2", t, 1))
                    ch(v.reciprocal(rrec[:, 4 * t:4 * t + 4], rsum[:, 4 * t:4 * t + 4]))
                    if t >= 2:
                        bk.wait(dve, ("om", t - 2, 1))
                    for hp in range(2):
                        b = bk.wait(dve, ("o2", t, hp))
                        bk.done(v.tensor_tensor(om[t % 2][:, NB * hp:NB * hp + NB].rearrange("p (h c) -> p h c", h=2), PS[:, b, :].rearrange("p (h c) -> p h c", h=2), bcs(rrec[:, 4 * t + 2 * hp:4 * t + 2 * hp + 2], MD), ALU.mult), ("o2", t, hp))
                elif kind == "y":
                    for j in range(2):
                        b = bk.wait(dve, ("ym", t, j))
                        x = X[:, t, NB * j:NB * j + NB]
                        bk.done(v.tensor_tensor(x, x, PS[:, b, :], ALU.add), ("ym", t, j))
                else:
                    scaled("n3", t, X[:, t, :], HN[t % 2], st[:, 76 + t:77 + t])
                    if t >= 2:
                        bk.wait(dve, ("lg", t - 2))
                    for j in range(2):
                        gained(("n3", t, j), rt[t % 2][:, 4 * j:4 * j + 4, :], R_FFN, 4 * j)
                    b = bk.wait(dve, ("lg", t))
                    v.tensor_reduce(st[:, 120 + t:121 + t], PS[:, b, 0:NE], AX.X, ALU.max, negate=True).then_inc(sem("r_max"), 1)
                    bk.read(dve, ("lg", t))
                    ch(v.reciprocal(st[:, 136 + t:137 + t], st[:, 128 + t:129 + t]))
                    v.tensor_scalar(aff[:, t, :], aff[:, t, :], st[:, 136 + t:137 + t], None, ALU.mult).then_inc(sem("aff"), 1)
            bk.read(dve, ("aft", 0)), bk.read(dve, ("aft", 1))
            for r in range(CAP // 8):
                top = vals[:, 8 * r:8 * r + 8]
                ch(v.max(top, affT))
                ch(v.max_index(inds[:, 8 * r:8 * r + 8], top, affT))
                ch(v.match_replace(affT, top, affT, -1.0))
            v.tensor_copy(indf, inds).then_inc(sem("top"), 1)
            b = bk.wait(dve, ("idx",))
            v.tensor_copy(gateT, PS[:, b, 0:NE])
            bk.done(v.tensor_copy(idxT, PS[:, b, NE:2 * NE]), ("idx",))

            def turned(par, banks, vals_):
                for j in range(2):
                    dve.wait_ge(full[banks[j]], vals_[j])
                    v.tensor_tensor(xt[par][:, 4 * j:4 * j + 4, :], b4(banks[j]), gain(R_FFN, 4 * j, 4 * j + 4), ALU.mult).then_inc(free[banks[j]], 1)

            turned(0, [bk.at[("tr0", j)][0] for j in range(2)], [bk.at[("tr0", j)][1] for j in range(2)])

            def expert(e, par, e1, last=False):
                def down_split(i):
                    lo = moe_slot[4 + i]
                    dve.wait_ge(moe_in[4 + i], 16 * e + 16)
                    dve.wait_ge(full[MOE_BANK[f"d{i}"]], moe_val(f"d{i}", e) - 1)
                    for j in range(2):
                        c = slice(2048 * j, 2048 * j + 2048)
                        v.tensor_copy(down_hi[i][:, c], lo[:, c]).then_inc(sem("down_hi"), 1)
                        dve.wait_ge(sem("down_hi"), 4 * e + 2 * i + j + 1)
                        v.tensor_tensor(down_lo[i][:, c], lo[:, c], value(down_hi[i][:, c]), ALU.subtract).then_inc(sem("down_split"), 1)

                for i in range(2):
                    dve.wait_ge(free[MOE_BANK[f"g{i}"]], moe_val(f"g{i}", e))
                    dve.wait_ge(full[MOE_BANK[f"u{i}"]], moe_val(f"u{i}", e))
                    v.tensor_tensor(sil[i], PS[:, MOE_BANK[f"u{i}"], :], sil[i], ALU.mult).then_inc(sem("hid_step"), 1)
                    dve.wait_ge(sem("hid_step"), 4 * e + 2 * i + 1)
                    c = slice(NB * i, NB * i + NB)
                    v.tensor_copy(hid_hi[:, c], sil[i]).then_inc(sem("hid_step"), 1)
                    dve.wait_ge(sem("hid_step"), 4 * e + 2 * i + 2)
                    v.tensor_tensor(hid_lo[:, c], sil[i], value(hid_hi[:, c]), ALU.subtract).then_inc(free[MOE_BANK[f"u{i}"]], 1)
                    if i == 0:
                        down_split(0)
                if not last:
                    turned(1 - par, [MOE_BANK["tr0"], MOE_BANK["tr1"]], [moe_val("tr0", e), moe_val("tr1", e)])
                down_split(1)

            dve.wait_ge(sem("gate_out"), 16)
            for e in range(2):
                expert(e, e, False)
            with dve.Fori(1, NE // 2 - 1, 1) as j:
                for sub in range(2):
                    expert(2 * j + sub, sub, True)
            for e in range(NE - 2, NE):
                expert(e, e % 2, True, e == NE - 1)

            dve.wait_ge(sem("gfin_in"), 16)
            dve.wait_ge(sem("affine"), 1)
            for t in range(T + 1):
                if t < T:
                    dve.wait_ge(sem("n4a_rstd"), t + 1)
                    v.scalar_tensor_tensor(XB[:, t, :], XB[:, t, :], st[:, 92 + t:93 + t], gfin, ALU.mult, ALU.mult).then_inc(sem("n4a_x"), 1)
                    if t >= 2:
                        bk.wait(dve, ("n4", t - 2, 1))
                    scaled("n4b", t, XB[:, t, :], HN[t % 2], st[:, 108 + t:109 + t])
                if t >= 1:
                    u = t - 1
                    for j in range(2):
                        bk.read(dve, ("n4", u, j))
                        s_ = n4_tmp[(2 * u + j) % 4].rearrange("p (k s) -> p k s", k=4)
                        hi, lo = (x[:, 4 * j:4 * j + 4, tile(u)] for x in ht_1)
                        ch(v.tensor_copy(hi, s_))
                        v.tensor_tensor(lo, s_, value(hi), ALU.subtract).then_inc(sem("n4_split"), 1)
            dve.wait_ge(sem("x4_out"), 16 * T)
            dve.wait_ge(sem("n4b_hn"), T)

            def conv_steps():
                for k in range(KC):
                    for j in reversed(range(TAPS)):
                        yield k, j
            conv = iter(list(conv_steps()))
            conv_n = [0]
            def conv_some(n, last_chunk):
                for _ in range(n):
                    if conv_n[0] // TAPS > last_chunk or conv_n[0] >= TAPS * KC:
                        return
                    k, j = next(conv)
                    if j == TAPS - 1:
                        bk.read(dve, ("glu_a", k // 2, k % 2, 0)), bk.read(dve, ("glu_a", k // 2, k % 2, 1))
                        ins = v.tensor_scalar(C[:, k, :], U[:, k, :], cols[:, k, R_TAP + j:R_TAP + j + 1], cols[:, k, R_CB:R_CB + 1], ALU.mult, ALU.add)
                    else:
                        d = TAPS - 1 - j
                        ins = v.scalar_tensor_tensor(C[:, k, d:S], U[:, k, 0:S - d], cols[:, k, R_TAP + j:R_TAP + j + 1], C[:, k, d:S], ALU.mult, ALU.add)
                    ins.then_inc(sem("conv"), 1)
                    conv_n[0] += 1
                    dve.wait_ge(sem("conv"), conv_n[0])

            for i in range(4):
                for pos, (c, h) in enumerate(QUAD):
                    bk.read(dve, ("glu_b", i, c, h))
                    b = bk.wait(dve, ("glu_a", i, c, h))
                    bk.done(v.tensor_tensor(U[:, 2 * i + c, NB * h:NB * h + NB], PS[:, b, :], sig[(4 * i + pos) % 8], ALU.mult), ("glu_a", i, c, h))
                    conv_some(10 if i < 3 else (4, 4, 0, 0)[pos], 2 * i - 1 + 2 * (pos == 3))

            def final_norm(t):
                dve.wait_ge(sem("n5_rstd"), t + 1)
                if t == 0:
                    dve.wait_ge(sem("fg_in"), 16)
                v.scalar_tensor_tensor(XB[:, t, :], XB[:, t, :], st[:, 60 + t:61 + t], fg, ALU.mult, ALU.mult).then_inc(sem("out_ready"), 1)

            bk.wait(dve, ("glu_a", 3, 1, 1))
            for h in range(2):
                c = slice(NB * h, NB * h + NB)
                v.tensor_tensor(HT[:, :, c], value(HT_r[:, :, c]), value(HT_Xr[:, :, c]), ALU.add).then_inc(sem("ht_whole"), 1)
            dve.wait_ge(sem("ht_whole"), 2)

            dve.wait_ge(sem("mask_in"), 16)
            nstep = -(-(TAPS * KC - conv_n[0]) // (3 * T))
            for kind, i in win_steps():
                g, t = tiles2[i]
                if kind == "qkv":
                    conv_some(nstep, KC)
                    bk.read(dve, ("wq", g, t)), bk.read(dve, ("wk", g, t))
                    x = qks.rearrange("p (h c) -> p h c", c=E2)
                    o = 16 * T + 8 * (T * g + t)
                    c, s = (y[:, o:o + 8].unsqueeze(1).to_broadcast([P, 2 * H2, 8]) for y in (cos_t, sin_t))
                    rope(x[:, :, 0:8], x[:, :, 8:16], c, s, *rtmp2).then_inc(sem("w_rope"), 1)
                    dve.wait_ge(sem("w_rope"), i + 1)
                elif kind == "att":
                    nk = len(keys_of(g, t))
                    w = P * nk
                    mk = mask[:, 0:256] if nk == 2 else (mask[:, 256:384] if g == 2 else mask[:, 128:256])
                    if i >= 1 and tiles2[i - 1][0] != 0:
                        dve.wait_ge(sem("num_out"), num_before(i))
                    if i >= 1 and tiles2[i - 1][0] == 0:
                        bk.wait(dve, ("at", tiles2[i - 1][1]))

                    def weights_out(hp):
                        b = bk.wait(dve, ("pw", g, t, hp))
                        if hp >= 2 or i >= 1:
                            wv_wait(dve, i, hp - 2)
                        bk.done(v.tensor_copy(pwt[hp % 2][:, 0:2 * nk, :], b4(b)[:, 0:2 * nk]), ("pw", g, t, hp))

                    for hp in range(4):
                        b = bk.wait(dve, ("sw", g, t, hp))
                        if hp >= 2:
                            bk.wait(dve, ("pw", g, t, hp - 2))
                        for hh in range(2):
                            h = win_head(hp, hh)
                            ins = v.tensor_tensor_reduce(pw[hp % 2][:, w * hh:w * hh + w], PS[:, b, w * hh:w * hh + w], mk, 1.0, -3.0e38, ALU.add, ALU.max, num[:, 512 + h:513 + h])
                        bk.done(ins, ("sw", g, t, hp))
                        bk.read(dve, ("sw", g, t, hp))
                        nm = num[:, 512 + win_head(hp, 0):513 + win_head(hp, 1):2]
                        v.tensor_scalar(nm, nm, -1.0, None, ALU.mult).then_inc(sem("w_max"), 1)
                        if hp >= 1:
                            weights_out(hp - 1)
                    weights_out(3)
                    b = bk.wait(dve, ("ow", g, t))
                    bk.done(v.tensor_copy(num[:, 0:512], PS[:, b, :]), ("ow", g, t))
                    bk.read(dve, ("ow", g, t))
                    dve.wait_ge(sem("w_exp"), 4 * i + 4)
                    dve.wait_ge(sem("w_max"), 4 * i + 4)
                    dve.sem_inc(sem("num_ready"), 1)
                    if g == 0:
                        dve.wait_ge(sem("lnum_in"), 64 * (t + 1))
                        nm = [num[:, 512:520], lst[:, 0:8], lst[:, 16:24]]
                        dn = [num[:, 520:528], lst[:, 8:16], lst[:, 24:32]]
                        nall, wsum = wcomb[:, 24:32], wcomb[:, 32:40]
                        ch(v.tensor_tensor(nall, nm[0], nm[1], ALU.min))
                        ch(v.tensor_tensor(nall, nall, nm[2], ALU.min))
                        for j in range(3):
                            ins = v.tensor_tensor(wcomb[:, 8 * j:8 * j + 8], nall, nm[j], ALU.subtract)
                        ins.then_inc(sem("c_diff"), 1)
                        dve.wait_ge(sem("c_exp"), t + 1)
                        for j in range(3):
                            ins = v.tensor_tensor(wcomb[:, 40 + 8 * j:48 + 8 * j], wcomb[:, 8 * j:8 * j + 8], dn[j], ALU.mult)
                        ch(ins)
                        ch(v.tensor_tensor(wsum, wcomb[:, 40:48], wcomb[:, 48:56], ALU.add))
                        ch(v.tensor_tensor(wsum, wsum, wcomb[:, 56:64], ALU.add))
                        ch(v.reciprocal(wsum, wsum))
                        for j in range(3):
                            ins = v.tensor_tensor(wcomb[:, 8 * j:8 * j + 8], wcomb[:, 8 * j:8 * j + 8], wsum, ALU.mult)
                        ch(ins)
                        full_ = [num[:, 0:512], lnum[0], lnum[1]]
                        for j in range(3):
                            f3 = full_[j].rearrange("p (h c) -> p h c", h=H2)
                            ins = v.tensor_tensor(f3, f3, bcs(wcomb[:, 8 * j:8 * j + 8], E2), ALU.mult)
                        ch(ins)
                        ch(v.tensor_tensor(full_[0], full_[0], full_[1], ALU.add))
                        v.tensor_tensor(full_[0], full_[0], full_[2], ALU.add).then_inc(sem("comb_done"), 1)
            conv_some(TAPS * KC, KC)
            for t in range(T + 1):
                if t < T:
                    bs = st[:, 68:80].rearrange("p (j s) -> p j s", j=2)
                    mv = st[:, 16 + 2 * t:18 + 2 * t]
                    bb = [bk.wait(dve, ("c1", t, j)) for j in range(2)]
                    for j in range(2):
                        ins = v.bn_stats(bs[:, j, :], PS[:, bb[j], :])
                    ch(ins)
                    ch(v.bn_aggr(mv, st[:, 68:80]))
                    v.sem_inc(sem("ln_var"), 1)
                if t >= 1:
                    for j in range(2):
                        b = bk.wait(dve, ("c2", t - 1, j))
                        c_ = C[:, 4 * j:4 * j + 4, tile(t - 1)]
                        bk.done(v.tensor_tensor(c_, b4(b), gain(R_LNG, 4 * j, 4 * j + 4), ALU.mult), ("c2", t - 1, j))
                        bk.read(dve, ("c2", t - 1, j))
                        v.tensor_tensor(c_, c_, gain(R_LNB, 4 * j, 4 * j + 4), ALU.add).then_inc(sem("ln_aff"), 1)
                if t < T:
                    dve.wait_ge(sem("ln_rstd"), t + 1)
                    bk.wait(dve, ("c2", t - 2, 1)) if t >= 2 else None
                    for j in range(2):
                        bk.done(v.tensor_scalar(HN[t % 2][:, NB * j:NB * j + NB], PS[:, bb[j], :], mv[:, 0:1], st[:, 32 + t:33 + t], ALU.subtract, ALU.mult), ("c1", t, j))
                for u in za_at.get(t, []):
                    c, h = ZA[u]
                    bk.read(dve, ("za", c, h))
                    bk.read(dve, ("at", 4 * h + 3))
                    a = attT[:, c, NB * h:NB * h + NB]
                    v.tensor_tensor(a, a, za_tmp[u % 2], ALU.mult).then_inc(sem("za_used"), 1)
            for c, h in CH:
                bk.read(dve, ("gt", c, h))
                b = bk.wait(dve, ("ya", c, h))
                a = M[:, c, NB * h:NB * h + NB]
                bk.done(v.tensor_tensor(a, PS[:, b, :], a, ALU.mult), ("ya", c, h))
            dve.wait_ge(sem("ln_silu"), 2 * T)
            for n, (c, h) in enumerate(CH):
                bk.read(dve, ("zc", c, h))
                a = C[:, c, NB * h:NB * h + NB]
                v.tensor_tensor(a, a, tmp[n % 4], ALU.mult).then_inc(sem("tmp_used"), 1)
            bk.read(dve, ("ya", 7, 1))
            for n, (c, h) in enumerate(CH):
                s_ = slice(NB * h, NB * h + NB)
                if n == 12:
                    bk.wait(dve, ("gc", 7, 1))
                    dve.wait_ge(sem("tmp_used"), 16 + 12)
                    for k in (4, 5):
                        ch(v.tensor_copy(M_hi[k], M[:, k, :]))
                        ch(v.tensor_tensor(M_lo[k], M[:, k, :], value(M_hi[k]), ALU.subtract))
                bk.read(dve, ("gc", c, h))
                b = bk.wait(dve, ("yc", c, h))
                bk.done(v.tensor_tensor(tmp[n % 4], PS[:, b, :], tmp[n % 4], ALU.mult), ("yc", c, h))
                bk.read(dve, ("yc", c, h))
                if c in (4, 5):
                    v.tensor_tensor(M[:, c, s_], M[:, c, s_], tmp[n % 4], ALU.add).then_inc(sem("tmp_used"), 1)
                else:
                    ch(v.tensor_tensor(tmp[n % 4], M[:, c, s_], tmp[n % 4], ALU.add))
                    ch(v.tensor_copy(M_hi[c][:, s_], tmp[n % 4]))
                    v.tensor_tensor(M_lo[c][:, s_], tmp[n % 4], value(M_hi[c][:, s_]), ALU.subtract).then_inc(sem("tmp_used"), 1)
            dve.wait_ge(sem("gate_in"), 16)
            n = 0
            for j in range(4):
                s_ = slice(HB * j, HB * j + HB)
                for t in range(T):
                    if j == 0:
                        dve.wait_ge(sem(f"xr_in{t}"), 16)
                    b = bk.wait(dve, ("y2", j, t))
                    wait_sum(dve, "y2_sum", n - 1)
                    bk.done(v.tensor_tensor(y2_tmp[n % 2], PS[:, b, 0:HB], gate_b[:, s_], ALU.mult), ("y2", j, t))
                    bk.read(dve, ("y2", j, t))
                    v.tensor_tensor(XB[:, t, s_], XB[:, t, s_], y2_tmp[n % 2], ALU.add).then_inc(sem("y2_sum"), 1)
                    n += 1
                    if j == 3 and t >= 1:
                        final_norm(t - 1)
            final_norm(T - 1)

        @block.tensor
        def _(pe):
            mm = nc.tensor.matmul

            def turn(dst, src, n=P):
                return nc.tensor.transpose(dst, src, ident[0:n, 0:n])

            def turns(name, src, n=4):
                b = bk.begin(pe, name)
                for k in range(n):
                    ins = turn(PS[:, b, P * k:P * k + P], src[:, P * k:P * k + P])
                bk.end(ins, name)

            def product(name, lhs, rhs, n, out_=None):
                b = bk.begin(pe, name)
                o = out_(b) if out_ else PS[:, b, :]
                for k in range(n):
                    ins = mm(o, lhs(k), rhs(k), start=(k == 0), stop=(k == n - 1))
                bk.end(ins, name)

            pe.wait_ge(sem("ident_in"), 16)
            pe.wait_ge(sem("rows_in"), 16 * 13)
            b = bk.begin(pe, "cols")
            for k in range(KC):
                ins = turn(PS[:, b, NROW * k:NROW * k + NROW], rows[0:NROW, tile(k)], NROW)
            bk.end(ins, "cols")
            pe.wait_ge(sem("wbd_in"), 32)
            pe.wait_ge(sem("chan_in"), 16)
            for m in range(2):
                product(("bd", m), lambda k: chan[:, m, :], lambda k: wbd.rearrange("p c j -> p (c j)"), 1)
            for t in range(T):
                pe.wait_ge(sem("n1_hn"), t + 1)
                for j in range(2):
                    turns(("n1", t, j), HN[t % 2][:, NB * j:NB * j + NB])
            w_wait(pe, "in0")
            for t in range(T):
                bk.read(pe, ("n1", t, 0)), bk.read(pe, ("n1", t, 1))
                product(("uf", t), lambda k: HT[:, k, tile(t)], lambda k: wview("in0")[:, k, :], KC)
            w_wait(pe, "in1"), w_wait(pe, "in2")

            def latent_turn(t):
                pe.wait_ge(sem("l_hn"), t + 1)
                turns(("lt", t, 0), HN[t % 2][:, 0:512])
                turns(("lt", t, 1), HN[t % 2][:, 512:640], 1)

            for t in range(T):
                product(("ua", t), lambda k: HT[:, k, tile(t)], lambda k: wview("in1")[:, k, :], KC)
                product(("ub", t), lambda k: HT[:, k, tile(t)], lambda k: wview("in2")[:, k, :], KC, lambda b: PS[:, b, 0:160])
                if t >= 1:
                    latent_turn(t - 1)
            latent_turn(T - 1)
            w_wait(pe, "twiddle")
            pe.wait_ge(sem("dft_done"), 1)
            tw = ring[wslot(seq["twiddle"])].rearrange("p (m r n) -> p m r n", m=2, r=RADIX)
            parts = {0: (0, None), 4: (1, None), 2: (2, 3), 6: (2, 3), 1: (4, 5), 7: (4, 5), 3: (6, 7), 5: (6, 7)}
            for c in range(4):
                for rp in range(4):
                    b = bk.begin(pe, ("pq", c, rp))
                    for j in range(2):
                        r = 2 * rp + j
                        re, im = parts[r]
                        o = PS[:, b, 256 * j:256 * j + 256]
                        ins = mm(o, gdft[:, re, tile(c)], tw[:, 0, r, :], start=True, stop=im is None)
                        if im is not None:
                            ins = mm(o, gdft[:, im, tile(c)], tw[:, 1, r, :], start=False, stop=True)
                    bk.end(ins, ("pq", c, rp))
                bk.read(pe, ("bd", 0)), bk.read(pe, ("bd", 1))
                for h in range(2):
                    bk.read(pe, ("pq", c, 2 * h)), bk.read(pe, ("pq", c, 2 * h + 1))
                    product(("yf", c, h), lambda k: bd[:, k, c, :], lambda k: pq[:, c, 4 * h:4 * h + 4, k, :], 2, b4)
            w_wait(pe, "kvup")

            def head_turns(nm, t):
                for j in range(2):
                    b = bk.begin(pe, (nm, t, j))
                    for h in range(4):
                        ins = turn(PS[0:HD1, b, tile(h)], HN[t % 2][:, HD1 * (4 * j + h):HD1 * (4 * j + h) + HD1])
                    bk.end(ins, (nm, t, j))

            def key_turn(t):
                pe.wait_ge(sem("k_rope"), t + 1)
                bk.read(pe, ("kv", t, 0)), bk.read(pe, ("kv", t, 1))
                head_turns("kt", t)

            for t in range(T):
                for j in range(2):
                    bk.read(pe, ("lt", t, 0)), bk.read(pe, ("lt", t, 1))
                    product(("kv", t, j), lambda k: kvn[:, k, tile(t)], lambda k: wview("kvup")[:, k, NB * j:NB * j + NB], 2)
                if t >= 1:
                    key_turn(t - 1)
            key_turn(T - 1)
            w_wait(pe, "qup")

            def query_turn(t):
                pe.wait_ge(sem("q_rope"), t + 1)
                head_turns("qt", t)

            for t in range(T):
                product(("q", t, 0), lambda k: qn[:, k, tile(t)], lambda k: wview("qup")[:, k, 0:512], 3)
                product(("q", t, 1), lambda k: qn[:, k, tile(t)], lambda k: wview("qup")[:, k, 512:768], 3, lambda b: PS[:, b, 0:256])
                if t >= 1:
                    query_turn(t - 1)
            query_turn(T - 1)
            w_wait(pe, "out0"), w_wait(pe, "out1")
            for kind, n in att1_steps():
                t, h = divmod(n, H1)
                if kind == "s":
                    if n == 0:
                        for u in range(T):
                            for j in range(2):
                                bk.read(pe, ("kt", u, j)), bk.read(pe, ("qt", u, j))
                    b = bk.begin(pe, ("s1", n))
                    for j in range(2):
                        ins = mm(PS[:, b + j, :], QT[:, h, tile(t)], KT[:, h, NB * j:NB * j + NB], start=True, stop=True)
                    bk.end(ins, ("s1", n))
                elif kind == "pt":
                    bk.read(pe, ("s1", n))
                    for j in range(2):
                        turns(("pt", n, j), pexp[n % 2][:, NB * j:NB * j + NB])
                elif kind == "pv":
                    if h == 0:
                        bk.begin(pe, ("o1", t))
                    bk.read(pe, ("pt", n, 0)), bk.read(pe, ("pt", n, 1))
                    for k in range(8):
                        ins = mm(PS[:, 6, VD * h:VD * h + VD], ptr[n % 2][:, k, :], V1[:, k, VD * h:VD * h + VD], start=(k == 0), stop=(k == 7))
                    if h == H1 - 1:
                        bk.end(ins, ("o1", t))
                    else:
                        ins.then_inc(sem("pv_done"), 1)
                elif kind == "y":
                    bk.read(pe, ("o1", n))
                    turns(("ot", n), o1[n % 2])
                    bk.read(pe, ("ot", n))
                    if n == 0:
                        bk.read(pe, ("yf", 3, 1))
                    for j in range(2):
                        product(("y1", n, j), lambda k: mixf[:, k, tile(n)] if k < 4 else mixa[n % 2][:, k - 4, :], lambda k: wview(f"out{j}")[:, k, :], KC)
            for m in range(2):
                pe.wait_ge(sem("nm_hn"), m + 1)
                for j in range(2):
                    turns(("nm", m, j), HN[m][:, NB * j:NB * j + NB])
            for c in range(8):
                if c == 0:
                    for m in range(2):
                        bk.read(pe, ("nm", m, 0)), bk.read(pe, ("nm", m, 1))
                if c % 4 == 0:
                    w_wait(pe, f"mkv{c // 4}")
                product(("mk", c), lambda k: wview(f"mkv{c // 4}")[:, k, tile(c % 4)], lambda k: mnT[:, k, :], KC, lambda b: PS[:, b, 0:MEM])
                pe.wait_ge(sem("n2_hn"), c + 1)
                for j in range(2):
                    turns(("n2", c, j), HN[c % 2][:, NB * j:NB * j + NB])
            for n in range(2):
                w_wait(pe, f"mkv{2 + n}")
                for m in range(2):
                    product(("mv", m, n), lambda k: mnT[:, k, tile(m)], lambda k: wview(f"mkv{2 + n}")[:, k, :], KC)
            for t in range(T):
                bk.read(pe, ("n2", t, 0)), bk.read(pe, ("n2", t, 1))
            for c in range(8):
                if c % 4 == 0:
                    w_wait(pe, f"mq{c // 4}")
                for h in range(2):
                    product(("mq", c, h), lambda k: wview(f"mq{c // 4}")[:, k, tile(c % 4)], lambda k: HT[:, k, NB * h:NB * h + NB], KC)
            for c in range(8):
                bk.read(pe, ("mk", c)), bk.read(pe, ("mq", c, 0)), bk.read(pe, ("mq", c, 1))
            w_wait(pe, "mo0"), w_wait(pe, "mo1")
            pe.wait_ge(sem("router_in"), 16)
            for kind, t in att2_steps():
                if kind == "s":
                    for hp in range(2):
                        b = bk.begin(pe, ("s2", t, hp))
                        for hh in range(2):
                            h = 2 * hp + hh
                            for k in range(2):
                                ins = mm(PS[:, b, 256 * hh:256 * hh + 256], QM[:, 2 * h + k, tile(t)], KM[:, 2 * h + k, :], start=(k == 0), stop=(k == 1))
                        bk.end(ins, ("s2", t, hp))
                elif kind == "pt":
                    for hp in range(2):
                        bk.read(pe, ("s2", t, hp))
                        turns(("p2", t, hp), p2[t % 2][:, 512 * hp:512 * hp + 512])
                elif kind == "pv":
                    if t == 0:
                        for n in range(2):
                            bk.read(pe, ("mv", 0, n)), bk.read(pe, ("mv", 1, n))
                    for hp in range(2):
                        bk.read(pe, ("p2", t, hp))
                        b = bk.begin(pe, ("o2", t, hp))
                        for hh in range(2):
                            h = 2 * hp + hh
                            for k in range(2):
                                ins = mm(PS[:, b, 256 * hh:256 * hh + 256], pt2[t % 2][:, P * (2 * h + k):P * (2 * h + k) + P], VM[:, k, MD * h:MD * h + MD], start=(k == 0), stop=(k == 1))
                        bk.end(ins, ("o2", t, hp))
                elif kind == "y":
                    for j in range(2):
                        bk.read(pe, ("o2", t, j))
                        turns(("om", t, j), om[t % 2][:, NB * j:NB * j + NB])
                    bk.read(pe, ("om", t, 0)), bk.read(pe, ("om", t, 1))
                    for j in range(2):
                        product(("ym", t, j), lambda k: omt[t % 2][:, k, :], lambda k: wview(f"mo{j}")[:, k, :], KC)
                else:
                    pe.wait_ge(sem("n3_hn"), t + 1)
                    for j in range(2):
                        turns(("n3", t, j), HN[t % 2][:, NB * j:NB * j + NB])
                    bk.read(pe, ("n3", t, 0)), bk.read(pe, ("n3", t, 1))
                    product(("lg", t), lambda k: rt[t % 2][:, k, :], lambda k: router[:, k, :], KC, lambda b: PS[:, b, 0:NE])
            pe.wait_ge(sem("aff"), T)
            for c in range(2):
                b = bk.begin(pe, ("aft", c))
                for j in range(4):
                    ins = turn(PS[0:NE, b, tile(j)], aff[:, 4 * c + j, :])
                bk.end(ins, ("aft", c))
            for i in range(6):
                w_wait(pe, f"ada{i}")
                if i < 4:
                    b = bk.begin(pe, ("ada", i))
                    for c in range(4):
                        for k in range(KC):
                            ins = mm(PS[:, b, c:c + 1], wview(f"ada{i}")[:, k, tile(c)], cols[:, k, R_C:R_C + 1], start=(k == 0), stop=(k == KC - 1))
                    bk.end(ins, ("ada", i))
                else:
                    pe.wait_ge(sem("c_wide"), 1)
                    product(("ada", i), lambda k: cb[:, k, :], lambda k: wview(f"ada{i}")[:, k, :], KC)
            pe.wait_ge(sem("top"), 1)
            b = bk.begin(pe, ("idx",))
            turn(PS[:, b, 0:NE], vals, NE)
            ins = turn(PS[:, b, NE:2 * NE], indf, NE)
            bk.end(ins, ("idx",))
            pe.wait_ge(sem("xg_in0"), 16)
            for j in range(2):
                turns(("tr0", j), xg[0][:, NB * j:NB * j + NB])
            for w in moe_first:
                for b_, v_ in w:
                    pe.wait_ge(free[b_], v_)

            def expert(e, par, last=False, half_e=None):
                def use(k, n_block):
                    pe.wait_ge(free[MOE_BANK[k]], moe_val(k, e) - 1)
                    if n_block is not None:
                        pe.wait_ge(moe_in[n_block], 16 * e + 16)
                        return moe_slot[n_block].rearrange("p (k n) -> p k n", k=KC)

                for i in range(2):
                    for gu, nb in (("g", 2 * i), ("u", 2 * i + 1)):
                        w = use(f"{gu}{i}", nb)
                        o = PS[:, MOE_BANK[f"{gu}{i}"], :]
                        for f in range(4):
                            for k in range(KC):
                                ins = mm(o[:, tile(f)], w[:, k, tile(f)], xt[par][:, k, :], start=(k == 0), stop=(k == KC - 1))
                        ins.then_inc(full[MOE_BANK[f"{gu}{i}"]], 1)
                if not last:
                    pe.wait_ge(sem(f"xg_in{1 - par}"), 16 * half_e)
                    for j in range(2):
                        use(f"tr{j}", None)
                        for k in range(4):
                            ins = turn(PS[:, MOE_BANK[f"tr{j}"], tile(k)], xg[1 - par][:, NB * j + P * k:NB * j + P * k + P])
                        ins.then_inc(full[MOE_BANK[f"tr{j}"]], 1)
                for i in range(2):
                    use(f"d{i}", None)
                    hi = down_hi[i].rearrange("p (k n) -> p k n", k=KC)
                    lo = down_lo[i].rearrange("p (k n) -> p k n", k=KC)
                    for j in range(2):
                        pe.wait_ge(free[MOE_BANK[f"u{j}"]], moe_val(f"u{j}", e))
                    for k in range(KC):
                        if k % 4 == 0:
                            pe.wait_ge(sem("down_split"), 4 * e + 2 * i + k // 4 + 1)
                        o = PS[:, MOE_BANK[f"d{i}"], :]
                        mm(o, hid_hi[:, tile(k)], hi[:, k, :], start=(k == 0), stop=False)
                        mm(o, hid_hi[:, tile(k)], lo[:, k, :], start=False, stop=False)
                        ins = mm(o, hid_lo[:, tile(k)], hi[:, k, :], start=False, stop=(k == KC - 1))
                    ins.then_inc(full[MOE_BANK[f"d{i}"]], 1)
                if not last:
                    for j in range(2):
                        pe.wait_ge(free[MOE_BANK[f"tr{j}"]], moe_val(f"tr{j}", e))

            for j in range(2):
                bk.read(pe, ("tr0", j))
            with pe.Fori(0, NE // 2 - 1, 1) as j:
                expert(2 * j, 0, half_e=j + 1)
                expert(2 * j + 1, 1, half_e=j + 2)
            expert(NE - 2, 0, half_e=NE // 2)
            expert(NE - 1, 1, last=True)
            for t in range(T):
                pe.wait_ge(sem("n4b_hn"), t + 1)
                for j in range(2):
                    turns(("n4", t, j), HN[t % 2][:, NB * j:NB * j + NB])

            def product3(name, lhs, rhs, n, out_=None):
                b = bk.begin(pe, name)
                o = out_(b) if out_ else PS[:, b, :]
                for k in range(n):
                    (l1, l2), (r1, r2) = lhs(k), rhs(k)
                    mm(o, l1, r1, start=(k == 0), stop=False)
                    mm(o, l1, r2, start=False, stop=False)
                    ins = mm(o, l2, r1, start=False, stop=(k == n - 1))
                bk.end(ins, name)

            def split_wait(name):
                pe.wait_ge(sem("split"), split_order.index(name) + 1)

            def feature_major(name, w, c, h, src):
                wv, sv = split_views(w), src
                product3(name, lambda k: [x[:, k, tile(c)] for x in wv], lambda k: [x[:, k, NB * h:NB * h + NB] for x in sv], KC)

            for i in range(4):
                for nm in ("b", "a"):
                    split_wait(f"g{nm}{i}")
                    for c, h in QUAD:
                        if i == 0:
                            pe.wait_ge(sem("n4_split"), T + T * h)
                        feature_major((f"glu_{nm}", i, c, h), f"g{nm}{i}", c, h, ht_1)

            def group_tokens(g, t, k):
                if g == 0:
                    return HT[:, k, tile(t)]
                if g == 1:
                    r, b_ = divmod(t, 2)
                    return HT[:, k, :].rearrange("p (b j r) -> p b r j", b=2, r=4)[:, b_, r, :]
                return HT[:, k, :].rearrange("p (j m) -> p m j", m=8)[:, t, :]

            for kind, i in win_steps():
                g, t = tiles2[i]
                if kind == "qkv":
                    if i < 2:
                        pe.wait_ge(sem("ht_whole"), i + 1)
                    for nm in "qkv":
                        if t == 0:
                            w_wait(pe, f"{nm}{g}")
                        product(("w" + nm, g, t), lambda k: group_tokens(g, t, k), lambda k: wview(f"{nm}{g}")[:, k, :], KC)
                    pe.wait_ge(sem("w_rope"), i + 1)
                    turns(("qkt", g, t, 0), qks[:, 0:512])
                    turns(("qkt", g, t, 1), qks[:, 512:1024])
                elif kind == "att":
                    ks = keys_of(g, t)
                    nk = len(ks)
                    bk.read(pe, ("qkt", g, t, 0)), bk.read(pe, ("qkt", g, t, 1)), bk.read(pe, ("wv", g, t))
                    for hp in range(4):
                        b = bk.begin(pe, ("sw", g, t, hp))
                        lo = slice(64 * (hp % 2), 64 * (hp % 2) + 64)
                        for hh in range(2):
                            pair = win_head(hp, hh) // 2
                            for j in range(nk):
                                kt_ = kT2[(i - (nk - 1 - j)) % 3]
                                ins = mm(PS[:, b, P * (nk * hh + j):P * (nk * hh + j) + P], qT2[i % 2][lo, pair, :], kt_[lo, pair, :], start=True, stop=True)
                        bk.end(ins, ("sw", g, t, hp))

                    def values(hp):
                        bk.read(pe, ("pw", g, t, hp))
                        if hp == 0:
                            bk.begin(pe, ("ow", g, t))
                        b = bk.at[("ow", g, t)][0]
                        for hh in range(2):
                            h = win_head(hp, hh)
                            for j in range(nk):
                                ins = mm(PS[:, b, E2 * h:E2 * h + E2], pwt[hp % 2][:, nk * hh + j, :], V2[(i - (nk - 1 - j)) % 3][:, E2 * h:E2 * h + E2], start=(j == 0), stop=(j == nk - 1))
                        if hp == 3:
                            bk.end(ins, ("ow", g, t))
                        else:
                            ins.then_inc(sem("wv_done"), 1)

                    for hp in range(4):
                        pe.wait_ge(sem("w_exp"), 4 * i + hp + 1)
                        turns(("pw", g, t, hp), pw[hp % 2], 2 * nk)
                        if hp >= 1:
                            values(hp - 1)
                    values(3)
                else:
                    pe.wait_ge(sem("comb_done"), t + 1)
                    turns(("at", t), num[:, 0:512])
            pe.wait_ge(sem("conv"), TAPS * KC)
            for t in range(T + 1):
                if t < T:
                    for j in range(2):
                        b = bk.begin(pe, ("c1", t, j))
                        for k in range(4):
                            ins = turn(PS[:, b, tile(k)], C[:, 4 * j + k, tile(t)])
                        bk.end(ins, ("c1", t, j))
                for u in za_at.get(t, []):
                    c, h = ZA[u]
                    split_wait(f"za{c // 2}")
                    pe.wait_ge(sem("ht_lo"), KC + KC * h)
                    feature_major(("za", c, h), f"za{c // 2}", c % 2, h, ht_2)
                if t >= 1:
                    for j in range(2):
                        bk.read(pe, ("c1", t - 1, j))
                    for j in range(2):
                        turns(("c2", t - 1, j), HN[(t - 1) % 2][:, NB * j:NB * j + NB])
            for nm in ("gt", "ya", "zc"):
                for c, h in CH:
                    if nm == "ya":
                        if (c, h) == (0, 0):
                            w_wait(pe, "ao")
                            pe.wait_ge(sem("za_used"), 8)
                        product((nm, c, h), lambda k: wview("ao")[:, k, tile(c)], lambda k: attT[:, k, NB * h:NB * h + NB], 4)
                    else:
                        split_wait(f"{nm}{c // 2}")
                        feature_major((nm, c, h), f"{nm}{c // 2}", c % 2, h, ht_2)
            for i in range(4):
                split_wait(f"gc{i}")
                for c, h in CH[4 * i:4 * i + 4]:
                    feature_major(("gc", c, h), f"gc{i}", c % 2, h, ht_2)
                w_wait(pe, f"co{i}")
                pe.wait_ge(sem("tmp_used"), 16)
                for c, h in CH[4 * i:4 * i + 4]:
                    product(("yc", c, h), lambda k: wview(f"co{i}")[:, k, tile(c % 2)], lambda k: C[:, k, NB * h:NB * h + NB], KC)
            for j in range(4):
                split_wait(f"wo{j}")
                for t in range(T):
                    if j == 0 and t == 0:
                        pe.wait_ge(sem("tmp_used"), 32)
                    wv = split_views(f"wo{j}")
                    product3(("y2", j, t), lambda k: (M_hi[k][:, tile(t)], M_lo[k][:, tile(t)]), lambda k: [x[:, k, :] for x in wv], KC, lambda b: PS[:, b, 0:HB])


_INS = ["x", "mem", "positions", "g_mix", "w_in", "g_q_lat", "w_q_up", "g_kv_lat", "w_kv_up", "w_fourier", "w_out",
        "g_mem_q", "g_mem_kv", "w_mem_q", "w_mem_kv", "w_mem_o", "g_ffn", "w_router", "w_exp_gate", "w_exp_up",
        "w_exp_down", "g_final", "c_2", "positions_2", "norm_g_2", "w_ada_2", "b_ada_2", "w_in_2", "conv_w_2",
        "conv_b_2", "conv_ln_g_2", "conv_ln_b_2", "w_conv_out_2", "w_att_out_2", "w_o_2", "final_g_2"]


def kernel(**inputs):
    import concourse.bacc as bacc
    from concourse.bass_utils import run_bass_kernel_spmd

    nc = bacc.Bacc("TRN2", target_bir_lowering=False, num_devices=1)
    arrays = {f"in_{n}": np.ascontiguousarray(inputs[n]) for n in _INS}
    arrays.update({f"in_{n}": v for n, v in constants().items()})
    A = {n[3:]: nc.dram_tensor(n, a.shape, mybir.dt.from_np(a.dtype), kind="ExternalInput").ap() for n, a in arrays.items()}
    out = nc.dram_tensor("out_0", (1, S, D), F32, kind="ExternalOutput").ap()
    build(nc, A, out)
    r = run_bass_kernel_spmd(nc, [arrays], core_ids=[0])
    return r.results[0]["out_0"]
```

```python
from contextlib import ExitStack

import concourse.bass as bass
import numpy as np
from concourse import mybir

F32 = mybir.dt.float32
F32R = mybir.dt.float32r
I32 = mybir.dt.int32
U32 = mybir.dt.uint32
ALU = mybir.AluOpType
ACT = mybir.ActivationFunctionType
AX = mybir.AxisListType

P = 128
S = 1024
D = 1024
T = S // P
KC = D // P
NB = 512
MEM = 256
QL, KVL, ROPE = 384, 256, 32
H1, NOPE, VD = 8, 64, 64
HD1 = NOPE + ROPE
MD = 256
NE, CAP = 16, 128
H2, E2 = 8, 64
ROT2 = E2 // 4
TAPS = 31
EPS = 1e-6
NEG = -1e30
RING = 3
RADIX = 8

(R_MIX, R_MQ, R_MKV, R_FFN, R_N2, R_SHIFT, R_SCALE, R_GATE, R_CB, R_LNG, R_LNB, R_C, R_QL, R_KVL,
 R_TAP) = range(15)
NROW = R_TAP + TAPS


def constants():
    two_pi = 2 * np.pi
    p, k = np.arange(P)[:, None], np.arange(P)[None, :]
    tw = np.zeros((P, 2, RADIX, 2, P), np.float64)
    for r in range(RADIX):
        ang = two_pi * ((p * (RADIX * k + r)) % S) / S
        tw[:, 0, r, 0], tw[:, 0, r, 1] = np.cos(ang), np.sin(ang)
        flip = -1.0 if r > RADIX // 2 else 1.0
        tw[:, 1, r, 0], tw[:, 1, r, 1] = flip * np.sin(ang), -flip * np.cos(ang)
    c = np.arange(64)
    ang = two_pi * ((c[:, None] * c[None, :]) % 64) / 64
    chan = np.zeros((P, 2, P))
    norm = 1.0 / np.sqrt(S * 64)
    for b in range(2):
        chan[64 * b:64 * b + 64, 0, 64 * b:64 * b + 64] = np.cos(ang) * norm
        chan[64 * b:64 * b + 64, 1, 64 * b:64 * b + 64] = -np.sin(ang) * norm
    f1 = (1.0 / (np.float32(10000.0) ** (np.arange(0, ROPE, 2, dtype=np.float32) / np.float32(ROPE)))).astype(np.float32)
    f2 = (np.float32(500000.0) ** (-(np.arange(ROT2 // 2, dtype=np.float32) * np.float32(2.0) / np.float32(ROT2)))).astype(np.float32)
    freq = np.concatenate([f1, f2])[None, :].repeat(P, 0)
    q, kk = np.arange(P)[:, None], np.arange(P)[None, :]
    prev = np.where(kk >= q, 0.0, NEG)
    cur = np.where(kk <= q, 0.0, NEG)
    pair = np.where((q % 2 == kk % 2) & (kk <= q), 0.0, NEG)
    return {
        "k_ident": np.eye(P, dtype=np.float32),
        "k_flip": np.eye(P, dtype=np.float32)[::-1].copy(),
        "k_twiddle": tw.reshape(P, -1).astype(np.float32),
        "k_chan": chan.reshape(P, -1).astype(np.float32),
        "k_freq": freq.astype(np.float32),
        "k_mask": np.concatenate([prev, cur, pair], 1).astype(np.float32),
    }


class Bank:

    def __init__(self, full, free):
        self.full, self.free = full, free
        self.count = [0] * 8
        self.last = [[] for _ in range(8)]
        self.next = 0
        self.at = {}
        self.order = []

    def add(self, name, pair=False, bank=None):
        if bank is None:
            if pair and self.next % 2:
                self.next = (self.next + 1) % 8
            bank = self.next
            self.next = (self.next + (2 if pair else 1)) % 8
        waits = self.last[bank] + (self.last[bank + 1] if pair else [])
        self.count[bank] += 1
        assert name not in self.at, name
        self.at[name] = (bank, self.count[bank], waits)
        self.last[bank] = [(bank, self.count[bank])]
        if pair:
            self.last[bank + 1] = [(bank, self.count[bank])]
        self.order.append(name)

    def begin(self, pe, name):
        for b, v in self.at[name][2]:
            pe.wait_ge(self.free[b], v)
        return self.at[name][0]

    def end(self, ins, name):
        ins.then_inc(self.full[self.at[name][0]], 1)

    def wait(self, eng, name):
        b, v, _ = self.at[name]
        eng.wait_ge(self.full[b], v)
        return b

    def done(self, ins, name):
        ins.then_inc(self.free[self.at[name][0]], 1)

    def read(self, eng, name):
        b, v, _ = self.at[name]
        eng.wait_ge(self.free[b], v)


def build(nc, A, out):
    sems = {}
    ctx = ExitStack()
    with ctx:
        def sem(name):
            if name not in sems:
                sems[name] = ctx.enter_context(nc.semaphore(name))
            return sems[name]

        full = [sem(f"psum_full{i}") for i in range(8)]
        free = [sem(f"psum_free{i}") for i in range(8)]
        w_full = [sem(f"weights_in{i}") for i in range(RING)]
        bk = Bank(full, free)

        X0, HT0, GA0, GB0, GC0, W0, S0, END = 0, 8192, 16384, 24576, 32768, 36864, 49152, 53200
        starts = [X0, HT0, GA0, GB0, GC0] + [W0 + 4096 * i for i in range(RING)] + [S0, END]
        names = ["x", "ht", "a", "b", "c", "w0", "w1", "w2", "small"]
        with ExitStack() as first:
            regions = [first.enter_context(nc.sbuf_tensor(f"{n}_f32", [P, starts[i + 1] - starts[i]], F32)) for i, n in enumerate(names)]
        rounded = [ctx.enter_context(nc.sbuf_tensor(f"{n}_f32r", [P, starts[i + 1] - starts[i]], F32R)) for i, n in enumerate(names[:-1])]
        ctx.enter_context(nc.sbuf_tensor("small_place", [P, END - S0], F32))
        PS = ctx.enter_context(nc.psum_tensor("ps", [P, 8, NB], F32))

        def place(tensors, at, n):
            i = max(i for i in range(len(names)) if starts[i] <= at)
            assert at + n <= starts[i + 1]
            return tensors[i][:, at - starts[i]:at - starts[i] + n]

        def mem(at, n):
            return place(regions, at, n)

        def mem_r(at, n):
            return place(rounded, at, n)

        def value(part):
            return part.bitcast(F32)

        X = mem(X0, 8192).rearrange("p (t d) -> p t d", t=T)
        HT = mem(HT0, 8192).rearrange("p (k s) -> p k s", k=KC)
        ring = [mem(W0 + 4096 * i, 4096) for i in range(RING)]
        at = [S0]

        def small(n):
            at[0] += n
            assert at[0] <= END
            return mem(at[0] - n, n)

        ident = small(P)
        cols = small(KC * NROW).rearrange("p (k r) -> p k r", r=NROW)
        NF = 16 * T + 8 * 3 * T
        sin_t, cos_t = small(NF), small(NF)
        router = small(KC * NE).rearrange("p (k e) -> p k e", e=NE)
        HN = [small(D) for _ in range(2)]
        mask = small(3 * P)
        st = small(160)
        half = small(8)
        affine = small(2 * KC)

        dram = {n: nc.dram_tensor(n, s, F32, kind="Internal").ap()
                for n, s in (("h0", (S, D)), ("acc", (S, D)), ("x4", (S, D)),
                             ("num1", (S, 528)), ("num2", (S, 528)), ("gate", (1, D)), ("att", (S, NB)))}

        def kcol(w, c0, n):
            return w[:, c0:c0 + n].rearrange("(k p) n -> p k n", p=P)

        w_in, w_in2 = A["w_in"][0], A["w_in_2"][0]
        weights = []

        def wadd(name, src, k, n, last):
            weights.append((name, src, k, n, last))

        wadd("in0", kcol(w_in, 0, NB), 8, NB, ("uf", T - 1))
        wadd("in1", kcol(w_in, NB, NB), 8, NB, ("ub", T - 1))
        wadd("in2", kcol(w_in, 2 * NB, 160), 8, 160, ("ub", T - 1))
        wadd("twiddle", A["k_twiddle"].rearrange("p (k n) -> p k n", k=2), 2, 2048, ("pq", 3, 3))
        wadd("kvup", A["w_kv_up"][0].rearrange("(k p) n -> p k n", p=P), 2, 1024, ("kv", T - 1, 1))
        wadd("qup", A["w_q_up"][0].rearrange("(k p) n -> p k n", p=P), 3, 768, ("q", T - 1, 1))
        for i in range(2):
            wadd(f"out{i}", kcol(A["w_out"][0], NB * i, NB), 8, NB, ("y1", T - 1, i))
        for i in range(4):
            wadd(f"mkv{i}", kcol(A["w_mem_kv"][0], NB * i, NB), 8, NB,
                 ("mk", 4 * i + 3) if i < 2 else ("mv", 1, i - 2))
        for i in range(2):
            wadd(f"mq{i}", kcol(A["w_mem_q"][0], NB * i, NB), 8, NB, ("mq", 4 * i + 3, 1))
        for i in range(2):
            wadd(f"mo{i}", kcol(A["w_mem_o"][0], NB * i, NB), 8, NB, ("ym", T - 1, i))
        for i in range(6):
            wadd(f"ada{i}", kcol(A["w_ada_2"][0], NB * i, NB), 8, NB, ("ada", i))
        MOE_W = 6
        n_post = len(weights)
        post = []

        def padd(name, src, k, n, last):
            post.append((name, src, k, n, last))

        HB = NB // 2
        for i in range(4):
            padd(f"gb{i}", kcol(w_in2, D + HB * i, HB), 8, HB, ("glu_b", i, 1, 1))
            padd(f"ga{i}", kcol(w_in2, HB * i, HB), 8, HB, ("glu_a", i, 1, 1))
        GORDER = (1, 2, 0)
        for g in GORDER:
            for j, c in enumerate("qkv"):
                padd(f"{c}{g}", kcol(w_in2, 3072 + 1536 * j + NB * g, NB), 8, NB, ("w" + c, g, T - 1))
        for i in range(2):
            padd(f"za{i}", kcol(w_in2, 7680 + HB * i, HB), 8, HB, ("za", 2 * i + 1, 1))
        for i in (3, 2, 1, 0):
            padd(f"gt{i}", kcol(w_in2, 9216 + HB * i, HB), 8, HB, ("gt", 2 * i + 1, 1))
        padd("ao", A["w_att_out_2"][0].rearrange("(k p) n -> p k n", p=P), 4, 1024, ("ya", 7, 1))
        for i in range(4):
            padd(f"zc{i}", kcol(w_in2, 2048 + HB * i, HB), 8, HB, ("zc", 2 * i + 1, 1))
        for i in range(4):
            padd(f"gc{i}", kcol(w_in2, 8192 + HB * i, HB), 8, HB, ("gc", 2 * i + 1, 1))
            padd(f"co{i}", kcol(A["w_conv_out_2"][0], HB * i, HB), 8, HB, ("yc", 2 * i + 1, 1))
        for i in range(4):
            padd(f"wo{i}", kcol(A["w_o_2"][0], HB * i, HB), 8, HB, ("y2", i, T - 1))
        split_order = [w[0] for w in post if w[0][:2] in ("gb", "ga", "gt", "zc", "gc", "wo") or w[0] == "za1"]
        seq = {w[0]: i for i, w in enumerate(weights)}
        seq.update({w[0]: n_post + i for i, w in enumerate(post)})
        shape = {w[0]: (w[2], w[3]) for w in weights + post}

        def wslot(n):
            return n % RING

        def wview(name):
            k, n = shape[name]
            return ring[wslot(seq[name])][:, 0:k * n].rearrange("p (k n) -> p k n", k=k)

        def w_wait(eng, name):
            n = seq[name]
            eng.wait_ge(w_full[wslot(n)], 16 * (n // RING + 1))

        def split_views(name):
            k, n = shape[name]
            slot = W0 + 4096 * wslot(seq[name])
            return [mem_r(slot + at_, k * n).rearrange("p (k n) -> p k n", k=k) for at_ in (2048, 0)]

        bk.add("cols")
        for t in range(T):
            bk.add(("n1", t, 0)), bk.add(("n1", t, 1))
        for c in range(2):
            bk.add(("bd", c))
        for t in range(T):
            bk.add(("uf", t))
        for t in range(T):
            bk.add(("ua", t)), bk.add(("ub", t))
            if t >= 1:
                bk.add(("lt", t - 1, 0)), bk.add(("lt", t - 1, 1))
        bk.add(("lt", T - 1, 0)), bk.add(("lt", T - 1, 1))
        for c in range(4):
            for r in range(4):
                bk.add(("pq", c, r))
            for h in range(2):
                bk.add(("yf", c, h))
        for t in range(T):
            bk.add(("kv", t, 0)), bk.add(("kv", t, 1))
            if t >= 1:
                bk.add(("kt", t - 1, 0)), bk.add(("kt", t - 1, 1))
        bk.add(("kt", T - 1, 0)), bk.add(("kt", T - 1, 1))
        for t in range(T):
            bk.add(("q", t, 0)), bk.add(("q", t, 1))
            if t >= 1:
                bk.add(("qt", t - 1, 0)), bk.add(("qt", t - 1, 1))
        bk.add(("qt", T - 1, 0)), bk.add(("qt", T - 1, 1))

        NS = T * H1

        def att1_steps():
            for n in range(-1, NS + 1):
                if n + 1 < NS:
                    yield "s", n + 1
                if 0 <= n < NS:
                    yield "pt", n
                if n - 1 >= 0:
                    yield "pv", n - 1
                    if (n - 1) % H1 == 2 and n - 1 > H1:
                        yield "y", (n - 1) // H1 - 1
            yield "pv_end", 0
            yield "y", T - 1

        for kind, n in att1_steps():
            t, h = divmod(n, H1)
            if kind == "s":
                bk.add(("s1", n), pair=True, bank=2 * (n % 2))
            elif kind == "pt":
                bk.add(("pt", n, 0), bank=4), bk.add(("pt", n, 1), bank=5)
            elif kind == "pv" and h == 0:
                bk.add(("o1", t), bank=6)
            elif kind == "y":
                bk.add(("ot", n), bank=7)
                bk.add(("y1", n, 0), bank=7), bk.add(("y1", n, 1), bank=7)
        bk.next = 0
        for m in range(2):
            bk.add(("nm", m, 0)), bk.add(("nm", m, 1))
        for c in range(8):
            bk.add(("mk", c))
            bk.add(("n2", c, 0)), bk.add(("n2", c, 1))
        for n in range(2):
            for m in range(2):
                bk.add(("mv", m, n))
        for c in range(8):
            bk.add(("mq", c, 0)), bk.add(("mq", c, 1))

        def att2_steps():
            for t in range(-1, T + 2):
                for kind, u in (("square", t - 2), ("s", t + 1), ("scale", t - 2), ("pt", t), ("om", t - 1), ("n3", t - 2),
                                ("pv", t), ("lg", t - 2), ("y", t - 1)):
                    if 0 <= u < T:
                        yield kind, u

        for kind, t in att2_steps():
            if kind == "s":
                bk.add(("s2", t, 0)), bk.add(("s2", t, 1))
            elif kind == "pt":
                bk.add(("p2", t, 0)), bk.add(("p2", t, 1))
            elif kind == "pv":
                bk.add(("o2", t, 0)), bk.add(("o2", t, 1))
            elif kind == "om":
                bk.add(("om", t, 0)), bk.add(("om", t, 1))
            elif kind == "y":
                bk.add(("ym", t, 0)), bk.add(("ym", t, 1))
            elif kind == "n3":
                bk.add(("n3", t, 0)), bk.add(("n3", t, 1))
            elif kind == "lg":
                bk.add(("lg", t))
        bk.add(("aft",))
        for i in range(6):
            bk.add(("ada", i))
        bk.add(("mod",)), bk.add(("idx",)), bk.add(("flip",))
        bk.next = 0
        for c in range(2):
            bk.add(("tr0", c))
        bk.next = 2
        MOE = ("g0", "u0", "g1", "u1", "tr0", "tr1", "d0", "d1")
        MOE_BANK = {k: (2 + i) % 8 for i, k in enumerate(MOE)}
        moe_base = list(bk.count)
        moe_first = [list(x) for x in bk.last]
        for e in range(NE):
            for k in MOE:
                if e == NE - 1 and k.startswith("tr"):
                    continue
                b = MOE_BANK[k]
                bk.count[b] += 1
                bk.last[b] = [(b, bk.count[b])]

        def moe_val(k, e):
            return moe_base[MOE_BANK[k]] + 1 + e

        bk.next = 0
        for t in range(T):
            bk.add(("n4", t, 0)), bk.add(("n4", t, 1))
        QUAD = [(c, h) for h in range(2) for c in range(2)]
        GLU = [(nm, 0, c, h) for h in range(2) for nm in "ba" for c in range(2)]
        GLU += [(nm, i, c, h) for i in range(1, 4) for nm in "ba" for c, h in QUAD]
        for nm, i, c, h in GLU:
            bk.add((f"glu_{nm}", i, c, h))
        def keys_of(g, tile):
            if g == 0:
                return [tile] if tile == 0 else [tile - 1, tile]
            if g == 1:
                return [tile] if tile % 2 == 0 else [tile - 1, tile]
            return [tile]

        tiles2 = [(g, t) for g in GORDER for t in range(T)]

        def win_steps():
            for i in range(len(tiles2) + 1):
                new, a = i < len(tiles2), i - 1
                if new:
                    yield "q", i, 0
                if a >= 0:
                    for u in range(4):
                        yield "scores", a, u
                if new:
                    yield "k", i, 0
                else:
                    yield "za", a, 0
                if a >= 0:
                    yield "turn", a, 0
                    yield "turn", a, 1
                if not new:
                    yield "za", a, 1
                if new:
                    yield "v", i, 0
                if a >= 0:
                    for kd, u in (("values", 0), ("values", 1), ("turn", 2), ("turn", 3)):
                        yield kd, a, u
                if new:
                    yield "qkt", i, 0
                if a >= 0:
                    yield "values", a, 2
                    yield "values", a, 3

        ZA = [(c, h) for c0 in (0, 2) for h in range(2) for c in (c0, c0 + 1)]
        for kind, i, u in win_steps():
            g, t = tiles2[i]
            if kind == "za":
                bk.add(("za", *ZA[u]))
            elif kind in ("q", "k", "v"):
                bk.add(("w" + kind, g, t))
            elif kind == "qkt":
                bk.add(("qkt", g, t, 0)), bk.add(("qkt", g, t, 1))
            elif kind == "scores":
                bk.add(("sw", g, t, u))
            elif kind == "turn":
                bk.add(("pw", g, t, u))
            elif u == 0:
                bk.add(("ow", g, t))
        at_at = {0: [0], 1: [1], 2: [2, 3], 3: [4, 5], 4: [6, 7]}
        za_at = {0: [2], 1: [3], 3: [4], 4: [5], 5: [6], 6: [7]}
        GT = [(c, h) for c in (6, 7, 4, 5, 2, 3, 0, 1) for h in range(2)]
        gt_at = {6: [0, 1], 7: [2], 8: [3]}
        za_mul_at = {3: [0, 1], 4: [2, 3], 5: [4], 6: [5], 7: [6], 8: [7]}
        for t in range(T + 1):
            if t < T:
                bk.add(("c1", t, 0)), bk.add(("c1", t, 1))
            for u in at_at.get(t, []):
                bk.add(("at", u))
            for u in za_at.get(t, []):
                bk.add(("za", *ZA[u]))
            for u in gt_at.get(t, []):
                bk.add(("gt", *GT[u]))
            if t >= 1:
                bk.add(("c2", t - 1, 0)), bk.add(("c2", t - 1, 1))
        CH = [(c, h) for c in range(8) for h in range(2)]
        for c, h in GT[4:]:
            bk.add(("gt", c, h))
        for nm in ("ya", "zc"):
            for c, h in CH:
                bk.add((nm, c, h))
        for i in range(4):
            for nm in ("gc", "yc"):
                for c, h in CH[4 * i:4 * i + 4]:
                    bk.add((nm, c, h))
        for j in range(4):
            for t in range(T):
                bk.add(("y2", j, t))

        uf = mem(GC0, 4096).rearrange("p (t c) -> p t c", t=T)
        gdft = mem(GA0, 4096).rearrange("p (j c) -> p j c", j=8)
        tdft = mem(GB0, 4096).rearrange("p (j c) -> p j c", j=8)
        kvn = mem(GA0 + 4096, 2048).rearrange("p (k s) -> p k s", k=2)
        uq = [mem(GA0 + 6144 + 672 * i, 672) for i in range(2)]
        krt = mem(GA0 + 7488, 256).rearrange("p (t c) -> p t c", t=T)
        mixf = mem(GB0, 4096).rearrange("p (c s) -> p c s", c=4)
        qn = mem(GB0 + 4096, 3072).rearrange("p (k s) -> p k s", k=3)
        bd = mem(GB0 + 7168, 1024).rearrange("p (m c j) -> p m c j", m=2, c=4)
        wbd = mem(GB0, 512).rearrange("p (c j) -> p c j", c=4)
        chan = mem(GB0 + 512, 256).rearrange("p (m j) -> p m j", m=2)
        rows = mem(GB0 + 1024, 1024)
        freq = mem(GB0 + 2048, 24)
        posi = mem(GB0 + 2080, 32).bitcast(I32).rearrange("p (g t) -> p g t", g=4)
        posf = mem(GB0 + 2112, 32).rearrange("p (g t) -> p g t", g=4)
        ang = mem(GB0 + 2176, NF)
        ang2 = mem(GB0 + 2176 + NF, NF)
        pq = mem(HT0, 8192).rearrange("p (c r m k) -> p c r m k", c=4, r=8, m=2)
        KT = mem(HT0, 8192)[0:HD1, :].rearrange("p (h s) -> p h s", h=H1)
        QT = mem(GA0, 8192)[0:HD1, :].rearrange("p (h s) -> p h s", h=H1)
        V1 = mem(GC0, 4096).rearrange("p (t c) -> p t c", t=T)
        pexp = [mem(GB0 + 4096 + 1024 * i, 1024) for i in range(2)]
        ptr = [mem(GB0 + 6144 + 1024 * i, 1024).rearrange("p (k q) -> p k q", k=8) for i in range(2)]
        o1 = [HN[0][:, 512 * i:512 * i + 512] for i in range(2)]
        mixa = [HN[1][:, 512 * i:512 * i + 512].rearrange("p (c s) -> p c s", c=4) for i in range(2)]
        memx = mem(GA0, 2048).rearrange("p (m d) -> p m d", m=2)
        mnT = mem(GB0 + 2048, 2048).rearrange("p (k s) -> p k s", k=KC)
        KM = mem(GB0 + 4096, 2048).rearrange("p (k s) -> p k s", k=KC)
        VM = mem(GB0 + 6144, 2048).rearrange("p (m d) -> p m d", m=2)
        QM = mem(GA0, 8192).rearrange("p (k s) -> p k s", k=KC)
        p2 = [mem(GC0 + 1024 * i, 1024) for i in range(2)]
        pt2 = [mem(GC0 + 2048 + 1024 * i, 1024) for i in range(2)]
        om = [mem(GB0 + 1024 * i, 1024) for i in range(2)]
        omt = [mem(GB0 + 2048 + 1024 * i, 1024).rearrange("p (k s) -> p k s", k=KC) for i in range(2)]
        rt = [mem(HT0 + 1024 * i, 1024).rearrange("p (k s) -> p k s", k=KC) for i in range(2)]
        aff_b = mem(HT0 + 2048, P)
        aff = [aff_b[:, 32 * (t % 4) + NE * (t // 4):32 * (t % 4) + NE * (t // 4) + NE] for t in range(T)]
        affT = mem(HT0 + 3072, NB)[0:2 * NE, :]
        flip = mem(HT0 + 3584, P)
        ranked = mem(HT0 + 3712, 4 * NE)
        merge = mem(HT0 + 3776, 3 * NE)
        row_ada = mem(HT0 + 5152, 2048)[0:1, :]
        vals = mem(HT0 + 4096, CAP)[0:2 * NE, :]
        inds = mem(HT0 + 4224, CAP)[0:2 * NE, :].bitcast(U32)
        indf = mem(HT0 + 4352, CAP)[0:2 * NE, :]
        gateT = mem(HT0 + 4480, NE)
        idxT = mem(HT0 + 4496, NE).bitcast(U32)
        idx_g = [mem(HT0 + 4520 + i, 1).bitcast(U32) for i in range(2)]
        idx_s = [mem(HT0 + 4524 + i, 1).bitcast(U32) for i in range(2)]
        moe_slot = [mem(X0, 4096), mem(X0 + 4096, 4096), mem(GC0, 4096)] + [ring[(n_post + j) % RING] for j in range(3)]
        moe_in = [sem(f"expert_weights_in{j}") for j in range(MOE_W)]
        down_hi = [mem_r(HT0, 4096), mem_r(GB0 + 4096, 4096)]
        down_lo = [mem_r(W0 + 4096 * ((n_post + j) % RING), 4096) for j in (1, 2)]
        xg = [mem(GA0 + 1024 * i, 1024) for i in range(2)]
        xt = [mem(GA0 + 2048 + 1024 * i, 1024).rearrange("p (k s) -> p k s", k=KC) for i in range(2)]
        hid_hi = mem_r(GA0 + 4096, 1024)
        hid_lo = mem_r(GA0 + 5120, 1024)
        sil = [mem(GA0 + 6144 + 512 * i, 512) for i in range(2)]
        ye = [mem(GB0 + 1024 * i, 1024) for i in range(2)]
        cb = mem(GB0 + 5120, 1024).rearrange("p (k m) -> p k m", k=KC)
        gate_b = mem(HT0 + 1024, 1024)
        bgate = mem(GB0 + 4096, 1024)
        gfin = mem(GA0 + 7168, 1024)
        modc = mem(HT0 + 5120, 2 * KC)
        gate_t = mem(GB0 + 6144, 1024)
        U = [mem(GB0 + S * (k + 1), S) for k in range(KC - 1)] + [mem(GA0, S)]
        XB = mem(GB0, 8192).rearrange("p (t d) -> p t d", t=T)
        n4_tmp = [mem(GC0 + 512 * i, 512) for i in range(4)]
        n4_junk = [mem(GC0 + 2048 + 1024 * i, 1024) for i in range(2)]
        HT_r, HT_Xr = (mem_r(at_, 8192).rearrange("p (k s) -> p k s", k=KC) for at_ in (HT0, X0))
        ht_1, ht_2 = (HT_r, HT_Xr), (HT_Xr, HT_r)
        sig = [mem(GA0 + 1024 + 512 * i, 512) for i in range(6)]
        qk_hi = {"q": mem_r(GA0 + 4096, 4096), "k": mem_r(GC0, 4096)}
        tile_parts = [[mem_r(at_, 1024).rearrange("p (k s) -> p k s", k=KC) for at_ in pair]
                      for pair in ((GA0 + 1024, GA0 + 3072), (GA0 + 2048, X0 + 7168))]
        att_tok = mem(GA0 + 4096, 4096).rearrange("p (t c) -> p t c", t=T)
        C = mem(GB0, 8192).rearrange("p (k s) -> p k s", k=KC)
        qT2 = [mem(X0 + 512 * i, 512).rearrange("p (h s) -> p h s", h=4) for i in range(2)]
        kT2 = [mem(X0 + 1024 + 512 * i, 512).rearrange("p (h s) -> p h s", h=4) for i in range(3)]
        V2 = [mem(X0 + 2560 + 512 * i, 512) for i in range(3)]
        pw = [mem(X0 + 4096 + 512 * i, 512) for i in range(2)]
        pwt = [mem(X0 + 5120 + 512 * i, 512).rearrange("p (j q) -> p j q", j=4) for i in range(2)]
        num = mem(X0 + 6144, 528)
        rtmp2 = [mem(X0 + 6672 + 128 * i, 128).rearrange("p (h f) -> p h f", f=8) for i in range(3)]
        lst = mem(X0 + 7056, 32)
        wcomb = mem(X0 + 7088, 80)
        ht_hi_order = [(h, k) for k0, k1 in ((0, 6), (6, KC)) for h in range(2) for k in range(k0, k1)]
        qks = HN[0]
        lnum = [HN[1][:, 0:512], HN[1][:, 512:1024]]

        def result(i):
            return HN[1][:, 0:528] if tiles2[i][0] != 0 and i % 2 else num
        attT = mem(GC0, 4096).rearrange("p (c s) -> p c s", c=4)
        M = mem(GA0, 8192).rearrange("p (k s) -> p k s", k=KC)
        za_tmp = [mem(GA0 + 1024 + 512 * i, 512) for i in range(4)] + [mem(GA0 + 512 * i, 512) for i in (0, 1, 0, 1)]
        tmp = [HN[i][:, 512 * j:512 * j + 512] for i in range(2) for j in range(2)]
        Mr = mem_r(GA0, 8192).rearrange("p (k s) -> p k s", k=KC)
        M_part = [mem_r(GC0 + S * k, S) if k < 4 else mem_r(X0 + S * (k - 4), S) for k in range(KC)]
        M_hi = [M_part[k] if k in (4, 5) else Mr[:, k, :] for k in range(KC)]
        M_lo = [Mr[:, k, :] if k in (4, 5) else M_part[k] for k in range(KC)]
        fg = mem(HT0, 1024)
        junk = mem(HT0 + 2048, 1024)
        y2_tmp = [mem(HT0 + 3072 + HB * i, HB) for i in range(2)]

        rtmp = [mask[:, 128 * i:128 * i + 128] for i in range(3)]
        negm, rsum, rrec = mask[:, 0:64], mask[:, 64:128], mask[:, 128:192]

        def tile(t):
            return slice(P * t, P * t + P)

        def gain(row, k0, k1, n=P):
            return cols[:, k0:k1, row].unsqueeze(2).to_broadcast([P, k1 - k0, n])

        def b4(b, n=4):
            return PS[:, b, 0:n * P].rearrange("p (k s) -> p k s", k=n)

        def wait_sum(eng, name, v):
            if v > 0:
                eng.wait_ge(sem(name), v)

        class Chain:

            def __init__(self, eng, name):
                self.eng, self.sem, self.n = eng, sem(name), 0

            def __call__(self, ins):
                self.n += 1
                ins.then_inc(self.sem, 1)
                self.eng.wait_ge(self.sem, self.n)

        def pv_wait(eng, n):
            t, h = divmod(n, H1)
            if h == H1 - 1:
                bk.wait(eng, ("o1", t))
            else:
                eng.wait_ge(sem("pv_done"), (H1 - 1) * t + h + 1)

        def group_tokens(g, t, src=HT):
            if g == 0:
                return src[:, :, tile(t)]
            if g == 1:
                r, b = divmod(t, 2)
                return src.rearrange("p k (b j r) -> p b r k j", b=2, r=4)[:, b, r, :, :]
            return src.rearrange("p k (j m) -> p m k j", m=8)[:, t, :, :]

        def win_head(u, j):
            return 4 * (u // 2) + u % 2 + 2 * j

        def wv_wait(eng, i, hp):
            if hp < 0:
                i, hp = i - 1, hp + 4
                if i < 0:
                    return
            if hp == 3:
                bk.wait(eng, ("ow", *tiles2[i]))
            else:
                eng.wait_ge(sem("wv_done"), 3 * i + hp + 1)

        block = ctx.enter_context(nc.Block())

        @block.sync
        def _(sp):
            def fetch(n, w):
                if n >= RING:
                    bk.wait(sp, weights[n - RING][4])
                sp.dma_start(wview(w[0]), w[1]).then_inc(w_full[wslot(n)], 16)

            sp.wait_ge(sem("rows_clear"), 1)
            vecs = [(R_MIX, A["g_mix"]), (R_MQ, A["g_mem_q"]), (R_MKV, A["g_mem_kv"]), (R_FFN, A["g_ffn"]),
                    (R_N2, A["norm_g_2"]), (R_CB, A["conv_b_2"]), (R_LNG, A["conv_ln_g_2"]),
                    (R_LNB, A["conv_ln_b_2"]), (R_C, A["c_2"]), (R_QL, A["g_q_lat"]), (R_KVL, A["g_kv_lat"])]
            for r, v in vecs:
                sp.dma_start(rows[r:r + 1, 0:v.shape[1]], v).then_inc(sem("rows_in"), 16)
            sp.dma_start(rows[R_SHIFT:R_SHIFT + 3, :], A["b_ada_2"][0].rearrange("(r d) -> r d", r=3)).then_inc(sem("rows_in"), 16)
            sp.dma_start(rows[R_TAP:R_TAP + TAPS, :], A["conv_w_2"][0]).then_inc(sem("rows_in"), 16)

            for n, w in enumerate(weights):
                fetch(n, w)
                if n == 0:
                    sp.dma_start(chan, A["k_chan"].rearrange("p (m j) -> p m j", m=2)).then_inc(sem("chan_in"), 16)
                    sp.dma_start(freq, A["k_freq"]).then_inc(sem("pos_in"), 16)
                    with nc.allow_non_contiguous_dma("positions"):
                        sp.dma_start(posi[:, 0, :], A["positions"].rearrange("o (t p) -> p (o t)", p=P)).then_inc(sem("pos_in"), 16)
                        sp.dma_start(posi[:, 1, :], A["positions_2"].rearrange("o (t p) -> p (o t)", p=P)).then_inc(sem("pos_in"), 16)
                        for b in range(2):
                            sp.dma_start(posi[:, 2, b:8:2], A["positions_2"][0].rearrange("(b j r) -> b j r", b=2, r=4)[b]).then_inc(sem("pos_in"), 16)
                        sp.dma_start(posi[:, 3, :], A["positions_2"][0].rearrange("(j m) -> j m", m=8)).then_inc(sem("pos_in"), 16)
                    sp.dma_start(router, A["w_router"][0].rearrange("(k p) e -> p k e", p=P)).then_inc(sem("router_in"), 16)

            def expert_block(e, j, w, c):
                src = A[f"w_exp_{w}"][0, bass.ds(e, 1), :, NB * c:NB * c + NB].rearrange("o (k p) n -> p (o k) n", p=P)
                sp.dma_start(moe_slot[j].rearrange("p (k n) -> p k n", k=KC), src).then_inc(moe_in[j], 16)

            sp.wait_ge(sem("acc_out"), 16 * T)
            sp.wait_ge(sem("n3_ssq"), T)
            sp.wait_ge(sem("n3_hn"), T)
            bk.wait(sp, ("o2", T - 1, 1))
            order = (("gate", 0), ("up", 0), ("gate", 1), ("up", 1), ("down", 0), ("down", 1))
            for j, (w, c) in enumerate(order):
                if j == 4:
                    sp.wait_ge(sem("xg_in0"), 16)
                if j >= 3:
                    bk.wait(sp, weights[n_post - 6 + j][4])
                expert_block(0, j, w, c)
            with sp.Fori(1, NE, 1) as e:
                for j, (w, c) in enumerate(order):
                    was = ("g0", "u0", "g1", "u1", "d0", "d1")[j]
                    sp.wait_ge(full[MOE_BANK[was]], moe_val(was, e) - 1)
                    expert_block(e, j, w, c)
            for i, w in enumerate(post):
                if i < RING:
                    was = ("u1", "d0", "d1")[i]
                    sp.wait_ge(full[MOE_BANK[was]], moe_val(was, NE - 1))
                if i >= RING:
                    bk.wait(sp, post[i - RING][4])
                sp.dma_start(wview(w[0]), w[1]).then_inc(w_full[wslot(n_post + i)], 16)
                if i == 1:
                    sp.wait_ge(sem("scattered"), 16 * NE)
                    for t in range(T):
                        sp.dma_start(XB[:, t, :], dram["acc"][tile(t), :]).then_inc(sem(f"x_back{t}"), 16)
            for t in range(T):
                sp.wait_ge(sem("out_ready"), t + 1)
                sp.dma_start(out[0, tile(t), :], XB[:, t, :]).then_inc(sem("out_done"), 16)
            sp.wait_ge(sem("out_done"), 16 * T)

        @block.gpsimd
        def _(pool):
            ch = Chain(pool, "pool_chain")

            def rstd(dst, src, n):
                ch(nc.gpsimd.tensor_scalar(dst, src, 1.0 / n, EPS, ALU.mult, ALU.add))
                return nc.gpsimd.tensor_tensor(dst, dst, half[:, 0:dst.shape[1]], ALU.pow)

            nc.gpsimd.memset(rows[0:NROW, :], 0.0).then_inc(sem("rows_clear"), 1)
            nc.gpsimd.memset(half[:, 0:4], -0.5)
            nc.gpsimd.memset(half[:, 4:8], float(np.pi / 2)).then_inc(sem("halves"), 1)
            ch(nc.gpsimd.memset(wbd, 0.0))
            wf = A["w_fourier"][0].rearrange("(c b) i j -> b i c j", b=2)
            for b in range(2):
                pool.dma_start(wbd[64 * b:64 * b + 64, :, 64 * b:64 * b + 64], wf[b]).then_inc(sem("wbd_in"), 16)

            for t in range(T):
                pool.wait_ge(sem("n1_ssq"), t + 1)
                rstd(st[:, 8 + t:9 + t], st[:, t:t + 1], D).then_inc(sem("n1_rstd"), 1)

            c8 = float(np.sqrt(0.5))
            X8 = [uf[:, t, :] for t in range(8)]
            td = [tdft[:, j, :] for j in range(8)]
            G = [gdft[:, j, :] for j in range(8)]
            tt = nc.gpsimd.tensor_tensor
            s_, d_ = td[0:4], td[4:8]
            steps = []
            for j in range(4):
                steps.append(lambda j=j: tt(s_[j], X8[j], X8[j + 4], ALU.add))
                steps.append(lambda j=j: tt(d_[j], X8[j], X8[j + 4], ALU.subtract))
            steps += [
                lambda: tt(G[2], s_[0], s_[2], ALU.subtract),
                lambda: tt(G[3], s_[3], s_[1], ALU.subtract),
                lambda: tt(s_[0], s_[0], s_[2], ALU.add),
                lambda: tt(s_[1], s_[1], s_[3], ALU.add),
                lambda: tt(G[0], s_[0], s_[1], ALU.add),
                lambda: tt(G[1], s_[0], s_[1], ALU.subtract),
                lambda: tt(s_[2], d_[1], d_[3], ALU.subtract),
                lambda: tt(s_[3], d_[1], d_[3], ALU.add),
                lambda: nc.gpsimd.tensor_scalar(s_[2], s_[2], c8, 0.0, ALU.mult, ALU.add),
                lambda: nc.gpsimd.tensor_scalar(s_[3], s_[3], c8, 0.0, ALU.mult, ALU.add),
                lambda: tt(G[4], d_[0], s_[2], ALU.add),
                lambda: tt(G[6], d_[0], s_[2], ALU.subtract),
                lambda: tt(G[7], d_[2], s_[3], ALU.subtract),
                lambda: tt(d_[2], d_[2], s_[3], ALU.add),
                lambda: nc.gpsimd.tensor_scalar(G[5], d_[2], -1.0, 0.0, ALU.mult, ALU.add),
            ]
            bk.read(pool, ("uf", T - 1))
            pool.wait_ge(sem("tables"), 1)
            bk.read(pool, ("bd", 1))
            bk.read(pool, "cols")
            for t in range(T):
                pool.wait_ge(sem("l_ssq"), 2 * t + 2)
                a, b = st[:, 16 + 2 * t:17 + 2 * t], st[:, 17 + 2 * t:18 + 2 * t]
                ra, rb = st[:, 32 + 2 * t:33 + 2 * t], st[:, 33 + 2 * t:34 + 2 * t]
                nc.gpsimd.tensor_scalar(ra, a, 1.0 / QL, EPS, ALU.mult, ALU.add)
                ch(nc.gpsimd.tensor_scalar(rb, b, 1.0 / KVL, EPS, ALU.mult, ALU.add))
                r2 = st[:, 32 + 2 * t:34 + 2 * t]
                nc.gpsimd.tensor_tensor(r2, r2, half[:, 0:2], ALU.pow).then_inc(sem("l_rstd"), 1)
                for f in steps[3 * t:3 * t + 3]:
                    ch(f())
            pool.sem_inc(sem("dft_done"), 1)

            for t in range(T):
                if t >= 2:
                    bk.wait(pool, ("kt", t - 2, 1))
                else:
                    bk.wait(pool, ("lt", T - 2 + t, 1))
                pool.wait_ge(sem("kr_done"), t + 1)
                kt_ = HN[t % 2][:, 0:H1 * HD1].rearrange("p (h c) -> p h c", h=H1)
                nc.gpsimd.tensor_copy(kt_[:, :, NOPE:HD1], krt[:, t, :].unsqueeze(1).to_broadcast([P, H1, ROPE])).then_inc(sem("k_rope"), 1)

            bk.wait(pool, ("s1", NS - 1))
            for m in range(2):
                pool.dma_start(memx[:, m, :], A["mem"][0, tile(m), :]).then_inc(sem(f"mem_in{m}"), 16)
            for m in range(2):
                pool.wait_ge(sem("nm_ssq"), m + 1)
                rstd(st[:, 50 + m:51 + m], st[:, 48 + m:49 + m], D).then_inc(sem("nm_rstd"), 1)
            for t in range(T):
                pool.wait_ge(sem("n2_ssq"), t + 1)
                rstd(st[:, 60 + t:61 + t], st[:, 52 + t:53 + t], D).then_inc(sem("n2_rstd"), 1)
            for t in range(T):
                pool.wait_ge(sem("n3_ssq"), t + 1)
                rstd(st[:, 76 + t:77 + t], st[:, 68 + t:69 + t], D).then_inc(sem("n3_rstd"), 1)
                bk.read(pool, ("ym", t, 1))
                pool.dma_start(dram["acc"][tile(t), :], X[:, t, :]).then_inc(sem("acc_out"), 16)
                pool.wait_ge(sem("n3_hn"), t + 1)
                pool.dma_start(dram["h0"][tile(t), :], HN[t % 2]).then_inc(sem(f"h0_out{t % 2}"), 16)
            nc.gpsimd.tensor_copy(cb, cols[:, :, R_C:R_C + 1].to_broadcast([P, KC, P])).then_inc(sem("c_wide"), 1)
            bcast = lambda v: v.rearrange("(o d) -> o d", o=1).to_broadcast([P, D])
            pool.dma_start(bgate, bcast(A["b_ada_2"][0, 2 * D:3 * D])).then_inc(sem("wide_in"), 16)
            bk.wait(pool, ("mq", 7, 1))
            pool.dma_start(flip, A["k_flip"]).then_inc(sem("flip_in"), 16)
            pool.dma_start(mask, A["k_mask"]).then_inc(sem("mask_in"), 16)

            def gather(e, par):
                nc.gpsimd.tensor_copy(idx_g[par], idxT[:, bass.ds(e, 1)]).then_inc(sem("idx_g"), 1)
                pool.wait_ge(sem("idx_g"), e + 1)
                pool.sem_inc(sem("pool_step"), 1)
                pool.indirect_dma_start(xg[par], None, dram["h0"], bass.IndirectOffsetOnAxis(ap=idx_g[par], axis=0)).then_inc(sem(f"xg_in{par}"), 16)

            def scatter(e, par, first=False):
                if not first:
                    pool.wait_ge(sem("scattered"), 16 * e)
                nc.gpsimd.tensor_copy(idx_s[par], idxT[:, bass.ds(e, 1)]).then_inc(sem("idx_s"), 1)
                pool.wait_ge(sem("idx_s"), e + 1)
                pool.wait_ge(sem("y_ready"), 2 * e + 2)
                pool.sem_inc(sem("pool_step"), 1)
                pool.indirect_dma_start(dram["acc"], bass.IndirectOffsetOnAxis(ap=idx_s[par], axis=0), ye[par], None, compute_op=ALU.add).then_inc(sem("scattered"), 16)

            bk.read(pool, ("flip",))
            for i in range(2):
                pool.wait_ge(sem(f"h0_out{i}"), 16 * (T // 2))
            pool.wait_ge(sem("acc_out"), 16 * T)
            gather(0, 0)
            gather(1, 1)
            bk.read(pool, ("mod",))
            mv_ = modc.rearrange("p (m k) -> p m k", m=2)
            av_ = affine.rearrange("p (m k) -> p m k", m=2)
            nc.gpsimd.tensor_tensor(av_[:, 1, :], mv_[:, 0, :], cols[:, :, R_SHIFT], ALU.add)
            ch(nc.gpsimd.tensor_tensor(av_[:, 0, :], mv_[:, 1, :], cols[:, :, R_SCALE], ALU.add))
            ch(nc.gpsimd.tensor_scalar(av_[:, 0, :], av_[:, 0, :], 1.0, 0.0, ALU.add, ALU.add))
            nc.gpsimd.tensor_tensor(av_[:, 0, :], av_[:, 0, :], cols[:, :, R_N2], ALU.mult).then_inc(sem("affine"), 1)
            bk.read(pool, ("ada", 5))
            pool.dma_start(gfin, bcast(A["g_final"])).then_inc(sem("gfin_in"), 16)
            pool.wait_ge(sem("wide_in"), 16)
            nc.gpsimd.tensor_tensor(gate_t, gate_t, bgate, ALU.add).then_inc(sem("gate"), 1)
            pool.wait_ge(sem("gate"), 1)
            pool.dma_start(dram["gate"], gate_t[0:1, :]).then_inc(sem("gate_out"), 16)

            scatter(0, 0, first=True)
            bk.wait(pool, ("tr0", 1))
            gather(2, 0)
            with pool.Fori(0, (NE - 4) // 2, 1) as j:
                for sub in range(2):
                    e = 2 * j + 1 + sub
                    par = (1 + sub) % 2
                    scatter(e, par)
                    pool.wait_ge(full[MOE_BANK["tr1"]], moe_val("tr1", e - 1))
                    gather(e + 2, par)

            def split(name):
                k, n = shape[name]
                slot = W0 + 4096 * wslot(seq[name])
                w_wait(pool, name)
                ch(nc.gpsimd.tensor_scalar(mem_r(slot + 2048, k * n), mem(slot, k * n), 1.0, 0.0, ALU.mult, ALU.add))
                nc.gpsimd.tensor_tensor(mem_r(slot, k * n), mem(slot, k * n), value(mem_r(slot + 2048, k * n)), ALU.subtract).then_inc(sem("split"), 1)

            for e in range(NE - 3, NE):
                scatter(e, e % 2)
                if e + 2 < NE:
                    pool.wait_ge(full[MOE_BANK["tr1"]], moe_val("tr1", e - 1))
                    gather(e + 2, e % 2)
            split("gb0")
            for t in range(-1, T):
                if t + 1 < T:
                    pool.wait_ge(sem("n4a_ssq"), t + 2)
                    rstd(st[:, 93 + t:94 + t], st[:, 85 + t:86 + t], D).then_inc(sem("n4a_rstd"), 1)
                if t < 0:
                    continue
                pool.wait_ge(sem("n4a_x"), t + 1)
                pool.wait_ge(sem("n4b_ssq"), t + 1)
                rstd(st[:, 108 + t:109 + t], st[:, 100 + t:101 + t], D).then_inc(sem("n4b_rstd"), 1)
                pool.dma_start(dram["x4"][tile(t), :], XB[:, t, :]).then_inc(sem("x4_out"), 16)

            for name in split_order[1:8]:
                split(name)

            def split_qk(g):
                for nm in "qk":
                    slot = W0 + 4096 * wslot(seq[f"{nm}{g}"])
                    w_wait(pool, f"{nm}{g}")
                    if nm == "k" and g == GORDER[0]:
                        bk.wait(pool, ("glu_a", 3, 1, 1))
                    for j in range(2):
                        hi = qk_hi[nm][:, 2048 * j:2048 * j + 2048]
                        ch(nc.gpsimd.tensor_scalar(hi, mem(slot + 2048 * j, 2048), 1.0, 0.0, ALU.mult, ALU.add))
                        nc.gpsimd.tensor_tensor(mem_r(slot + 2048 * j, 2048), mem(slot + 2048 * j, 2048), value(hi), ALU.subtract).then_inc(sem("qk_split"), 1)

            split_qk(GORDER[0])
            for i, (g, t) in enumerate(tiles2):
                if t == 6 and g != 0:
                    split_qk(GORDER[GORDER.index(g) + 1])
                if g != 0:
                    pool.wait_ge(sem("num_ready"), i + 1)
                    if g == 1:
                        r, b = divmod(t, 2)
                        dst = dram["num1"].rearrange("(b j r) c -> b r j c", b=2, r=4)[b, r]
                    else:
                        dst = dram["num2"].rearrange("(j m) c -> m j c", m=8)[t]
                    pool.dma_start(dst, result(i)).then_inc(sem(f"num_out{i % 2}"), 16)
            for i in range(2):
                pool.wait_ge(sem(f"num_out{i}"), 16 * T)

            def att_load(h):
                dst, src = att_tok[:, 4 * h:4 * h + 4, :], dram["att"][NB * h:NB * h + NB, :].rearrange("(t p) c -> p t c", p=P)
                pool.dma_start(dst, src).then_inc(sem(f"att_in{h}"), 16)

            for t in range(T):
                if t >= 1:
                    pool.wait_ge(sem("comb_done"), t)
                    pool.dma_start(dram["att"][tile(t - 1), :], lnum[0]).then_inc(sem("att_out"), 16)
                    pool.wait_ge(sem("att_out"), 16 * t)
                for gi, n in enumerate(("num1", "num2")):
                    pool.dma_start(lnum[gi], dram[n][tile(t), 0:512]).then_inc(sem("lnum_in"), 16)
                    pool.dma_start(lst[:, 16 * gi:16 * gi + 16], dram[n][tile(t), 512:528]).then_inc(sem("lnum_in"), 16)

            bk.wait(pool, ("wq", 0, T - 1))
            att_load(0)
            split("za1")
            pool.wait_ge(sem("comb_done"), T)
            pool.dma_start(dram["att"][tile(T - 1), :], lnum[0]).then_inc(sem("att_out"), 16)

            rest = iter([(h, k) for h in range(2) for k in range(KC)])

            def ht_rest(n):
                for _ in range(n):
                    h, k = next(rest)
                    bk.wait(pool, ("za", 1, h))
                    pool.wait_ge(sem("ht_hi"), ht_hi_order.index((h, k)) + 1)
                    c = slice(NB * h, NB * h + NB)
                    nc.gpsimd.tensor_tensor(HT_r[:, k, c], HT[:, k, c], value(HT_Xr[:, k, c]), ALU.subtract).then_inc(sem("ht_lo"), 1)

            for t in range(T):
                pool.wait_ge(sem("ln_var"), t + 1)
                v = st[:, 16 + 2 * t + 1:16 + 2 * t + 2]
                ch(nc.gpsimd.tensor_scalar(st[:, 32 + t:33 + t], v, 1.0, EPS, ALU.mult, ALU.add))
                nc.gpsimd.tensor_tensor(st[:, 32 + t:33 + t], st[:, 32 + t:33 + t], half[:, 0:1], ALU.pow).then_inc(sem("ln_rstd"), 1)
                if t == 0:
                    pool.wait_ge(sem("att_out"), 16 * T)
                    att_load(1)
                if t < 4:
                    ht_rest(4)
                elif t == 4:
                    split("gt3")
            for name in split_order[10:21]:
                split(name)
            bk.wait(pool, ("gc", 7, 1))
            pool.dma_start(gate_b, dram["gate"].to_broadcast([P, D])).then_inc(sem("gate_in"), 16)
            pool.dma_start(fg, bcast(A["final_g_2"])).then_inc(sem("fg_in"), 16)
            pool.wait_ge(sem("x4_out"), 16 * T)
            split("wo0")
            bk.wait(pool, ("yc", 7, 1))
            for t in range(T):
                pool.dma_start(XB[:, t, :], dram["x4"][tile(t), :]).then_inc(sem(f"xr_in{t}"), 16)
            for i in range(1, 4):
                split(f"wo{i}")
            for t in range(T):
                pool.wait_ge(sem("n5_ssq"), t + 1)
                rstd(st[:, 60 + t:61 + t], st[:, 52 + t:53 + t], D).then_inc(sem("n5_rstd"), 1)

        @block.scalar
        def _(act):
            def copy(name, dst, src, scale=1.0):
                ins = nc.scalar.activation(dst, src, ACT.Copy, scale=scale)
                bk.done(ins, name)

            act.dma_start(ident, A["k_ident"]).then_inc(sem("ident_in"), 16)
            for t in range(T):
                act.dma_start(X[:, t, :], A["x"][0, tile(t), :]).then_inc(sem(f"x_in{t}"), 16)

            def square(src, n, acc, jk):
                return nc.scalar.activation(jk[:, 0:n], src, ACT.Square, accum_out=acc)

            for t in range(T):
                act.wait_ge(sem(f"x_in{t}"), 16)
                if t >= 2:
                    bk.wait(act, ("n1", t - 2, 1))
                square(X[:, t, :], D, st[:, t:t + 1], HN[t % 2]).then_inc(sem("n1_ssq"), 1)
            act.wait_ge(sem("ang"), 1)
            act.wait_ge(sem("halves"), 1)
            nc.scalar.activation(sin_t, ang, ACT.Sin)
            nc.scalar.activation(cos_t, ang2, ACT.Sin, bias=half[:, 4:5], scale=-1.0).then_inc(sem("tables"), 1)
            for m in range(2):
                b = bk.wait(act, ("bd", m))
                copy(("bd", m), bd[:, m], b4(b))
            for t in range(T):
                b = bk.wait(act, ("uf", t))
                copy(("uf", t), uf[:, t, :], PS[:, b, :])
            for t in range(T):
                if t >= 2:
                    act.wait_ge(sem("l_hn"), t - 1)
                b = bk.wait(act, ("ua", t))
                copy(("ua", t), uq[t % 2][:, 0:512], PS[:, b, :])
                b = bk.wait(act, ("ub", t))
                copy(("ub", t), uq[t % 2][:, 512:672], PS[:, b, 0:160])
                bk.read(act, ("ua", t)), bk.read(act, ("ub", t))
                bk.wait(act, ("lt", t - 2, 1) if t >= 2 else ("n1", T - 2 + t, 1))
                square(uq[t % 2][:, 0:QL], QL, st[:, 16 + 2 * t:17 + 2 * t], HN[t % 2]).then_inc(sem("l_ssq"), 1)
                square(uq[t % 2][:, QL:QL + KVL], KVL, st[:, 17 + 2 * t:18 + 2 * t], HN[t % 2][:, QL:QL + KVL]).then_inc(sem("l_ssq"), 1)
            for c in range(4):
                for r in (0, 2):
                    b = bk.wait(act, ("pq", c, r))
                    copy(("pq", c, r), pq[:, c, 2 * r:2 * r + 2, :, :].rearrange("p r m k -> p (r m k)"), PS[:, b, :])
                for h in range(2):
                    b = bk.wait(act, ("yf", c, h))
                    copy(("yf", c, h), mixf[:, c, :].rearrange("p (k r) -> p r k", r=8)[:, 4 * h:4 * h + 4, :], b4(b))
            act.wait_ge(sem("dft_done"), 1)
            for t in range(T):
                bk.wait(act, ("kt", t - 2, 1) if t >= 2 else ("lt", T - 2 + t, 1))
                ktok = HN[t % 2][:, 0:H1 * HD1].rearrange("p (h c) -> p h c", h=H1)
                for j in range(2):
                    b = bk.wait(act, ("kv", t, j))
                    nc.scalar.activation(V1[:, t, 256 * j:256 * j + 256].rearrange("p (h c) -> p h c", h=4), b4(b)[:, :, 64:128], ACT.Copy)
                    copy(("kv", t, j), ktok[:, 4 * j:4 * j + 4, 0:NOPE], b4(b)[:, :, 0:64])
            for t in range(T + 1):
                if t < T:
                    bk.wait(act, ("qt", t - 2, 1) if t >= 2 else ("kt", T - 2 + t, 1))
                    b = bk.wait(act, ("q", t, 0))
                    copy(("q", t, 0), HN[t % 2][:, 0:512], PS[:, b, :])
                    b = bk.wait(act, ("q", t, 1))
                    copy(("q", t, 1), HN[t % 2][:, 512:768], PS[:, b, 0:256])
                if t >= 1:
                    for j in range(2):
                        b = bk.wait(act, ("qt", t - 1, j))
                        copy(("qt", t - 1, j), QT[:, 4 * j:4 * j + 4, tile(t - 1)], b4(b)[0:HD1], scale=HD1 ** -0.5)
            for kind, n in att1_steps():
                if kind == "s":
                    act.wait_ge(sem("a_max"), n + 1)
                    if n >= 2:
                        bk.wait(act, ("pt", n - 2, 1))
                    b = bk.wait(act, ("s1", n))
                    ins = nc.scalar.activation(pexp[n % 2], PS[:, b:b + 2, :].rearrange("p b n -> p (b n)"), ACT.Exp, bias=negm[:, n:n + 1], accum_out=rsum[:, n:n + 1])
                    bk.done(ins, ("s1", n))
                elif kind == "pt":
                    if n >= 2:
                        pv_wait(act, n - 2)
                    b = bk.wait(act, ("pt", n, 0))
                    copy(("pt", n, 0), ptr[n % 2][:, 0:4, :], b4(b))
                elif kind == "y":
                    b = bk.wait(act, ("ot", n))
                    copy(("ot", n), mixa[n % 2], b4(b))
            for m in range(2):
                act.wait_ge(sem(f"mem_in{m}"), 16)
                bk.wait(act, ("y1", T - 1, 1))
                square(memx[:, m, :], D, st[:, 48 + m:49 + m], HN[m]).then_inc(sem("nm_ssq"), 1)
            for c in range(8):
                bk.read(act, ("y1", c, 1))
                bk.wait(act, ("n2", c - 2, 1) if c >= 2 else ("nm", c, 1))
                square(X[:, c, :], D, st[:, 52 + c:53 + c], HN[c % 2]).then_inc(sem("n2_ssq"), 1)
                b = bk.wait(act, ("mk", c))
                copy(("mk", c), KM[:, c, :], PS[:, b, 0:MEM])
            for n in range(2):
                for m in range(2):
                    b = bk.wait(act, ("mv", m, n))
                    copy(("mv", m, n), VM[:, m, NB * n:NB * n + NB], PS[:, b, :])
            for c in range(8):
                for h in range(2):
                    b = bk.wait(act, ("mq", c, h))
                    copy(("mq", c, h), QM[:, c, NB * h:NB * h + NB], PS[:, b, :], scale=MD ** -0.5)
            for kind, t in att2_steps():
                if kind == "s":
                    if t >= 2:
                        bk.wait(act, ("p2", t - 2, 1))
                    for hp in range(2):
                        act.wait_ge(sem("m_max"), 2 * t + hp + 1)
                        b = bk.wait(act, ("s2", t, hp))
                        for hh in range(2):
                            i = 4 * t + 2 * hp + hh
                            ins = nc.scalar.activation(p2[t % 2][:, 256 * (2 * hp + hh):256 * (2 * hp + hh) + 256], PS[:, b, 256 * hh:256 * hh + 256], ACT.Exp, bias=negm[:, i:i + 1], accum_out=rsum[:, i:i + 1])
                        bk.done(ins, ("s2", t, hp))
                elif kind == "pt":
                    if t >= 2:
                        bk.wait(act, ("o2", t - 2, 0))
                    b = bk.wait(act, ("p2", t, 0))
                    copy(("p2", t, 0), pt2[t % 2][:, 0:512], PS[:, b, :])
                elif kind == "om":
                    if t >= 2:
                        bk.wait(act, ("ym", t - 2, 1))
                    for j in range(2):
                        b = bk.wait(act, ("om", t, j))
                        copy(("om", t, j), omt[t % 2][:, 4 * j:4 * j + 4, :], b4(b))
                elif kind == "square":
                    bk.read(act, ("ym", t, 1))
                    if t >= 2:
                        act.wait_ge(sem(f"h0_out{t % 2}"), 16 * (t // 2))
                    bk.wait(act, ("n3", t - 2, 1) if t >= 2 else ("n2", T - 2 + t, 1))
                    square(X[:, t, :], D, st[:, 68 + t:69 + t], HN[t % 2]).then_inc(sem("n3_ssq"), 1)
                elif kind == "lg":
                    act.wait_ge(sem("r_max"), t + 1)
                    b = bk.wait(act, ("lg", t))
                    ins = nc.scalar.activation(aff[t], PS[:, b, 0:NE], ACT.Exp, bias=st[:, 120 + t:121 + t], accum_out=st[:, 128 + t:129 + t])
                    bk.done(ins, ("lg", t))
            b = bk.wait(act, ("aft",))
            copy(("aft",), affT, PS[0:2 * NE, b, :])
            for i in range(6):
                b = bk.wait(act, ("ada", i))
                if i < 4:
                    copy(("ada", i), row_ada[:, NB * i:NB * i + NB], PS[0:1, b, :])
                else:
                    copy(("ada", i), gate_t[:, NB * (i - 4):NB * (i - 4) + NB], PS[:, b, :])
            b = bk.wait(act, ("mod",))
            copy(("mod",), modc, PS[:, b, 0:2 * KC])

            def expert(e, par, first=False):
                for i in range(2):
                    act.wait_ge(full[MOE_BANK[f"g{i}"]], moe_val(f"g{i}", e))
                    act.wait_ge(free[MOE_BANK[f"u{i}"]], moe_val(f"u{i}", e) - 1)
                    nc.scalar.activation(sil[i], PS[:, MOE_BANK[f"g{i}"], :], ACT.Silu).then_inc(free[MOE_BANK[f"g{i}"]], 1)
                if not first:
                    act.wait_ge(sem("scattered"), 16 * (e - 1))
                for i in range(2):
                    act.wait_ge(full[MOE_BANK[f"d{i}"]], moe_val(f"d{i}", e))
                    act.sem_inc(sem("act_step"), 1)
                    ins = nc.scalar.activation(ye[par][:, NB * i:NB * i + NB], PS[:, MOE_BANK[f"d{i}"], :], ACT.Copy, scale=gateT[:, bass.ds(e, 1)])
                    ins.then_inc(free[MOE_BANK[f"d{i}"]], 1)
                    act.wait_ge(free[MOE_BANK[f"d{i}"]], moe_val(f"d{i}", e))
                    act.sem_inc(sem("y_ready"), 1)

            bk.read(act, ("flip",))
            for e in range(2):
                expert(e, e, first=True)
            with act.Fori(1, NE // 2, 1) as j:
                for sub in range(2):
                    expert(2 * j + sub, sub)

            def first_square(t):
                act.wait_ge(sem(f"x_back{t}"), 16)
                if t >= 2:
                    act.wait_ge(sem("n4a_ssq"), t)
                square(XB[:, t, :], D, st[:, 84 + t:85 + t], n4_junk[min(t, 1)]).then_inc(sem("n4a_ssq"), 1)

            first_square(0)
            first_square(1)
            for t in range(T + 1):
                if t < T:
                    act.wait_ge(sem("n4a_x"), t + 1)
                    wait_sum(act, "n4b_ssq", t)
                    square(XB[:, t, :], D, st[:, 100 + t:101 + t], n4_junk[0]).then_inc(sem("n4b_ssq"), 1)
                if t + 2 < T:
                    first_square(t + 2)
                if t >= 1:
                    u = t - 1
                    for j in range(2):
                        b = bk.wait(act, ("n4", u, j))
                        wait_sum(act, "n4_split", 2 * u + j - 3)
                        for k in range(4):
                            c = slice(P * k, P * k + P)
                            kk = 4 * j + k
                            ins = nc.scalar.activation(n4_tmp[(2 * u + j) % 4][:, c], PS[:, b, c], ACT.Identity, bias=affine[:, KC + kk:KC + kk + 1], scale=affine[:, kk:kk + 1])
                        bk.done(ins, ("n4", u, j))
            act.wait_ge(sem("n4_split"), 2 * T)
            for i in range(4):
                for pos, (c, h) in enumerate(QUAD):
                    b = bk.wait(act, ("glu_b", i, c, h))
                    n = 4 * i + pos
                    if n >= 6:
                        bk.read(act, ("glu_a", (n - 6) // 4, *QUAD[(n - 6) % 4]))
                    ins = nc.scalar.activation(sig[n % 6], PS[:, b, :], ACT.Sigmoid)
                    bk.done(ins, ("glu_b", i, c, h))

            def tile_hi(i):
                nc.scalar.activation(tile_parts[i % 2][0], group_tokens(*tiles2[i]), ACT.Copy).then_inc(sem("tile_hi"), 1)

            bk.read(act, ("glu_a", 3, 1, 1))
            nc.scalar.activation(tile_parts[0][0], value(group_tokens(*tiles2[0], src=HT_r)), ACT.Copy).then_inc(sem("tile_hi"), 1)
            act.wait_ge(sem("ht_whole"), 2)

            def window_exp(i, u):
                g, t = tiles2[i]
                w = P * len(keys_of(g, t))
                act.wait_ge(sem("w_max"), 4 * i + u + 1)
                for hh in range(2):
                    h = win_head(u, hh)
                    p_ = pw[u % 2][:, w * hh:w * hh + w]
                    r_ = result(i)
                    ins = nc.scalar.activation(p_, p_, ACT.Exp, bias=r_[:, 512 + h:513 + h], accum_out=r_[:, 520 + h:521 + h])
                ins.then_inc(sem("w_exp"), 1)

            def gate(u):
                b = bk.wait(act, ("za", *ZA[u]))
                if u >= 6:
                    act.wait_ge(sem("za_used"), u - 1)
                bk.done(nc.scalar.activation(za_tmp[u], PS[:, b, :], ACT.Silu), ("za", *ZA[u]))

            for kind, i, u in win_steps():
                g, t = tiles2[i]
                if kind == "za":
                    gate(u)
                elif kind in ("q", "k"):
                    if kind == "q":
                        if i >= 1:
                            bk.wait(act, ("qkt", *tiles2[i - 1], 1))
                        if i + 1 < len(tiles2):
                            tile_hi(i + 1)
                    j = "qk".index(kind)
                    b = bk.wait(act, ("w" + kind, g, t))
                    copy(("w" + kind, g, t), qks[:, 512 * j:512 * j + 512], PS[:, b, :])
                elif kind == "v":
                    if i >= 3:
                        bk.wait(act, ("ow", *tiles2[i - 2]))
                    b = bk.wait(act, ("wv", g, t))
                    copy(("wv", g, t), V2[i % 3], PS[:, b, :])
                elif kind == "qkt":
                    b = bk.wait(act, ("qkt", g, t, 0))
                    copy(("qkt", g, t, 0), qT2[i % 2], b4(b), scale=E2 ** -0.5)
                    b = bk.wait(act, ("qkt", g, t, 1))
                    copy(("qkt", g, t, 1), kT2[i % 3], b4(b))
                elif kind == "scores" and u < 2:
                    window_exp(i, u)
                elif kind == "turn" and u < 2:
                    window_exp(i, u + 2)
                elif kind == "values" and u == 3 and g == 0:
                    act.wait_ge(sem("c_diff"), t + 1)
                    nc.scalar.activation(wcomb[:, 0:24], wcomb[:, 0:24], ACT.Exp).then_inc(sem("c_exp"), 1)
            bk.wait(act, ("ow", 0, T - 1))
            for n, (h, k) in enumerate(ht_hi_order):
                if n == 12:
                    act.wait_ge(sem("comb_done"), T)
                c = slice(NB * h, NB * h + NB)
                nc.scalar.activation(HT_Xr[:, k, c], HT[:, k, c], ACT.Copy).then_inc(sem("ht_hi"), 1)
            def merge_gate(c, h):
                b = bk.wait(act, ("gt", c, h))
                bk.done(nc.scalar.activation(M[:, c, NB * h:NB * h + NB], PS[:, b, :], ACT.Sigmoid), ("gt", c, h))

            act.wait_ge(sem("conv"), TAPS * KC)
            for t in range(T + 1):
                for u in at_at.get(t, []):
                    b = bk.wait(act, ("at", u))
                    copy(("at", u), attT[:, :, tile(u)], b4(b))
                for u in za_at.get(t, []):
                    gate(u)
                for u in gt_at.get(t, []):
                    merge_gate(*GT[u])
                if t >= 1:
                    for j in range(2):
                        act.wait_ge(sem("ln_aff"), 2 * (t - 1) + j + 1)
                        c_ = C[:, 4 * j:4 * j + 4, tile(t - 1)]
                        nc.scalar.activation(c_, c_, ACT.Silu).then_inc(sem("ln_silu"), 1)
            act.wait_ge(sem("za_used"), 8)
            for c, h in GT[4:]:
                merge_gate(c, h)
            for n, (c, h) in enumerate(CH):
                b = bk.wait(act, ("zc", c, h))
                wait_sum(act, "tmp_used", n - 3)
                bk.done(nc.scalar.activation(tmp[n % 4], PS[:, b, :], ACT.Silu), ("zc", c, h))
            for n, (c, h) in enumerate(CH):
                b = bk.wait(act, ("gc", c, h))
                act.wait_ge(sem("tmp_used"), 16 + n - 3)
                bk.done(nc.scalar.activation(tmp[n % 4], PS[:, b, :], ACT.Sigmoid), ("gc", c, h))
            for t in range(T):
                act.wait_ge(sem("y2_sum"), 3 * T + t + 1)
                if t >= 1:
                    act.wait_ge(sem("n5_ssq"), t)
                square(XB[:, t, :], D, st[:, 52 + t:53 + t], junk).then_inc(sem("n5_ssq"), 1)

        @block.vector
        def _(dve):
            v = nc.vector
            ch = Chain(dve, "dve_chain")
            bcs = lambda a, n: a.unsqueeze(2).to_broadcast([P, a.shape[1], n])

            b = bk.wait(dve, "cols")
            bk.done(v.tensor_copy(cols, PS[:, b, 0:KC * NROW].rearrange("p (k r) -> p k r", r=NROW)), "cols")
            bk.read(dve, "cols")

            def scaled(name, t, src, dst, rs):
                dve.wait_ge(sem(name + "_rstd"), t + 1)
                v.tensor_scalar(dst, src, rs, None, ALU.mult).then_inc(sem(name + "_hn"), 1)

            def gained(name, dst, row, k0, n=4):
                b = bk.wait(dve, name)
                bk.done(v.tensor_tensor(dst, b4(b, n), gain(row, k0, k0 + n), ALU.mult), name)

            for t in range(T + 1):
                if t < T:
                    scaled("n1", t, X[:, t, :], HN[t % 2], st[:, 8 + t:9 + t])
                if t >= 1:
                    for j in range(2):
                        gained(("n1", t - 1, j), HT[:, 4 * j:4 * j + 4, tile(t - 1)], R_MIX, 4 * j)

            dve.wait_ge(sem("pos_in"), 16 * 6)
            ch(v.tensor_copy(posf, posi))
            ang_1 = ang[:, 0:16 * T].rearrange("p (t f) -> p t f", f=16)
            ang_2 = ang[:, 16 * T:NF].rearrange("p (t f) -> p t f", f=8)
            v.tensor_tensor(ang_1, bcs(posf[:, 0, :], 16), freq[:, 0:16].unsqueeze(1).to_broadcast([P, T, 16]), ALU.mult)
            ch(v.tensor_tensor(ang_2, bcs(posf[:, 1:4, :].rearrange("p g t -> p (g t)"), 8), freq[:, 16:24].unsqueeze(1).to_broadcast([P, 3 * T, 8]), ALU.mult))
            ch(v.tensor_scalar(ang2, ang, float(1 / (2 * np.pi)), None, ALU.mult))
            magic = float(1.5 * 2 ** 23)
            ch(v.tensor_scalar(ang2, ang2, magic, None, ALU.add))
            ch(v.tensor_scalar(ang2, ang2, magic, None, ALU.subtract))
            rest = 2 * np.pi
            for bits in (6, 14, 22, None):
                part = float(np.float32(rest)) if bits is None else float(np.floor(rest * 2.0 ** bits) / 2.0 ** bits)
                rest -= part
                ch(v.scalar_tensor_tensor(ang, ang2, -part, ang, ALU.mult, ALU.add))
            pi = float(np.float32(np.pi))
            ch(v.tensor_scalar(ang, ang, pi, -pi, ALU.min, ALU.max))
            ch(v.tensor_scalar(ang2, ang, -1.0, None, ALU.mult))
            v.tensor_tensor(ang2, ang2, ang, ALU.max).then_inc(sem("ang"), 1)

            def rope(x1, x2, c, s, t1, t2, t3):
                v.tensor_tensor(t1, x1, c, ALU.mult)
                v.tensor_tensor(t2, x2, s, ALU.mult)
                ch(v.tensor_tensor(t3, x1, s, ALU.mult))
                ch(v.tensor_tensor(x1, t1, t2, ALU.subtract))
                ch(v.tensor_tensor(t1, x2, c, ALU.mult))
                return v.tensor_tensor(x2, t1, t3, ALU.add)

            dve.wait_ge(sem("tables"), 1)
            for t in range(T + 1):
                if t < T:
                    dve.wait_ge(sem("l_rstd"), t + 1)
                    v.tensor_scalar(HN[t % 2][:, 0:QL], uq[t % 2][:, 0:QL], st[:, 32 + 2 * t:33 + 2 * t], None, ALU.mult)
                    ch(v.tensor_scalar(HN[t % 2][:, QL:QL + KVL], uq[t % 2][:, QL:QL + KVL], st[:, 33 + 2 * t:34 + 2 * t], None, ALU.mult))
                    kr = uq[t % 2][:, 640:672]
                    c, s = cos_t[:, 16 * t:16 * t + 16], sin_t[:, 16 * t:16 * t + 16]
                    t1, t2, t3 = (x[:, 0:16] for x in rtmp)
                    ch(rope(kr[:, 0:16], kr[:, 16:32], c, s, t1, t2, t3))
                    v.tensor_copy(krt[:, t, :], kr).then_inc(sem("kr_done"), 1)
                    dve.wait_ge(sem("kr_done"), t + 1)
                    dve.sem_inc(sem("l_hn"), 1)
                if t >= 1:
                    u = t - 1
                    b = bk.wait(dve, ("lt", u, 0))
                    v.tensor_tensor(qn[:, :, tile(u)], b4(b)[:, 0:3], gain(R_QL, 0, 3), ALU.mult)
                    ins = v.tensor_tensor(kvn[:, 0:1, tile(u)], b4(b)[:, 3:4], gain(R_KVL, 0, 1), ALU.mult)
                    bk.done(ins, ("lt", u, 0))
                    gained(("lt", u, 1), kvn[:, 1:2, tile(u)], R_KVL, 1, 1)
            for c in range(4):
                for r in (1, 3):
                    b = bk.wait(dve, ("pq", c, r))
                    bk.done(v.tensor_copy(pq[:, c, 2 * r:2 * r + 2, :, :].rearrange("p r m k -> p (r m k)"), PS[:, b, :]), ("pq", c, r))
            for t in range(T):
                for j in range(2):
                    b = bk.wait(dve, ("kt", t, j))
                    bk.done(v.tensor_copy(KT[:, 4 * j:4 * j + 4, tile(t)], b4(b)[0:HD1]), ("kt", t, j))
            for t in range(T):
                bk.read(dve, ("q", t, 0)), bk.read(dve, ("q", t, 1))
                if t >= 1:
                    dve.wait_ge(sem("q_rope"), t)
                q = HN[t % 2][:, 0:H1 * HD1].rearrange("p (h c) -> p h c", h=H1)
                c, s = (x[:, 16 * t:16 * t + 16].unsqueeze(1).to_broadcast([P, H1, 16]) for x in (cos_t, sin_t))
                t1, t2, t3 = (x.rearrange("p (h f) -> p h f", f=16) for x in rtmp)
                rope(q[:, :, NOPE:NOPE + 16], q[:, :, NOPE + 16:HD1], c, s, t1, t2, t3).then_inc(sem("q_rope"), 1)
            dve.wait_ge(sem("q_rope"), T)
            for kind, n in att1_steps():
                if kind == "s":
                    b = bk.wait(dve, ("s1", n))
                    v.tensor_reduce(negm[:, n:n + 1], PS[:, b:b + 2, :].rearrange("p b n -> p (b n)"), AX.X, ALU.max, negate=True).then_inc(sem("a_max"), 1)
                elif kind == "pt":
                    if n >= 2:
                        pv_wait(dve, n - 2)
                    b = bk.wait(dve, ("pt", n, 1))
                    bk.done(v.tensor_copy(ptr[n % 2][:, 4:8, :], b4(b)), ("pt", n, 1))
                elif kind == "pv" and n % H1 == H1 - 1:
                    t = n // H1
                    bk.read(dve, ("s1", n))
                    ch(v.reciprocal(rrec[:, 8 * t:8 * t + 8], rsum[:, 8 * t:8 * t + 8]))
                    b = bk.wait(dve, ("o1", t))
                    bk.done(v.tensor_tensor(o1[t % 2].rearrange("p (h c) -> p h c", h=H1), PS[:, b, :].rearrange("p (h c) -> p h c", h=H1), bcs(rrec[:, 8 * t:8 * t + 8], VD), ALU.mult), ("o1", t))
                elif kind == "y":
                    for j in range(2):
                        b = bk.wait(dve, ("y1", n, j))
                        x = X[:, n, NB * j:NB * j + NB]
                        bk.done(v.tensor_tensor(x, x, PS[:, b, :], ALU.add), ("y1", n, j))
            for m in range(2):
                scaled("nm", m, memx[:, m, :], HN[m], st[:, 50 + m:51 + m])
            for m in range(2):
                for j in range(2):
                    gained(("nm", m, j), mnT[:, 4 * j:4 * j + 4, tile(m)], R_MKV, 4 * j)
            for t in range(T):
                scaled("n2", t, X[:, t, :], HN[t % 2], st[:, 60 + t:61 + t])
                for j in range(2):
                    gained(("n2", t, j), HT[:, 4 * j:4 * j + 4, tile(t)], R_MQ, 4 * j)
            for kind, t in att2_steps():
                if kind == "s":
                    for hp in range(2):
                        b = bk.wait(dve, ("s2", t, hp))
                        i = 4 * t + 2 * hp
                        v.tensor_reduce(negm[:, i:i + 2], PS[:, b, :].rearrange("p (h k) -> p h k", h=2), AX.X, ALU.max, negate=True).then_inc(sem("m_max"), 1)
                elif kind == "pt":
                    if t >= 2:
                        bk.wait(dve, ("o2", t - 2, 1))
                    b = bk.wait(dve, ("p2", t, 1))
                    bk.done(v.tensor_copy(pt2[t % 2][:, 512:1024], PS[:, b, :]), ("p2", t, 1))
                elif kind == "pv":
                    bk.read(dve, ("s2", t, 0)), bk.read(dve, ("s2", t, 1))
                    ch(v.reciprocal(rrec[:, 4 * t:4 * t + 4], rsum[:, 4 * t:4 * t + 4]))
                    if t >= 2:
                        bk.wait(dve, ("om", t - 2, 1))
                    for hp in range(2):
                        b = bk.wait(dve, ("o2", t, hp))
                        bk.done(v.tensor_tensor(om[t % 2][:, NB * hp:NB * hp + NB].rearrange("p (h c) -> p h c", h=2), PS[:, b, :].rearrange("p (h c) -> p h c", h=2), bcs(rrec[:, 4 * t + 2 * hp:4 * t + 2 * hp + 2], MD), ALU.mult), ("o2", t, hp))
                elif kind == "y":
                    for j in range(2):
                        b = bk.wait(dve, ("ym", t, j))
                        x = X[:, t, NB * j:NB * j + NB]
                        bk.done(v.tensor_tensor(x, x, PS[:, b, :], ALU.add), ("ym", t, j))
                elif kind == "scale":
                    scaled("n3", t, X[:, t, :], HN[t % 2], st[:, 76 + t:77 + t])
                elif kind == "n3":
                    if t >= 2:
                        bk.wait(dve, ("lg", t - 2))
                    for j in range(2):
                        gained(("n3", t, j), rt[t % 2][:, 4 * j:4 * j + 4, :], R_FFN, 4 * j)
                elif kind == "lg":
                    b = bk.wait(dve, ("lg", t))
                    v.tensor_reduce(st[:, 120 + t:121 + t], PS[:, b, 0:NE], AX.X, ALU.max, negate=True).then_inc(sem("r_max"), 1)
                    bk.read(dve, ("lg", t))
                    ch(v.reciprocal(st[:, 136 + t:137 + t], st[:, 128 + t:129 + t]))
                    v.tensor_scalar(aff[t], aff[t], st[:, 136 + t:137 + t], None, ALU.mult).then_inc(sem("aff"), 1)
            bk.read(dve, ("aft",))
            for r in range(CAP // 8):
                top = vals[:, 8 * r:8 * r + 8]
                ch(v.max(top, affT))
                ch(v.max_index(inds[:, 8 * r:8 * r + 8], top, affT))
                ch(v.match_replace(affT, top, affT, -1.0))
            v.tensor_copy(indf, inds).then_inc(sem("top"), 1)
            b = bk.wait(dve, ("idx",))
            bk.done(v.tensor_copy(ranked, PS[:, b, 0:4 * NE]), ("idx",))
            b = bk.wait(dve, ("flip",))
            sel, idx_b, idx_d = (merge[:, NE * i:NE * i + NE] for i in range(3))
            first, second = ranked[:, 0:NE], PS[:, b, NE:2 * NE]
            v.tensor_tensor(sel, first, second, ALU.is_ge)
            v.tensor_tensor(gateT, first, second, ALU.max)
            ch(v.tensor_scalar(idx_b, PS[:, b, 3 * NE:4 * NE], float(NB), None, ALU.add))
            ch(v.tensor_tensor(idx_d, ranked[:, 2 * NE:3 * NE], idx_b, ALU.subtract))
            ch(v.tensor_tensor(idx_d, idx_d, sel, ALU.mult))
            bk.done(v.tensor_tensor(idxT, idx_d, idx_b, ALU.add), ("flip",))

            def turned(par, banks, vals_):
                for j in range(2):
                    dve.wait_ge(full[banks[j]], vals_[j])
                    v.tensor_tensor(xt[par][:, 4 * j:4 * j + 4, :], b4(banks[j]), gain(R_FFN, 4 * j, 4 * j + 4), ALU.mult).then_inc(free[banks[j]], 1)

            turned(0, [bk.at[("tr0", j)][0] for j in range(2)], [bk.at[("tr0", j)][1] for j in range(2)])

            def expert(e, par, last=False):
                def down_split(i):
                    lo = moe_slot[4 + i]
                    dve.wait_ge(moe_in[4 + i], 16 * e + 16)
                    dve.wait_ge(full[MOE_BANK[f"d{i}"]], moe_val(f"d{i}", e) - 1)
                    for j in range(2):
                        c = slice(2048 * j, 2048 * j + 2048)
                        v.tensor_copy(down_hi[i][:, c], lo[:, c]).then_inc(sem("down_hi"), 1)
                        dve.wait_ge(sem("down_hi"), 4 * e + 2 * i + j + 1)
                        v.tensor_tensor(down_lo[i][:, c], lo[:, c], value(down_hi[i][:, c]), ALU.subtract).then_inc(sem("down_split"), 1)

                for i in range(2):
                    dve.wait_ge(free[MOE_BANK[f"g{i}"]], moe_val(f"g{i}", e))
                    dve.wait_ge(full[MOE_BANK[f"u{i}"]], moe_val(f"u{i}", e))
                    v.tensor_tensor(sil[i], PS[:, MOE_BANK[f"u{i}"], :], sil[i], ALU.mult).then_inc(sem("hid_step"), 1)
                    dve.wait_ge(sem("hid_step"), 4 * e + 2 * i + 1)
                    c = slice(NB * i, NB * i + NB)
                    v.tensor_copy(hid_hi[:, c], sil[i]).then_inc(sem("hid_step"), 1)
                    dve.wait_ge(sem("hid_step"), 4 * e + 2 * i + 2)
                    v.tensor_tensor(hid_lo[:, c], sil[i], value(hid_hi[:, c]), ALU.subtract).then_inc(free[MOE_BANK[f"u{i}"]], 1)
                    if i == 0:
                        down_split(0)
                if not last:
                    turned(1 - par, [MOE_BANK["tr0"], MOE_BANK["tr1"]], [moe_val("tr0", e), moe_val("tr1", e)])
                down_split(1)

            dve.wait_ge(sem("gate_out"), 16)
            with dve.Fori(0, NE // 2 - 1, 1) as j:
                for sub in range(2):
                    expert(2 * j + sub, sub)
            for e in range(NE - 2, NE):
                expert(e, e % 2, last=e == NE - 1)

            dve.wait_ge(sem("gfin_in"), 16)
            dve.wait_ge(sem("affine"), 1)
            def first_norm(t):
                dve.wait_ge(sem("n4a_rstd"), t + 1)
                v.scalar_tensor_tensor(XB[:, t, :], XB[:, t, :], st[:, 92 + t:93 + t], gfin, ALU.mult, ALU.mult).then_inc(sem("n4a_x"), 1)

            first_norm(0)
            for t in range(T + 1):
                if t + 1 < T:
                    first_norm(t + 1)
                if t < T:
                    dve.wait_ge(sem("n4a_x"), t + 1)
                    if t >= 2:
                        bk.wait(dve, ("n4", t - 2, 1))
                    scaled("n4b", t, XB[:, t, :], HN[t % 2], st[:, 108 + t:109 + t])
                if t >= 1:
                    u = t - 1
                    for j in range(2):
                        bk.read(dve, ("n4", u, j))
                        s_ = n4_tmp[(2 * u + j) % 4].rearrange("p (k s) -> p k s", k=4)
                        hi, lo = (x[:, 4 * j:4 * j + 4, tile(u)] for x in ht_1)
                        ch(v.tensor_copy(hi, s_))
                        v.tensor_tensor(lo, s_, value(hi), ALU.subtract).then_inc(sem("n4_split"), 1)
            dve.wait_ge(sem("x4_out"), 16 * T)
            dve.wait_ge(sem("n4b_hn"), T)

            def conv_steps():
                for k in range(KC):
                    for j in reversed(range(TAPS)):
                        yield k, j
            conv = conv_steps()
            conv_n = [0]

            def conv_some(n, last_chunk):
                for _ in range(n):
                    if conv_n[0] // TAPS > last_chunk or conv_n[0] >= TAPS * KC:
                        return
                    k, j = next(conv)
                    if j == TAPS - 1:
                        bk.read(dve, ("glu_a", k // 2, k % 2, 0)), bk.read(dve, ("glu_a", k // 2, k % 2, 1))
                        ins = v.tensor_scalar(C[:, k, :], U[k], cols[:, k, R_TAP + j:R_TAP + j + 1], cols[:, k, R_CB:R_CB + 1], ALU.mult, ALU.add)
                    else:
                        d = TAPS - 1 - j
                        ins = v.scalar_tensor_tensor(C[:, k, d:S], U[k][:, 0:S - d], cols[:, k, R_TAP + j:R_TAP + j + 1], C[:, k, d:S], ALU.mult, ALU.add)
                    ins.then_inc(sem("conv"), 1)
                    conv_n[0] += 1
                    dve.wait_ge(sem("conv"), conv_n[0])

            for i in range(4):
                for pos, (c, h) in enumerate(QUAD):
                    bk.read(dve, ("glu_b", i, c, h))
                    b = bk.wait(dve, ("glu_a", i, c, h))
                    bk.done(v.tensor_tensor(U[2 * i + c][:, NB * h:NB * h + NB], PS[:, b, :], sig[(4 * i + pos) % 6], ALU.mult), ("glu_a", i, c, h))
                    conv_some(8 if i < 3 else (3, 3, 0, 0)[pos], 2 * i - 1 + 2 * (pos == 3))

            def final_norm(t):
                dve.wait_ge(sem("n5_rstd"), t + 1)
                if t == 0:
                    dve.wait_ge(sem("fg_in"), 16)
                v.scalar_tensor_tensor(XB[:, t, :], XB[:, t, :], st[:, 60 + t:61 + t], fg, ALU.mult, ALU.mult).then_inc(sem("out_ready"), 1)

            def tile_lo(i):
                dve.wait_ge(sem("tile_hi"), i + 1)
                hi, lo = tile_parts[i % 2]
                v.tensor_tensor(lo, group_tokens(*tiles2[i]), value(hi), ALU.subtract).then_inc(sem("tile_lo"), 1)

            bk.read(dve, ("glu_a", 3, 1, 1))
            v.tensor_copy(tile_parts[0][1], value(group_tokens(*tiles2[0], src=HT_Xr))).then_inc(sem("tile_lo"), 1)
            dve.wait_ge(sem("tile_hi"), 1)
            for h in range(2):
                c = slice(NB * h, NB * h + NB)
                v.tensor_tensor(HT[:, :, c], value(HT_r[:, :, c]), value(HT_Xr[:, :, c]), ALU.add).then_inc(sem("ht_whole"), 1)
            dve.wait_ge(sem("ht_whole"), 2)

            dve.wait_ge(sem("mask_in"), 16)
            per_tile = -(-(TAPS * KC - conv_n[0]) // (3 * T))

            def window_max(i, u):
                g, t = tiles2[i]
                nk = len(keys_of(g, t))
                w = P * nk
                mk = mask[:, 0:256] if nk == 2 else (mask[:, 256:384] if g == 2 else mask[:, 128:256])
                b = bk.wait(dve, ("sw", g, t, u))
                if u >= 2:
                    bk.wait(dve, ("pw", g, t, u - 2))
                elif i >= 1:
                    bk.wait(dve, ("pw", *tiles2[i - 1], u + 2))
                for hh in range(2):
                    h = win_head(u, hh)
                    ins = v.tensor_tensor_reduce(pw[u % 2][:, w * hh:w * hh + w], PS[:, b, w * hh:w * hh + w], mk, 1.0, -3.0e38, ALU.add, ALU.max, result(i)[:, 512 + h:513 + h])
                bk.done(ins, ("sw", g, t, u))
                bk.read(dve, ("sw", g, t, u))
                nm = result(i)[:, 512 + win_head(u, 0):513 + win_head(u, 1):2]
                v.tensor_scalar(nm, nm, -1.0, None, ALU.mult).then_inc(sem("w_max"), 1)

            for kind, i, u in win_steps():
                g, t = tiles2[i]
                nk = len(keys_of(g, t))
                if kind == "k":
                    bk.read(dve, ("wq", g, t)), bk.read(dve, ("wk", g, t))
                    x = qks.rearrange("p (h c) -> p h c", c=E2)
                    o = 16 * T + 8 * (T * g + t)
                    c, s = (y[:, o:o + 8].unsqueeze(1).to_broadcast([P, 2 * H2, 8]) for y in (cos_t, sin_t))
                    rope(x[:, :, 0:8], x[:, :, 8:16], c, s, *rtmp2).then_inc(sem("w_rope"), 1)
                    dve.wait_ge(sem("w_rope"), i + 1)
                elif kind == "v":
                    if i + 1 < len(tiles2):
                        tile_lo(i + 1)
                    conv_some(2, KC)
                elif kind == "scores":
                    if u == 0 and 2 <= i <= 2 * T:
                        dve.wait_ge(sem(f"num_out{i % 2}"), 16 * (i // 2))
                    if u < 2:
                        window_max(i, u)
                    if u == 1:
                        conv_some(per_tile // 2 - 1, KC)
                elif kind == "turn":
                    b = bk.wait(dve, ("pw", g, t, u))
                    if u >= 2 or i >= 1:
                        wv_wait(dve, i, u - 2)
                    bk.done(v.tensor_copy(pwt[u % 2][:, 0:2 * nk, :], b4(b)[:, 0:2 * nk]), ("pw", g, t, u))
                    if u < 2:
                        window_max(i, u + 2)
                elif kind == "values" and u == 3:
                    b = bk.wait(dve, ("ow", g, t))
                    bk.done(v.tensor_copy(result(i)[:, 0:512], PS[:, b, :]), ("ow", g, t))
                    bk.read(dve, ("ow", g, t))
                    dve.wait_ge(sem("w_exp"), 4 * i + 4)
                    dve.wait_ge(sem("w_max"), 4 * i + 4)
                    dve.sem_inc(sem("num_ready"), 1)
                    if g == 0:
                        dve.wait_ge(sem("lnum_in"), 64 * (t + 1))
                        nm = [num[:, 512:520], lst[:, 0:8], lst[:, 16:24]]
                        dn = [num[:, 520:528], lst[:, 8:16], lst[:, 24:32]]
                        nall, wsum = wcomb[:, 24:32], wcomb[:, 32:40]
                        ch(v.tensor_tensor(nall, nm[0], nm[1], ALU.min))
                        ch(v.tensor_tensor(nall, nall, nm[2], ALU.min))
                        for j in range(3):
                            ins = v.tensor_tensor(wcomb[:, 8 * j:8 * j + 8], nall, nm[j], ALU.subtract)
                        ins.then_inc(sem("c_diff"), 1)
                        dve.wait_ge(sem("c_exp"), t + 1)
                        for j in range(3):
                            ins = v.tensor_tensor(wcomb[:, 40 + 8 * j:48 + 8 * j], wcomb[:, 8 * j:8 * j + 8], dn[j], ALU.mult)
                        ch(ins)
                        ch(v.tensor_tensor(wsum, wcomb[:, 40:48], wcomb[:, 48:56], ALU.add))
                        ch(v.tensor_tensor(wsum, wsum, wcomb[:, 56:64], ALU.add))
                        ch(v.reciprocal(wsum, wsum))
                        for j in range(3):
                            ins = v.tensor_tensor(wcomb[:, 8 * j:8 * j + 8], wcomb[:, 8 * j:8 * j + 8], wsum, ALU.mult)
                        ch(ins)
                        full_ = [num[:, 0:512], lnum[0], lnum[1]]
                        for j in range(3):
                            f3 = full_[j].rearrange("p (h c) -> p h c", h=H2)
                            ins = v.tensor_tensor(f3, f3, bcs(wcomb[:, 8 * j:8 * j + 8], E2), ALU.mult)
                        ch(ins)
                        ch(v.tensor_tensor(full_[1], full_[0], full_[1], ALU.add))
                        v.tensor_tensor(full_[1], full_[1], full_[2], ALU.add).then_inc(sem("comb_done"), 1)
                    conv_some(per_tile - per_tile // 2 - 1, KC)
            conv_some(TAPS * KC, KC)
            for t in range(T + 1):
                if t < T:
                    bs = st[:, 68:80].rearrange("p (j s) -> p j s", j=2)
                    mv = st[:, 16 + 2 * t:18 + 2 * t]
                    bb = [bk.wait(dve, ("c1", t, j)) for j in range(2)]
                    for j in range(2):
                        ins = v.bn_stats(bs[:, j, :], PS[:, bb[j], :])
                    ch(ins)
                    ch(v.bn_aggr(mv, st[:, 68:80]))
                    v.sem_inc(sem("ln_var"), 1)
                    dve.wait_ge(sem("ln_rstd"), t + 1)
                    if t >= 2:
                        bk.wait(dve, ("c2", t - 2, 1))
                    for j in range(2):
                        bk.done(v.tensor_scalar(HN[t % 2][:, NB * j:NB * j + NB], PS[:, bb[j], :], mv[:, 0:1], st[:, 32 + t:33 + t], ALU.subtract, ALU.mult), ("c1", t, j))
                if t >= 1:
                    for j in range(2):
                        b = bk.wait(dve, ("c2", t - 1, j))
                        c_ = C[:, 4 * j:4 * j + 4, tile(t - 1)]
                        bk.done(v.tensor_tensor(c_, b4(b), gain(R_LNG, 4 * j, 4 * j + 4), ALU.mult), ("c2", t - 1, j))
                        bk.read(dve, ("c2", t - 1, j))
                        v.tensor_tensor(c_, c_, gain(R_LNB, 4 * j, 4 * j + 4), ALU.add).then_inc(sem("ln_aff"), 1)
                for u in za_mul_at.get(t, []):
                    c, h = ZA[u]
                    bk.read(dve, ("za", c, h))
                    bk.read(dve, ("at", 4 * h + 2)), bk.read(dve, ("at", 4 * h + 3))
                    a = attT[:, c, NB * h:NB * h + NB]
                    v.tensor_tensor(a, a, za_tmp[u], ALU.mult).then_inc(sem("za_used"), 1)
            for c, h in CH:
                bk.read(dve, ("gt", c, h))
                b = bk.wait(dve, ("ya", c, h))
                a = M[:, c, NB * h:NB * h + NB]
                bk.done(v.tensor_tensor(a, PS[:, b, :], a, ALU.mult), ("ya", c, h))
            dve.wait_ge(sem("ln_silu"), 2 * T)
            for n, (c, h) in enumerate(CH):
                bk.read(dve, ("zc", c, h))
                a = C[:, c, NB * h:NB * h + NB]
                v.tensor_tensor(a, a, tmp[n % 4], ALU.mult).then_inc(sem("tmp_used"), 1)
            bk.read(dve, ("ya", 7, 1))
            for n, (c, h) in enumerate(CH):
                s_ = slice(NB * h, NB * h + NB)
                if n == 12:
                    bk.wait(dve, ("gc", 7, 1))
                    dve.wait_ge(sem("tmp_used"), 16 + 12)
                    for k in (4, 5):
                        ch(v.tensor_copy(M_hi[k], M[:, k, :]))
                        ch(v.tensor_tensor(M_lo[k], M[:, k, :], value(M_hi[k]), ALU.subtract))
                bk.read(dve, ("gc", c, h))
                b = bk.wait(dve, ("yc", c, h))
                bk.done(v.tensor_tensor(tmp[n % 4], PS[:, b, :], tmp[n % 4], ALU.mult), ("yc", c, h))
                bk.read(dve, ("yc", c, h))
                if c in (4, 5):
                    v.tensor_tensor(M[:, c, s_], M[:, c, s_], tmp[n % 4], ALU.add).then_inc(sem("tmp_used"), 1)
                else:
                    ch(v.tensor_tensor(tmp[n % 4], M[:, c, s_], tmp[n % 4], ALU.add))
                    ch(v.tensor_copy(M_hi[c][:, s_], tmp[n % 4]))
                    v.tensor_tensor(M_lo[c][:, s_], tmp[n % 4], value(M_hi[c][:, s_]), ALU.subtract).then_inc(sem("tmp_used"), 1)
            dve.wait_ge(sem("gate_in"), 16)
            n = 0
            for j in range(4):
                s_ = slice(HB * j, HB * j + HB)
                for t in range(T):
                    if j == 0:
                        dve.wait_ge(sem(f"xr_in{t}"), 16)
                    b = bk.wait(dve, ("y2", j, t))
                    wait_sum(dve, "y2_sum", n - 1)
                    bk.done(v.tensor_tensor(y2_tmp[n % 2], PS[:, b, 0:HB], gate_b[:, s_], ALU.mult), ("y2", j, t))
                    bk.read(dve, ("y2", j, t))
                    v.tensor_tensor(XB[:, t, s_], XB[:, t, s_], y2_tmp[n % 2], ALU.add).then_inc(sem("y2_sum"), 1)
                    n += 1
                    if j == 3 and t >= 1:
                        final_norm(t - 1)
            final_norm(T - 1)

        @block.tensor
        def _(pe):
            mm = nc.tensor.matmul

            def turn(dst, src, n=P):
                return nc.tensor.transpose(dst, src, ident[0:n, 0:n])

            def turns(name, src, n=4):
                b = bk.begin(pe, name)
                for k in range(n):
                    ins = turn(PS[:, b, P * k:P * k + P], src[:, P * k:P * k + P])
                bk.end(ins, name)

            def product(name, lhs, rhs, n, out_=None):
                b = bk.begin(pe, name)
                o = out_(b) if out_ else PS[:, b, :]
                for k in range(n):
                    ins = mm(o, lhs(k), rhs(k), start=(k == 0), stop=(k == n - 1))
                bk.end(ins, name)

            pe.wait_ge(sem("ident_in"), 16)
            pe.wait_ge(sem("rows_in"), 16 * 13)
            b = bk.begin(pe, "cols")
            for k in range(KC):
                ins = turn(PS[:, b, NROW * k:NROW * k + NROW], rows[0:NROW, tile(k)], NROW)
            bk.end(ins, "cols")
            for t in range(T):
                pe.wait_ge(sem("n1_hn"), t + 1)
                for j in range(2):
                    turns(("n1", t, j), HN[t % 2][:, NB * j:NB * j + NB])
            pe.wait_ge(sem("wbd_in"), 32)
            pe.wait_ge(sem("chan_in"), 16)
            for m in range(2):
                product(("bd", m), lambda k: chan[:, m, :], lambda k: wbd.rearrange("p c j -> p (c j)"), 1)
            w_wait(pe, "in0")
            for t in range(T):
                bk.read(pe, ("n1", t, 0)), bk.read(pe, ("n1", t, 1))
                product(("uf", t), lambda k: HT[:, k, tile(t)], lambda k: wview("in0")[:, k, :], KC)
            w_wait(pe, "in1"), w_wait(pe, "in2")

            def latent_turn(t):
                pe.wait_ge(sem("l_hn"), t + 1)
                turns(("lt", t, 0), HN[t % 2][:, 0:512])
                turns(("lt", t, 1), HN[t % 2][:, 512:640], 1)

            for t in range(T):
                product(("ua", t), lambda k: HT[:, k, tile(t)], lambda k: wview("in1")[:, k, :], KC)
                product(("ub", t), lambda k: HT[:, k, tile(t)], lambda k: wview("in2")[:, k, :], KC, lambda b: PS[:, b, 0:160])
                if t >= 1:
                    latent_turn(t - 1)
            latent_turn(T - 1)
            w_wait(pe, "twiddle")
            pe.wait_ge(sem("dft_done"), 1)
            tw = ring[wslot(seq["twiddle"])].rearrange("p (m r n) -> p m r n", m=2, r=RADIX)
            parts = {0: (0, None), 4: (1, None), 2: (2, 3), 6: (2, 3), 1: (4, 5), 7: (4, 5), 3: (6, 7), 5: (6, 7)}
            for c in range(4):
                for rp in range(4):
                    b = bk.begin(pe, ("pq", c, rp))
                    for j in range(2):
                        r = 2 * rp + j
                        re, im = parts[r]
                        o = PS[:, b, 256 * j:256 * j + 256]
                        ins = mm(o, gdft[:, re, tile(c)], tw[:, 0, r, :], start=True, stop=im is None)
                        if im is not None:
                            ins = mm(o, gdft[:, im, tile(c)], tw[:, 1, r, :], start=False, stop=True)
                    bk.end(ins, ("pq", c, rp))
                bk.read(pe, ("bd", 0)), bk.read(pe, ("bd", 1))
                for h in range(2):
                    bk.read(pe, ("pq", c, 2 * h)), bk.read(pe, ("pq", c, 2 * h + 1))
                    product(("yf", c, h), lambda k: bd[:, k, c, :], lambda k: pq[:, c, 4 * h:4 * h + 4, k, :], 2, b4)
            w_wait(pe, "kvup")

            def head_turns(nm, t):
                for j in range(2):
                    b = bk.begin(pe, (nm, t, j))
                    for h in range(4):
                        ins = turn(PS[0:HD1, b, tile(h)], HN[t % 2][:, HD1 * (4 * j + h):HD1 * (4 * j + h) + HD1])
                    bk.end(ins, (nm, t, j))

            def key_turn(t):
                pe.wait_ge(sem("k_rope"), t + 1)
                bk.read(pe, ("kv", t, 0)), bk.read(pe, ("kv", t, 1))
                head_turns("kt", t)

            for t in range(T):
                for j in range(2):
                    bk.read(pe, ("lt", t, 0)), bk.read(pe, ("lt", t, 1))
                    product(("kv", t, j), lambda k: kvn[:, k, tile(t)], lambda k: wview("kvup")[:, k, NB * j:NB * j + NB], 2)
                if t >= 1:
                    key_turn(t - 1)
            key_turn(T - 1)
            w_wait(pe, "qup")

            def query_turn(t):
                pe.wait_ge(sem("q_rope"), t + 1)
                head_turns("qt", t)

            for t in range(T):
                product(("q", t, 0), lambda k: qn[:, k, tile(t)], lambda k: wview("qup")[:, k, 0:512], 3)
                product(("q", t, 1), lambda k: qn[:, k, tile(t)], lambda k: wview("qup")[:, k, 512:768], 3, lambda b: PS[:, b, 0:256])
                if t >= 1:
                    query_turn(t - 1)
            query_turn(T - 1)
            w_wait(pe, "out0"), w_wait(pe, "out1")
            for kind, n in att1_steps():
                t, h = divmod(n, H1)
                if kind == "s":
                    if n == 0:
                        for u in range(T):
                            for j in range(2):
                                bk.read(pe, ("kt", u, j)), bk.read(pe, ("qt", u, j))
                    b = bk.begin(pe, ("s1", n))
                    for j in range(2):
                        ins = mm(PS[:, b + j, :], QT[:, h, tile(t)], KT[:, h, NB * j:NB * j + NB], start=True, stop=True)
                    bk.end(ins, ("s1", n))
                elif kind == "pt":
                    bk.read(pe, ("s1", n))
                    for j in range(2):
                        turns(("pt", n, j), pexp[n % 2][:, NB * j:NB * j + NB])
                elif kind == "pv":
                    if h == 0:
                        bk.begin(pe, ("o1", t))
                    bk.read(pe, ("pt", n, 0)), bk.read(pe, ("pt", n, 1))
                    for k in range(8):
                        ins = mm(PS[:, 6, VD * h:VD * h + VD], ptr[n % 2][:, k, :], V1[:, k, VD * h:VD * h + VD], start=(k == 0), stop=(k == 7))
                    if h == H1 - 1:
                        bk.end(ins, ("o1", t))
                    else:
                        ins.then_inc(sem("pv_done"), 1)
                elif kind == "y":
                    bk.read(pe, ("o1", n))
                    turns(("ot", n), o1[n % 2])
                    bk.read(pe, ("ot", n))
                    if n == 0:
                        bk.read(pe, ("yf", 3, 1))
                    for j in range(2):
                        product(("y1", n, j), lambda k: mixf[:, k, tile(n)] if k < 4 else mixa[n % 2][:, k - 4, :], lambda k: wview(f"out{j}")[:, k, :], KC)
            for m in range(2):
                pe.wait_ge(sem("nm_hn"), m + 1)
                for j in range(2):
                    turns(("nm", m, j), HN[m][:, NB * j:NB * j + NB])
            for c in range(8):
                if c == 0:
                    for m in range(2):
                        bk.read(pe, ("nm", m, 0)), bk.read(pe, ("nm", m, 1))
                if c % 4 == 0:
                    w_wait(pe, f"mkv{c // 4}")
                product(("mk", c), lambda k: wview(f"mkv{c // 4}")[:, k, tile(c % 4)], lambda k: mnT[:, k, :], KC, lambda b: PS[:, b, 0:MEM])
                pe.wait_ge(sem("n2_hn"), c + 1)
                for j in range(2):
                    turns(("n2", c, j), HN[c % 2][:, NB * j:NB * j + NB])
            for n in range(2):
                w_wait(pe, f"mkv{2 + n}")
                for m in range(2):
                    product(("mv", m, n), lambda k: mnT[:, k, tile(m)], lambda k: wview(f"mkv{2 + n}")[:, k, :], KC)
            for t in range(T):
                bk.read(pe, ("n2", t, 0)), bk.read(pe, ("n2", t, 1))
            for c in range(8):
                if c % 4 == 0:
                    w_wait(pe, f"mq{c // 4}")
                for h in range(2):
                    product(("mq", c, h), lambda k: wview(f"mq{c // 4}")[:, k, tile(c % 4)], lambda k: HT[:, k, NB * h:NB * h + NB], KC)
            for c in range(8):
                bk.read(pe, ("mk", c)), bk.read(pe, ("mq", c, 0)), bk.read(pe, ("mq", c, 1))
            w_wait(pe, "mo0"), w_wait(pe, "mo1")
            pe.wait_ge(sem("router_in"), 16)
            for kind, t in att2_steps():
                if kind == "s":
                    for hp in range(2):
                        b = bk.begin(pe, ("s2", t, hp))
                        for hh in range(2):
                            h = 2 * hp + hh
                            for k in range(2):
                                ins = mm(PS[:, b, 256 * hh:256 * hh + 256], QM[:, 2 * h + k, tile(t)], KM[:, 2 * h + k, :], start=(k == 0), stop=(k == 1))
                        bk.end(ins, ("s2", t, hp))
                elif kind == "pt":
                    for hp in range(2):
                        bk.read(pe, ("s2", t, hp))
                        turns(("p2", t, hp), p2[t % 2][:, 512 * hp:512 * hp + 512])
                elif kind == "pv":
                    if t == 0:
                        for n in range(2):
                            bk.read(pe, ("mv", 0, n)), bk.read(pe, ("mv", 1, n))
                    for hp in range(2):
                        bk.read(pe, ("p2", t, hp))
                        b = bk.begin(pe, ("o2", t, hp))
                        for hh in range(2):
                            h = 2 * hp + hh
                            for k in range(2):
                                ins = mm(PS[:, b, 256 * hh:256 * hh + 256], pt2[t % 2][:, P * (2 * h + k):P * (2 * h + k) + P], VM[:, k, MD * h:MD * h + MD], start=(k == 0), stop=(k == 1))
                        bk.end(ins, ("o2", t, hp))
                elif kind == "om":
                    for j in range(2):
                        bk.read(pe, ("o2", t, j))
                        turns(("om", t, j), om[t % 2][:, NB * j:NB * j + NB])
                elif kind == "y":
                    bk.read(pe, ("om", t, 0)), bk.read(pe, ("om", t, 1))
                    for j in range(2):
                        product(("ym", t, j), lambda k: omt[t % 2][:, k, :], lambda k: wview(f"mo{j}")[:, k, :], KC)
                elif kind == "n3":
                    pe.wait_ge(sem("n3_hn"), t + 1)
                    for j in range(2):
                        turns(("n3", t, j), HN[t % 2][:, NB * j:NB * j + NB])
                elif kind == "lg":
                    bk.read(pe, ("n3", t, 0)), bk.read(pe, ("n3", t, 1))
                    product(("lg", t), lambda k: rt[t % 2][:, k, :], lambda k: router[:, k, :], KC, lambda b: PS[:, b, 0:NE])
            pe.wait_ge(sem("aff"), T)
            b = bk.begin(pe, ("aft",))
            for j in range(4):
                ins = turn(PS[0:2 * NE, b, tile(j)], aff_b[:, 32 * j:32 * j + 32])
            bk.end(ins, ("aft",))
            for i in range(6):
                w_wait(pe, f"ada{i}")
                if i < 4:
                    b = bk.begin(pe, ("ada", i))
                    for k in range(KC):
                        ins = mm(PS[0:1, b, :], cols[:, k, R_C:R_C + 1], wview(f"ada{i}")[:, k, :], start=(k == 0), stop=(k == KC - 1))
                    bk.end(ins, ("ada", i))
                else:
                    pe.wait_ge(sem("c_wide"), 1)
                    product(("ada", i), lambda k: cb[:, k, :], lambda k: wview(f"ada{i}")[:, k, :], KC)
            b = bk.begin(pe, ("mod",))
            for i in range(4):
                bk.read(pe, ("ada", i))
            for j in range(2 * KC):
                ins = turn(PS[:, b, j:j + 1], row_ada[:, tile(j)], 1)
            bk.end(ins, ("mod",))
            pe.wait_ge(sem("top"), 1)
            b = bk.begin(pe, ("idx",))
            turn(PS[:, b, 0:2 * NE], vals, 2 * NE)
            ins = turn(PS[:, b, 2 * NE:4 * NE], indf, 2 * NE)
            bk.end(ins, ("idx",))
            bk.read(pe, ("idx",))
            pe.wait_ge(sem("flip_in"), 16)
            b = bk.begin(pe, ("flip",))
            bk.end(mm(PS[:, b, 0:4 * NE], flip, ranked, start=True, stop=True), ("flip",))
            pe.wait_ge(sem("xg_in0"), 16)
            for j in range(2):
                turns(("tr0", j), xg[0][:, NB * j:NB * j + NB])
            for readers in moe_first:
                for b_, v_ in readers:
                    pe.wait_ge(free[b_], v_)

            def expert(e, par, gathered=0, last=False):
                def use(k, n_block):
                    pe.wait_ge(free[MOE_BANK[k]], moe_val(k, e) - 1)
                    if n_block is not None:
                        pe.wait_ge(moe_in[n_block], 16 * e + 16)
                        return moe_slot[n_block].rearrange("p (k n) -> p k n", k=KC)

                for i in range(2):
                    for gu, nb in (("g", 2 * i), ("u", 2 * i + 1)):
                        w = use(f"{gu}{i}", nb)
                        o = PS[:, MOE_BANK[f"{gu}{i}"], :]
                        for f in range(4):
                            for k in range(KC):
                                ins = mm(o[:, tile(f)], w[:, k, tile(f)], xt[par][:, k, :], start=(k == 0), stop=(k == KC - 1))
                        ins.then_inc(full[MOE_BANK[f"{gu}{i}"]], 1)
                if not last:
                    pe.wait_ge(sem(f"xg_in{1 - par}"), 16 * gathered)
                    for j in range(2):
                        use(f"tr{j}", None)
                        for k in range(4):
                            ins = turn(PS[:, MOE_BANK[f"tr{j}"], tile(k)], xg[1 - par][:, NB * j + P * k:NB * j + P * k + P])
                        ins.then_inc(full[MOE_BANK[f"tr{j}"]], 1)
                for i in range(2):
                    use(f"d{i}", None)
                    hi = down_hi[i].rearrange("p (k n) -> p k n", k=KC)
                    lo = down_lo[i].rearrange("p (k n) -> p k n", k=KC)
                    for j in range(2):
                        pe.wait_ge(free[MOE_BANK[f"u{j}"]], moe_val(f"u{j}", e))
                    for k in range(KC):
                        if k % 4 == 0:
                            pe.wait_ge(sem("down_split"), 4 * e + 2 * i + k // 4 + 1)
                        o = PS[:, MOE_BANK[f"d{i}"], :]
                        mm(o, hid_hi[:, tile(k)], hi[:, k, :], start=(k == 0), stop=False)
                        mm(o, hid_hi[:, tile(k)], lo[:, k, :], start=False, stop=False)
                        ins = mm(o, hid_lo[:, tile(k)], hi[:, k, :], start=False, stop=(k == KC - 1))
                    ins.then_inc(full[MOE_BANK[f"d{i}"]], 1)
                if not last:
                    for j in range(2):
                        pe.wait_ge(free[MOE_BANK[f"tr{j}"]], moe_val(f"tr{j}", e))

            for j in range(2):
                bk.read(pe, ("tr0", j))
            with pe.Fori(0, NE // 2 - 1, 1) as j:
                expert(2 * j, 0, gathered=j + 1)
                expert(2 * j + 1, 1, gathered=j + 2)
            expert(NE - 2, 0, gathered=NE // 2)
            expert(NE - 1, 1, last=True)
            for t in range(T):
                pe.wait_ge(sem("n4b_hn"), t + 1)
                for j in range(2):
                    turns(("n4", t, j), HN[t % 2][:, NB * j:NB * j + NB])

            def product3(name, lhs, rhs, n, out_=None):
                b = bk.begin(pe, name)
                o = out_(b) if out_ else PS[:, b, :]
                for k in range(n):
                    (l1, l2), (r1, r2) = lhs(k), rhs(k)
                    mm(o, l1, r1, start=(k == 0), stop=False)
                    mm(o, l1, r2, start=False, stop=False)
                    ins = mm(o, l2, r1, start=False, stop=(k == n - 1))
                bk.end(ins, name)

            def split_wait(name):
                pe.wait_ge(sem("split"), split_order.index(name) + 1)

            def feature_major(name, w, c, h, src):
                wv, sv = split_views(w), src
                product3(name, lambda k: [x[:, k, tile(c)] for x in wv], lambda k: [x[:, k, NB * h:NB * h + NB] for x in sv], KC)

            for nm, i, c, h in GLU:
                split_wait(f"g{nm}{i}")
                if i == 0:
                    pe.wait_ge(sem("n4_split"), T + T * h)
                feature_major((f"glu_{nm}", i, c, h), f"g{nm}{i}", c, h, ht_1)

            def gate(u):
                c, h = ZA[u]
                if u < 4:
                    w_wait(pe, "za0")
                    product(("za", c, h), lambda k: wview("za0")[:, k, tile(c)], lambda k: HT[:, k, NB * h:NB * h + NB], KC)
                else:
                    split_wait("za1")
                    pe.wait_ge(sem("ht_lo"), KC + KC * h)
                    feature_major(("za", c, h), "za1", c % 2, h, ht_2)

            for kind, i, u in win_steps():
                g, t = tiles2[i]
                ks = keys_of(g, t)
                nk = len(ks)
                if kind == "za":
                    gate(u)
                elif kind in ("q", "k"):
                    if kind == "q":
                        pe.wait_ge(sem("tile_hi"), i + 1)
                        pe.wait_ge(sem("tile_lo"), i + 1)
                    j = "qk".index(kind)
                    b = bk.begin(pe, ("w" + kind, g, t))
                    hi, lo = (x.rearrange("p (k n) -> p k n", k=KC) for x in (qk_hi[kind], mem_r(W0 + 4096 * wslot(seq[f"{kind}{g}"]), 4096)))
                    x1, x2 = tile_parts[i % 2]
                    for k in range(KC):
                        if t == 0 and k % 4 == 0:
                            pe.wait_ge(sem("qk_split"), 4 * GORDER.index(g) + 2 * j + k // 4 + 1)
                        mm(PS[:, b, :], x1[:, k, :], hi[:, k, :], start=(k == 0), stop=False)
                        mm(PS[:, b, :], x1[:, k, :], lo[:, k, :], start=False, stop=False)
                        ins = mm(PS[:, b, :], x2[:, k, :], hi[:, k, :], start=False, stop=(k == KC - 1))
                    bk.end(ins, ("w" + kind, g, t))
                elif kind == "v":
                    if t == 0:
                        w_wait(pe, f"v{g}")
                    pe.wait_ge(sem("ht_whole"), 2)
                    product(("wv", g, t), lambda k: group_tokens(g, t)[:, k, :], lambda k: wview(f"v{g}")[:, k, :], KC)
                elif kind == "qkt":
                    pe.wait_ge(sem("w_rope"), i + 1)
                    turns(("qkt", g, t, 0), qks[:, 0:512])
                    turns(("qkt", g, t, 1), qks[:, 512:1024])
                elif kind == "scores":
                    if u == 0:
                        bk.read(pe, ("qkt", g, t, 0)), bk.read(pe, ("qkt", g, t, 1))
                    b = bk.begin(pe, ("sw", g, t, u))
                    rows_ = slice(64 * (u % 2), 64 * (u % 2) + 64)
                    for hh in range(2):
                        pair = win_head(u, hh) // 2
                        for j in range(nk):
                            kt_ = kT2[(i - (nk - 1 - j)) % 3]
                            ins = mm(PS[:, b, P * (nk * hh + j):P * (nk * hh + j) + P], qT2[i % 2][rows_, pair, :], kt_[rows_, pair, :], start=True, stop=True)
                    bk.end(ins, ("sw", g, t, u))
                elif kind == "turn":
                    pe.wait_ge(sem("w_exp"), 4 * i + u + 1)
                    turns(("pw", g, t, u), pw[u % 2], 2 * nk)
                else:
                    bk.read(pe, ("pw", g, t, u))
                    if u == 0:
                        bk.read(pe, ("wv", g, t))
                        bk.begin(pe, ("ow", g, t))
                    b = bk.at[("ow", g, t)][0]
                    for hh in range(2):
                        h = win_head(u, hh)
                        for j in range(nk):
                            ins = mm(PS[:, b, E2 * h:E2 * h + E2], pwt[u % 2][:, nk * hh + j, :], V2[(i - (nk - 1 - j)) % 3][:, E2 * h:E2 * h + E2], start=(j == 0), stop=(j == nk - 1))
                    if u == 3:
                        bk.end(ins, ("ow", g, t))
                    else:
                        ins.then_inc(sem("wv_done"), 1)
            pe.wait_ge(sem("conv"), TAPS * KC)
            for t in range(T + 1):
                if t < T:
                    for j in range(2):
                        b = bk.begin(pe, ("c1", t, j))
                        for k in range(4):
                            ins = turn(PS[:, b, tile(k)], C[:, 4 * j + k, tile(t)])
                        bk.end(ins, ("c1", t, j))
                for u in at_at.get(t, []):
                    pe.wait_ge(sem(f"att_in{u // 4}"), 16)
                    turns(("at", u), att_tok[:, u, :])
                for u in za_at.get(t, []):
                    gate(u)
                for u in gt_at.get(t, []):
                    c, h = GT[u]
                    split_wait(f"gt{c // 2}")
                    pe.wait_ge(sem("ht_lo"), 2 * KC)
                    feature_major(("gt", c, h), f"gt{c // 2}", c % 2, h, ht_2)
                if t >= 1:
                    for j in range(2):
                        bk.read(pe, ("c1", t - 1, j))
                    for j in range(2):
                        turns(("c2", t - 1, j), HN[(t - 1) % 2][:, NB * j:NB * j + NB])
            for nm in ("gt", "ya", "zc"):
                for c, h in (GT[4:] if nm == "gt" else CH):
                    if nm == "ya":
                        if (c, h) == (0, 0):
                            w_wait(pe, "ao")
                            pe.wait_ge(sem("za_used"), 8)
                        product((nm, c, h), lambda k: wview("ao")[:, k, tile(c)], lambda k: attT[:, k, NB * h:NB * h + NB], 4)
                    else:
                        split_wait(f"{nm}{c // 2}")
                        feature_major((nm, c, h), f"{nm}{c // 2}", c % 2, h, ht_2)
            for i in range(4):
                split_wait(f"gc{i}")
                for c, h in CH[4 * i:4 * i + 4]:
                    feature_major(("gc", c, h), f"gc{i}", c % 2, h, ht_2)
                w_wait(pe, f"co{i}")
                pe.wait_ge(sem("tmp_used"), 16)
                for c, h in CH[4 * i:4 * i + 4]:
                    product(("yc", c, h), lambda k: wview(f"co{i}")[:, k, tile(c % 2)], lambda k: C[:, k, NB * h:NB * h + NB], KC)
            for j in range(4):
                split_wait(f"wo{j}")
                for t in range(T):
                    if j == 0 and t == 0:
                        pe.wait_ge(sem("tmp_used"), 32)
                    wv = split_views(f"wo{j}")
                    product3(("y2", j, t), lambda k: (M_hi[k][:, tile(t)], M_lo[k][:, tile(t)]), lambda k: [x[:, k, :] for x in wv], KC, lambda b: PS[:, b, 0:HB])


_INS = ["x", "mem", "positions", "g_mix", "w_in", "g_q_lat", "w_q_up", "g_kv_lat", "w_kv_up", "w_fourier", "w_out",
        "g_mem_q", "g_mem_kv", "w_mem_q", "w_mem_kv", "w_mem_o", "g_ffn", "w_router", "w_exp_gate", "w_exp_up",
        "w_exp_down", "g_final", "c_2", "positions_2", "norm_g_2", "w_ada_2", "b_ada_2", "w_in_2", "conv_w_2",
        "conv_b_2", "conv_ln_g_2", "conv_ln_b_2", "w_conv_out_2", "w_att_out_2", "w_o_2", "final_g_2"]


def kernel(**inputs):
    import concourse.bacc as bacc
    from concourse.bass_utils import run_bass_kernel_spmd

    nc = bacc.Bacc("TRN2", target_bir_lowering=False, num_devices=1)
    arrays = {f"in_{n}": np.ascontiguousarray(inputs[n]) for n in _INS}
    arrays.update({f"in_{n}": v for n, v in constants().items()})
    A = {n[3:]: nc.dram_tensor(n, a.shape, mybir.dt.from_np(a.dtype), kind="ExternalInput").ap() for n, a in arrays.items()}
    out = nc.dram_tensor("out_0", (1, S, D), F32, kind="ExternalOutput").ap()
    build(nc, A, out)
    r = run_bass_kernel_spmd(nc, [arrays], core_ids=[0])
    return r.results[0]["out_0"]
```
